# Optimizing a Trainium2 kernel written in Bass

```python
import math
import jax, jax.numpy as jnp
from jax import lax
import numpy as np

D_MODEL = 2048
BATCH = 1
SEQ = 512
DEPTH = 1
DEC_BATCH = 8
DEC_SEQ = 4
PAST_LEN = 2048
PAGE_SIZE = 128

HEAD_DIM = 128
NSA_HEADS = D_MODEL // (2 * HEAD_DIM)
NSA_KV_HEADS = 2
NSA_GROUP = NSA_HEADS // NSA_KV_HEADS
NSA_WIDTH = NSA_HEADS * HEAD_DIM
NSA_BLOCK = 64
NSA_TOP_N = 16
NSA_WINDOW = 512
GDN_HEADS = D_MODEL // (2 * HEAD_DIM)
GDN_WIDTH = GDN_HEADS * HEAD_DIM
GDN_CONV = 4
GDN_CHUNK = 64
MIX_WIDTH = NSA_WIDTH + GDN_WIDTH
D_FF = (11 * D_MODEL) // 4
FFN_CONV = 3
KV_COLS = NSA_KV_HEADS * 2 * HEAD_DIM
IN_COLS = NSA_WIDTH + 3 * KV_COLS + 3 * NSA_HEADS + 4 * GDN_WIDTH + 2 * GDN_HEADS
DN_ALPHA = (2 * DEPTH) ** 0.25
DN_BETA = (8 * DEPTH) ** -0.25
LN_EPS = 1e-5
NORM_EPS = 1e-6
NEG = -1e30
FORCE = 1e4
SLC_QBLOCK = 64
WIN_QBLOCK = 128

kernel_name = 'hybrid_nsa_gdn_decoder_step'

F32 = jnp.float32

def split_sizes():
    sizes = [NSA_WIDTH, KV_COLS, KV_COLS, KV_COLS, 3 * NSA_HEADS,
             3 * GDN_WIDTH, GDN_WIDTH, GDN_HEADS, GDN_HEADS]
    return np.cumsum(sizes)[:-1].tolist()

def alibi_slopes():
    h = np.arange(1, NSA_HEADS + 1, dtype=np.float32)
    m = np.power(np.float32(2.0), -8.0 * h / NSA_HEADS).astype(np.float32)
    return jnp.asarray(m, dtype=F32).reshape(NSA_KV_HEADS, NSA_GROUP)

def layer_norm(x, g, b):
    xf = x.astype(F32)
    mu = jnp.mean(xf, -1, keepdims=True)
    var = jnp.mean(jnp.square(xf - mu), -1, keepdims=True)
    return ((xf - mu) * lax.rsqrt(var + LN_EPS) * g.astype(F32) + b.astype(F32)).astype(x.dtype)

def l2norm(t):
    tf = t.astype(F32)
    return tf * lax.rsqrt(jnp.sum(tf * tf, -1, keepdims=True) + NORM_EPS)

def causal_dwconv(x, buf, w):
    K = w.shape[0]
    T = x.shape[1]
    ext = jnp.concatenate([buf.astype(x.dtype), x], axis=1)
    y = sum(ext[:, j:j + T] * w[j] for j in range(K))
    return y, ext[:, T:]

def compress_kv(kv, pe, w1, w2):
    B, L = kv.shape[:2]
    nc = L // NSA_BLOCK
    blk = kv[:, :nc * NSA_BLOCK].reshape(B, nc, NSA_BLOCK, NSA_KV_HEADS, 2, HEAD_DIM)
    blk = blk + pe[None, None, :, None]
    flat = blk.transpose(0, 1, 3, 4, 2, 5).reshape(B, nc, NSA_KV_HEADS, 2, NSA_BLOCK * HEAD_DIM)
    hid = jax.nn.silu(jnp.einsum('bngcf,cfe->bngce', flat, w1))
    return jnp.einsum('bngce,ced->bngcd', hid, w2)

def cmp_slc_block(q, qpos, ck, cv, fetch, n_blocks):
    scale = HEAD_DIM ** -0.5
    slopes = alibi_slopes()[None, None, :, :, None]
    nc = ck.shape[1]
    cpos = jnp.arange(nc, dtype=jnp.int32) * NSA_BLOCK + (NSA_BLOCK - 1)
    dist_c = (qpos[:, None] - cpos[None, :]).astype(F32)
    vm = (cpos[None, :] <= qpos[:, None])[None, :, None, None, :]
    s = jnp.einsum('bqgrd,bngd->bqgrn', q, ck, preferred_element_type=F32) * scale
    s = s - slopes * dist_c[None, :, None, None, :]
    p = jax.nn.softmax(jnp.where(vm, s, NEG), axis=-1) * vm
    o_cmp = jnp.einsum('bqgrn,bngd->bqgrd', p.astype(cv.dtype), cv)
    imp = jnp.pad(p.sum(axis=3), ((0, 0), (0, 0), (0, 0), (0, n_blocks - nc)))
    bidx = jnp.arange(n_blocks, dtype=jnp.int32)[None, :]
    cur = (qpos // NSA_BLOCK)[:, None]
    forced = ((bidx == 0) | (bidx == cur) | (bidx == cur - 1))[None, :, None, :]
    allowed = (bidx * NSA_BLOCK <= qpos[:, None])[None, :, None, :]
    score = jnp.where(allowed, jnp.where(forced, FORCE, imp), NEG)
    top_n = min(NSA_TOP_N, n_blocks)
    _, sel = lax.top_k(score, top_n)
    pos = sel[..., None] * NSA_BLOCK + jnp.arange(NSA_BLOCK, dtype=jnp.int32)
    pos = pos.reshape(*sel.shape[:3], top_n * NSA_BLOCK)
    kv = fetch(pos)
    ks, vs = kv[..., 0, :], kv[..., 1, :]
    s2 = jnp.einsum('bqgrd,bqgnd->bqgrn', q, ks, preferred_element_type=F32) * scale
    dist_s = (qpos[None, :, None, None] - pos).astype(F32)[:, :, :, None, :]
    s2 = s2 - slopes * dist_s
    m2 = (pos <= qpos[None, :, None, None])[:, :, :, None, :]
    p2 = jax.nn.softmax(jnp.where(m2, s2, NEG), axis=-1)
    o_slc = jnp.einsum('bqgrn,bqgnd->bqgrd', p2.astype(vs.dtype), vs)
    return o_cmp, o_slc

def sweep_queries(fn, q, qpos, qb):
    B, Q = q.shape[:2]
    if Q <= qb or Q % qb:
        return fn(q, qpos)
    n = Q // qb
    qs = jnp.swapaxes(q.reshape(B, n, qb, *q.shape[2:]), 0, 1)
    outs = lax.map(lambda a: fn(a[0], a[1]), (qs, qpos.reshape(n, qb)))
    return tuple(jnp.swapaxes(o, 0, 1).reshape(B, Q, *o.shape[3:]) for o in outs)

def window_core(q, qpos, kv, kpos):
    scale = HEAD_DIM ** -0.5
    slopes = alibi_slopes()[None, None, :, :, None]
    s = jnp.einsum('bqgrd,bkgd->bqgrk', q, kv[..., 0, :], preferred_element_type=F32) * scale
    dist = qpos[:, None] - kpos[None, :]
    s = s - slopes * dist.astype(F32)[None, :, None, None, :]
    m = ((kpos[None, :] >= 0) & (dist >= 0) & (dist < NSA_WINDOW))[None, :, None, None, :]
    p = jax.nn.softmax(jnp.where(m, s, NEG), axis=-1)
    return jnp.einsum('bqgrk,bkgd->bqgrd', p.astype(kv.dtype), kv[..., 1, :])

def window_prompt(q, kv):
    B, S = q.shape[:2]
    qb = WIN_QBLOCK if S % WIN_QBLOCK == 0 else S
    nb = S // qb
    span = NSA_WINDOW + qb
    kvp = jnp.pad(kv, ((0, 0), (NSA_WINDOW, 0), (0, 0), (0, 0), (0, 0)))
    idx = jnp.arange(nb, dtype=jnp.int32)[:, None] * qb + jnp.arange(span, dtype=jnp.int32)[None, :]
    kv_blk = kvp[:, idx]
    kpos = idx - NSA_WINDOW
    qpos = jnp.arange(S, dtype=jnp.int32).reshape(nb, qb)
    q_blk = q.reshape(B, nb, qb, *q.shape[2:])
    o = jax.vmap(window_core, in_axes=(1, 0, 1, 0), out_axes=1)(q_blk, qpos, kv_blk, kpos)
    return o.reshape(q.shape)

def combine_branches(gates, o_cmp, o_slc, o_win):
    B, T = gates.shape[:2]
    g = jax.nn.sigmoid(gates.astype(F32)).reshape(B, T, NSA_KV_HEADS, NSA_GROUP, 3).astype(o_cmp.dtype)
    o = g[..., 0:1] * o_cmp + g[..., 1:2] * o_slc + g[..., 2:3] * o_win
    return o.reshape(B, T, NSA_WIDTH)

def nsa_prompt(q, kv_cmp, kv_slc, kv_win, gates, pe, w1, w2):
    B, S = q.shape[:2]
    ckv = compress_kv(kv_cmp, pe, w1, w2)
    ck, cv = ckv[..., 0, :], ckv[..., 1, :]
    n_blocks = -(-S // NSA_BLOCK)
    b_ix = jnp.arange(B)[:, None, None, None]
    g_ix = jnp.arange(NSA_KV_HEADS)[None, None, :, None]

    def fetch(pos):
        return kv_slc[b_ix, jnp.minimum(pos, S - 1), g_ix]

    o_cmp, o_slc = sweep_queries(lambda qq, pp: cmp_slc_block(qq, pp, ck, cv, fetch, n_blocks),
                                 q, jnp.arange(S, dtype=jnp.int32), SLC_QBLOCK)
    o_win = window_prompt(q, kv_win)
    return combine_branches(gates, o_cmp, o_slc, o_win)

def nsa_sample(q, kv_cmp, kv_slc, kv_win, gates, pe, w1, w2, cache_cmp, cache_slc, win_buf, page_table, layer):
    B, T = q.shape[:2]
    page = cache_cmp.shape[2]
    past = page_table.shape[1] * page
    past_cmp = cache_cmp[layer, page_table].reshape(B, past, NSA_KV_HEADS, 2, HEAD_DIM)
    ckv = compress_kv(jnp.concatenate([past_cmp, kv_cmp.astype(past_cmp.dtype)], axis=1), pe, w1, w2)
    ck, cv = ckv[..., 0, :], ckv[..., 1, :]
    n_blocks = -(-(past + T) // NSA_BLOCK)
    qpos = past + jnp.arange(T, dtype=jnp.int32)
    b_ix = jnp.arange(B)[:, None, None, None]
    g_ix = jnp.arange(NSA_KV_HEADS)[None, None, :, None]

    def fetch(pos):
        pp = jnp.minimum(pos, past - 1)
        phys = page_table[b_ix, pp // page]
        from_pool = cache_slc[layer, phys, pp % page, g_ix]
        from_new = kv_slc[b_ix, jnp.clip(pos - past, 0, T - 1), g_ix].astype(from_pool.dtype)
        return jnp.where((pos < past)[..., None, None], from_pool, from_new)

    o_cmp, o_slc = sweep_queries(lambda qq, pp: cmp_slc_block(qq, pp, ck, cv, fetch, n_blocks),
                                 q, qpos, SLC_QBLOCK)
    wb = win_buf.shape[1]
    keys = jnp.concatenate([win_buf.astype(kv_win.dtype), kv_win], axis=1)
    kpos = past - wb + jnp.arange(wb + T, dtype=jnp.int32)
    o_win = window_core(q, qpos, keys, kpos)
    return combine_branches(gates, o_cmp, o_slc, o_win), keys[:, -wb:]

def chunk_gated_delta(q, k, v, g, beta, s0):
    B, T, H, Dk = q.shape
    Dv = v.shape[-1]
    C = GDN_CHUNK
    n = -(-T // C)
    pad = n * C - T

    def prep(t):
        t = jnp.pad(t.astype(F32), ((0, 0), (0, pad)) + ((0, 0),) * (t.ndim - 2))
        return jnp.moveaxis(t.reshape(B, n, C, H, *t.shape[3:]), 3, 1)

    q, k, v, g, beta = prep(q), prep(k), prep(v), prep(g), prep(beta)
    G = jnp.cumsum(g, axis=-1)
    tril = jnp.tril(jnp.ones((C, C), dtype=bool))
    eye = jnp.eye(C, dtype=F32)
    decay = jnp.exp(jnp.where(tril, G[..., :, None] - G[..., None, :], -jnp.inf))
    kb = k * beta[..., None]
    A = jnp.where(tril & (eye == 0), jnp.einsum('bhncd,bhnsd->bhncs', kb, k) * decay, 0.0)
    Tm = lax.linalg.triangular_solve(eye + A, jnp.broadcast_to(eye, A.shape), left_side=True, lower=True)
    u = Tm @ (v * beta[..., None])
    w = Tm @ (kb * jnp.exp(G)[..., None])
    qk = jnp.einsum('bhncd,bhnsd->bhncs', q, k) * decay
    qg = q * jnp.exp(G)[..., None]
    kd = k * jnp.exp(G[..., -1:] - G)[..., None]
    gl = jnp.exp(G[..., -1])
    xs = tuple(jnp.moveaxis(t, 2, 0) for t in (qg, qk, u, w, kd, gl))

    def step(S, xs_n):
        qg_n, qk_n, u_n, w_n, kd_n, gl_n = xs_n
        v_new = u_n - w_n @ S
        o = qg_n @ S + qk_n @ v_new
        S = S * gl_n[..., None, None] + jnp.swapaxes(kd_n, -1, -2) @ v_new
        return S, o

    S, o = lax.scan(step, s0.astype(F32), xs)
    o = jnp.transpose(o, (1, 0, 3, 2, 4)).reshape(B, n * C, H, Dv)[:, :T]
    return o, S

def gated_deltanet(qkv, z, a, b, conv_buf, s0, conv_w, a_log, dt_bias, norm_g):
    B, T, _ = qkv.shape
    c, new_buf = causal_dwconv(qkv, conv_buf, conv_w)
    c = jax.nn.silu(c)
    q, k, v = [t.reshape(B, T, GDN_HEADS, HEAD_DIM) for t in jnp.split(c, 3, axis=-1)]
    q = l2norm(q) * (HEAD_DIM ** -0.5)
    k = l2norm(k)
    beta = jax.nn.sigmoid(b.astype(F32))
    g = -jnp.exp(a_log.astype(F32)) * jax.nn.softplus(a.astype(F32) + dt_bias.astype(F32))
    o, S = chunk_gated_delta(q, k, v.astype(F32), g, beta, s0)
    o = o * lax.rsqrt(jnp.mean(o * o, -1, keepdims=True) + NORM_EPS) * norm_g.astype(F32)
    o = o * jax.nn.silu(z.astype(F32).reshape(B, T, GDN_HEADS, HEAD_DIM))
    return o.reshape(B, T, GDN_WIDTH), S, new_buf

def conv_ffn(x, buf, w_up, conv_w, w_down):
    u, v = jnp.split(x @ w_up, 2, axis=-1)
    uc, new_buf = causal_dwconv(u, buf, conv_w)
    return (jax.nn.gelu(uc) * v) @ w_down, new_buf

def run_layer(x, nsa_fn, gdn_s0, gdn_buf, ffn_buf, w_in, w_o, gdn_conv_w, gdn_a_log, gdn_dt_bias,
              gdn_norm_g, ln1_g, ln1_b, ffn_w_up, ffn_conv_w, ffn_w_down, ln2_g, ln2_b):
    B, T, _ = x.shape
    q, kvc, kvs, kvw, gates, qkv, z, a, b = jnp.split(x @ w_in, split_sizes(), axis=-1)
    kvc, kvs, kvw = [t.reshape(B, T, NSA_KV_HEADS, 2, HEAD_DIM) for t in (kvc, kvs, kvw)]
    q5 = q.reshape(B, T, NSA_KV_HEADS, NSA_GROUP, HEAD_DIM)
    o_nsa, win_state = nsa_fn(q5, kvc, kvs, kvw, gates)
    o_gdn, s_new, gbuf = gated_deltanet(qkv, z, a, b, gdn_buf, gdn_s0, gdn_conv_w, gdn_a_log,
                                        gdn_dt_bias, gdn_norm_g)
    mixed = jnp.concatenate([o_nsa.astype(x.dtype), o_gdn.astype(x.dtype)], axis=-1) @ w_o
    h = layer_norm(DN_ALPHA * x + mixed, ln1_g, ln1_b)
    f, fbuf = conv_ffn(h, ffn_buf, ffn_w_up, ffn_conv_w, ffn_w_down)
    y = layer_norm(DN_ALPHA * h + f, ln2_g, ln2_b)
    return y, (kvc, kvs, win_state, s_new.astype(x.dtype), gbuf, fbuf)

def setup_inputs(seed: int = 0) -> dict:
    key = jax.random.key(seed)
    ks = jax.random.split(key, 32)
    n_pages = PAST_LEN // PAGE_SIZE
    n_pool = (DEC_BATCH * n_pages * 5) // 4
    wb = min(NSA_WINDOW, PAST_LEN)

    def nrm(k, shape, s=1.0):
        return jax.random.normal(k, shape, F32) * s

    page_table = jax.random.permutation(ks[8], n_pool)[:DEC_BATCH * n_pages]
    page_table = page_table.reshape(DEC_BATCH, n_pages).astype(jnp.int32)
    dt = jnp.exp(jax.random.uniform(ks[14], (DEPTH, GDN_HEADS), F32, math.log(1e-3), math.log(1e-1)))
    return {
        'x_prompt': nrm(ks[0], (BATCH, SEQ, D_MODEL)),
        'x_sample': nrm(ks[1], (DEC_BATCH, DEC_SEQ, D_MODEL)),
        'cache_cmp_kv': nrm(ks[2], (DEPTH, n_pool, PAGE_SIZE, NSA_KV_HEADS, 2, HEAD_DIM)),
        'cache_slc_kv': nrm(ks[3], (DEPTH, n_pool, PAGE_SIZE, NSA_KV_HEADS, 2, HEAD_DIM)),
        'cache_win_kv': nrm(ks[4], (DEPTH, DEC_BATCH, wb, NSA_KV_HEADS, 2, HEAD_DIM)),
        'state_gdn': nrm(ks[5], (DEPTH, DEC_BATCH, GDN_HEADS, HEAD_DIM, HEAD_DIM), 0.5),
        'state_gdn_conv': nrm(ks[6], (DEPTH, DEC_BATCH, GDN_CONV - 1, 3 * GDN_WIDTH)),
        'state_ffn_conv': nrm(ks[7], (DEPTH, DEC_BATCH, FFN_CONV - 1, D_FF)),
        'page_table': page_table,
        'w_in': nrm(ks[9], (DEPTH, D_MODEL, IN_COLS), D_MODEL ** -0.5),
        'w_o': nrm(ks[10], (DEPTH, MIX_WIDTH, D_MODEL), DN_BETA * MIX_WIDTH ** -0.5),
        'cmp_pe': nrm(ks[11], (DEPTH, NSA_BLOCK, 2, HEAD_DIM), 0.02),
        'cmp_w1': nrm(ks[12], (DEPTH, 2, NSA_BLOCK * HEAD_DIM, HEAD_DIM), (NSA_BLOCK * HEAD_DIM) ** -0.5),
        'cmp_w2': nrm(ks[13], (DEPTH, 2, HEAD_DIM, HEAD_DIM), HEAD_DIM ** -0.5),
        'gdn_conv_w': nrm(ks[15], (DEPTH, GDN_CONV, 3 * GDN_WIDTH), GDN_CONV ** -0.5),
        'gdn_a_log': jnp.log(jax.random.uniform(ks[16], (DEPTH, GDN_HEADS), F32, 1.0, 16.0)),
        'gdn_dt_bias': dt + jnp.log(-jnp.expm1(-dt)),
        'gdn_norm_g': 1.0 + nrm(ks[17], (DEPTH, HEAD_DIM), 0.02),
        'ln1_g': 1.0 + nrm(ks[18], (DEPTH, D_MODEL), 0.02),
        'ln1_b': nrm(ks[19], (DEPTH, D_MODEL), 0.02),
        'ffn_w_up': nrm(ks[20], (DEPTH, D_MODEL, 2 * D_FF), D_MODEL ** -0.5),
        'ffn_conv_w': nrm(ks[21], (DEPTH, FFN_CONV, D_FF), FFN_CONV ** -0.5),
        'ffn_w_down': nrm(ks[22], (DEPTH, D_FF, D_MODEL), DN_BETA * D_FF ** -0.5),
        'ln2_g': 1.0 + nrm(ks[23], (DEPTH, D_MODEL), 0.02),
        'ln2_b': nrm(ks[24], (DEPTH, D_MODEL), 0.02),
    }

def reference(x_prompt, x_sample, cache_cmp_kv, cache_slc_kv, cache_win_kv, state_gdn, state_gdn_conv,
              state_ffn_conv, page_table, w_in, w_o, cmp_pe, cmp_w1, cmp_w2, gdn_conv_w, gdn_a_log,
              gdn_dt_bias, gdn_norm_g, ln1_g, ln1_b, ffn_w_up, ffn_conv_w, ffn_w_down, ln2_g, ln2_b):
    B, S, _ = x_prompt.shape
    dtype = x_prompt.dtype
    xp, xs = x_prompt, x_sample
    p_states, s_states = [], []
    for l in range(DEPTH):
        shared = (w_in[l], w_o[l], gdn_conv_w[l], gdn_a_log[l], gdn_dt_bias[l], gdn_norm_g[l],
                  ln1_g[l], ln1_b[l], ffn_w_up[l], ffn_conv_w[l], ffn_w_down[l], ln2_g[l], ln2_b[l])
        pe, w1, w2 = cmp_pe[l], cmp_w1[l], cmp_w2[l]

        def nsa_p(q, kc, kslc, kw, g, pe=pe, w1=w1, w2=w2):
            return nsa_prompt(q, kc, kslc, kw, g, pe, w1, w2), kw[:, -min(NSA_WINDOW, S):]

        def nsa_s(q, kc, kslc, kw, g, pe=pe, w1=w1, w2=w2, l=l):
            return nsa_sample(q, kc, kslc, kw, g, pe, w1, w2, cache_cmp_kv, cache_slc_kv,
                              cache_win_kv[l], page_table, l)

        xp, st_p = run_layer(xp, nsa_p,
                             jnp.zeros((B, GDN_HEADS, HEAD_DIM, HEAD_DIM), dtype),
                             jnp.zeros((B, GDN_CONV - 1, 3 * GDN_WIDTH), dtype),
                             jnp.zeros((B, FFN_CONV - 1, D_FF), dtype), *shared)
        xs, st_s = run_layer(xs, nsa_s, state_gdn[l], state_gdn_conv[l], state_ffn_conv[l], *shared)
        p_states.append(st_p)
        s_states.append(st_s)

    def stk(states, i):
        return jnp.stack([st[i] for st in states], axis=0)

    return (xp, xs,
            stk(p_states, 0), stk(p_states, 1), stk(p_states, 2), stk(p_states, 3), stk(p_states, 4), stk(p_states, 5),
            stk(s_states, 0), stk(s_states, 1), stk(s_states, 2), stk(s_states, 3), stk(s_states, 4), stk(s_states, 5))


_drawn_inputs = setup_inputs


def setup_inputs(seed=0):
    import zlib

    import numpy as np

    out = dict(_drawn_inputs(seed))
    spreads = {}
    factors = {'cmp_pe': 40.032,
     'gdn_norm_g': 21.846,
     'ln1_g': 2.701,
     'ln1_b': 2.752,
     'ln2_g': 23.354,
     'ln2_b': 23.221,
     'cache_slc_kv': 5.639}
    for name, (base, spread) in spreads.items():
        noise = np.random.default_rng([zlib.crc32(name.encode()), seed]).standard_normal(out[name].shape)
        drawn = base * np.exp(spread * noise) if base else spread * noise
        out[name] = __import__('jax').numpy.asarray(drawn.astype(out[name].dtype))
    for name, factor in factors.items():
        out[name] = (out[name] * factor).astype(out[name].dtype)
    return out
```

```python
import numpy as np
import concourse.bass as bass
from concourse import mybir
from contextlib import ExitStack

F32 = mybir.dt.float32
I32 = mybir.dt.int32
ACT = mybir.ActivationFunctionType
ALU = mybir.AluOpType
AX = mybir.AxisListType.X

P = 128
DM = 2048
SEQ = 512
B, T = 8, 4
NS = B * T
TOK = SEQ + NS
PAST, PAGE = 2048, 128
NPG = PAST // PAGE
NPOOL = B * NPG * 5 // 4
HD = 128
H, KVH = 8, 2
GRP = H // KVH
BLK = 64
NB = PAST // BLK
NBT = NB + 1
WIN = 512
GH = 8
KT = DM // P
FF = 11 * DM // 4
FT = FF // P
QT = SEQ // P
KVC = KVH * 2 * HD
O_KV = H * HD
O_GATE = O_KV + 3 * KVC
O_QKV = O_GATE + 3 * H
O_Z = O_QKV + 3 * GH * HD
O_AB = O_Z + GH * HD
G_FIRST = O_GATE // 512
G_ALL = (O_AB - 3 * H) // 512
ALPHA = 2.0 ** 0.25
SCALE = HD ** -0.5
BIG = 1e33
R_Q, R_KV, R_QKV = 0, O_KV, O_GATE
R_Z = R_QKV + 3 * GH * HD


def shape_constants():
    i = np.arange(P)
    c = {"ident": np.eye(P), "ones": np.ones((P, P)), "upto": (i[:, None] <= i[None, :])}
    lv = []
    for l in range(7):
        s = 1 << l
        same = (i[:, None] // (2 * s)) == (i[None, :] // (2 * s))
        lv.append(same & ((i[:, None] // s) % 2 == 0) & ((i[None, :] // s) % 2 == 1))
    c["level"] = np.concatenate(lv, 1)
    same = (i[:, None] // T == i[None, :NS] // T) & (i[:, None] < NS)
    c["s_upto"] = same & (i[:, None] <= i[None, :NS])
    c["s_same"] = same
    c["s_batch"] = (i[:, None] // T == np.arange(B)[None, :])
    d = i[:, None] - np.arange(SEQ)[None, :] + SEQ - P
    c["dist"] = np.where(d >= 0, d, BIG)
    q = i[:, None, None] + P * np.arange(QT)[None, :, None]
    d = q - (BLK * np.arange(SEQ // BLK)[None, None, :] + BLK - 1)
    c["dist_c"] = np.where(d >= 0, d, BIG).reshape(P, -1)
    c["seen_c"] = (q[:, :, 0] >= BLK - 1)
    slope = 2.0 ** -(np.arange(H) + 1.0)
    c["slope"] = np.broadcast_to(-slope, (P, H))
    j, r, t = i // 32, (i % 32) // T, i % T
    real = (i % 32) < GRP * T
    sl = np.where(real, slope[(j % 2) * GRP + r % GRP], 0)[:, None]
    key = np.arange(PAST + T)[None, :]
    d = PAST + t[:, None] - key
    c["ali_s"] = np.where(d >= 0, -sl * d, -1e30)
    d = d[:, PAST - WIN:]
    c["ali_w"] = np.where((d >= 0) & (d < WIN), -sl * d, -1e30)
    c["ali_c"] = -sl * (PAST + t[:, None] - (BLK * np.arange(NB)[None, :] + BLK - 1))
    forced = np.zeros(NBT)
    forced[[0, NBT - 2, NBT - 1]] = 1
    c["unforced"] = np.broadcast_to(1 - forced, (P, NBT))
    c["forced"] = np.broadcast_to(1e4 * forced, (P, NBT))
    c["same_q"] = (j[:, None] == j[None, :]) & (t[:, None] == t[None, :]) & real[:, None] & real[None, :]
    at, parts, n = {}, [], 0
    for k, v in c.items():
        at[k] = (n, n + v.shape[1])
        n += v.shape[1]
        parts.append(np.asarray(v, np.float32))
    return np.concatenate(parts, 1), at


class Count:

    def __init__(self, eng, sem, base=0):
        self.eng, self.sem, self.base, self.n = eng, sem, base, 0

    def link(self, ins):
        self.n += 1
        ins.then_inc(self.sem, 1)
        self.eng.wait_ge(self.sem, self.base + self.n)


def build(nc, A, O, C_dram, AT):
    top = ExitStack()
    with top:
        held = []

        def sem(name):
            held.append(nc.alloc_semaphore(name=name))
            return held[-1]

        def clear_semaphores():
            nc.clear_and_free_semaphores(held)
            held.clear()
            nc.all_engine_barrier()

        def sb(ctx, name, shape, dt=F32):
            return ctx.enter_context(nc.sbuf_tensor(name, shape, dt))

        def banks(ctx, name):
            return [ctx.enter_context(nc.psum_tensor(f"{name}{i}", [P, 512], F32)) for i in range(8)]

        S_proj = nc.dram_tensor("s_proj", (G_ALL * 512, TOK), F32, kind="Internal").ap()
        S_xt = nc.dram_tensor("s_xt", (KT, P, TOK), F32, kind="Internal").ap()
        S_gate = nc.dram_tensor("s_gate", (NS, 3 * H), F32, kind="Internal").ap()

        C_N = AT["upto"][0]
        CS = sb(top, "consts", [P, C_N])
        GAB = sb(top, "gab", [P, QT + 1, 40])

        def cst(name, rows=P):
            a, b = AT[name]
            return CS[0:rows, a:b]

        ident = cst("ident")

        main = ExitStack()
        top.enter_context(main)
        XT = sb(main, "xt", [P, KT, TOK])
        c_sem = sem("consts_in")
        with ExitStack() as ph:
            xn = sb(ph, "x_nat", [P, QT + 1, DM])
            ps = banks(ph, "a")
            x_in, tr, ev_v, ev_a = (sem(n) for n in ("x_in", "x_tr", "x_ev_v", "x_ev_a"))
            block = ph.enter_context(nc.Block())

            @block.sync
            def _(sp):
                sp.dma_start(CS[:, :], C_dram[:, 0:C_N]).then_inc(c_sem, 16)
                sp.dma_start(xn[:, 0:QT, :], A["x_prompt"][0].rearrange("(t p) d -> p t d", p=P)).then_inc(x_in, 16)
                sp.dma_start(xn[0:NS, QT, :], A["x_sample"].rearrange("b t d -> (b t) d")).then_inc(x_in, 16)
                sp.wait_ge(ev_v, 10)
                sp.wait_ge(ev_a, 10)

            @block.tensor
            def _(pe):
                pe.wait_ge(c_sem, 16)
                pe.wait_ge(x_in, 32)
                for u in range(20):
                    tt, kg = u // 4, u % 4
                    n = P if tt < QT else NS
                    if u >= 8:
                        pe.wait_ge(ev_v if u % 2 == 0 else ev_a, (u - 8) // 2 + 1)
                    for k in range(4):
                        last = nc.tensor.transpose(ps[u % 8][:, k * n:(k + 1) * n],
                                                   xn[0:n, tt, (kg * 4 + k) * P:(kg * 4 + k + 1) * P],
                                                   ident[0:n, 0:n])
                    last.then_inc(tr, 1)

            def evac(eng, copy, par, s):
                for u in range(par, 20, 2):
                    tt, kg = u // 4, u % 4
                    n = P if tt < QT else NS
                    eng.wait_ge(tr, u + 1)
                    copy(XT[:, kg * 4:kg * 4 + 4, tt * P:tt * P + n],
                         ps[u % 8][:, 0:4 * n].rearrange("p (k n) -> p k n", k=4)).then_inc(s, 1)

            @block.vector
            def _(dve):
                evac(dve, nc.vector.tensor_copy, 0, ev_v)

            @block.scalar
            def _(act):
                evac(act, nc.scalar.copy, 1, ev_a)

        W_in = A["w_in"][0].rearrange("(k p) n -> p k n", p=P)
        with ExitStack() as ph:
            W = sb(ph, "w_ring", [P, 4, KT, P])
            WG = sb(ph, "w_small", [P, KT, 40])
            ST = sb(ph, "stage", [P, 4, TOK])
            tmp = sb(ph, "g_tmp", [P, QT + 1, 16])
            par = sb(ph, "g_par", [P, 2, GH])
            ps = banks(ph, "b")
            w_in = [sem(f"w_in{i}") for i in range(4)]
            st_out = [sem(f"st_out{i}") for i in range(4)]
            acc, ev, wg, sm, smd, small, gs = (sem(n) for n in ("acc", "acc_ev", "wg_in", "sm_ps", "sm_done", "par_in", "gs_out"))
            dch, ach, sx = (sem(n) for n in ("ch2_v", "ch2_a", "sm_exp"))
            block = ph.enter_context(nc.Block())

            @block.sync
            def _(sp):
                for n in range(4):
                    sp.dma_start(W[:, n], W_in[:, :, n * P:(n + 1) * P]).then_inc(w_in[n], 16)
                sp.dma_start(S_xt.rearrange("k p n -> p k n"), XT[:]).then_inc(gs, 16)
                sp.dma_start(WG[:, :, 0:24], W_in[:, :, O_GATE:O_QKV]).then_inc(wg, 16)
                sp.dma_start(WG[:, :, 24:40], W_in[:, :, O_AB:O_AB + 16]).then_inc(wg, 16)
                sp.dma_start(par[:, 0, :], A["gdn_a_log"].partition_broadcast(P)[:, 0, :]).then_inc(small, 16)
                sp.dma_start(par[:, 1, :], A["gdn_dt_bias"].partition_broadcast(P)[:, 0, :]).then_inc(small, 16)
                for lo, hi, off in ((1, G_FIRST, 0), (G_FIRST, G_ALL, 24)):
                    with sp.Fori(lo, hi) as g:
                        for n in range(4):
                            sp.wait_ge(acc, g * 4 + n - 3)
                            sp.dma_start(W[:, n], W_in[:, :, bass.ds(g * 512 + (n * P + off), P)]).then_inc(w_in[n], 16)
                sp.wait_ge(smd, 1)
                sp.dma_start(S_gate[:, :], GAB[0:NS, QT, 0:24]).then_inc(gs, 16)
                sp.wait_ge(gs, 32)

            @block.tensor
            def _(pe):
                with pe.Fori(0, G_ALL) as g:
                    for n in range(4):
                        pe.wait_ge(w_in[n], g * 16 + 16)
                        pe.wait_ge(ev, g * 4 + n + 1)
                        a, b = ps[2 * (n % 2)], ps[2 * (n % 2) + 1]
                        for k in range(KT):
                            nc.tensor.matmul(a[:, :], W[:, n, k], XT[:, k, 0:SEQ], start=k == 0, stop=k == KT - 1)
                            last = nc.tensor.matmul(b[:, 0:NS], W[:, n, k], XT[:, k, SEQ:TOK], start=k == 0, stop=k == KT - 1)
                        last.then_inc(acc, 1)
                pe.wait_ge(wg, 32)
                for tt in range(QT + 1):
                    n = P if tt < QT else NS
                    for k in range(KT):
                        last = nc.tensor.matmul(ps[4 if tt < QT else 5][0:n, (tt % QT) * 40:(tt % QT) * 40 + 40], XT[:, k, tt * P:tt * P + n], WG[:, k],
                                                start=k == 0, stop=k == KT - 1)
                last.then_inc(sm, 1)

            @block.scalar
            def _(act):
                act.sem_inc(ev, 2)
                for n in range(4):
                    act.sem_inc(st_out[n], 16)
                with act.Fori(0, G_ALL) as g:
                    for n in range(4):
                        act.wait_ge(acc, g * 4 + n + 1)
                        act.wait_ge(st_out[n], g * 16 + 16)
                        nc.scalar.copy(ST[:, n, 0:SEQ], ps[2 * (n % 2)][:, :])
                        nc.scalar.copy(ST[:, n, SEQ:TOK], ps[2 * (n % 2) + 1][:, 0:NS]).then_inc(ev, 1)
                        act.wait_ge(ev, g * 4 + n + 3)
                        act.dma_start(S_proj[bass.ds(g * 512 + n * P, P), :], ST[:, n]).then_inc(st_out[n], 16)
                for n in range(4):
                    act.wait_ge(st_out[n], 16 * G_ALL + 16)
                ch = Count(act, ach)
                act.wait_ge(small, 32)
                nc.scalar.activation(par[:, 0, :], par[:, 0, :], ACT.Exp).then_inc(sx, 1)
                act.wait_ge(dch, 4)
                nc.scalar.activation(tmp[:, 0:QT, 8:16], tmp[:, 0:QT, 8:16], ACT.Exp, scale=-1.0)
                ch.link(nc.scalar.activation(tmp[0:NS, QT, 8:16], tmp[0:NS, QT, 8:16], ACT.Exp, scale=-1.0))
                nc.scalar.activation(tmp[:, 0:QT, 8:16], tmp[:, 0:QT, 8:16], ACT.Ln, bias=1.0)
                nc.scalar.activation(tmp[0:NS, QT, 8:16], tmp[0:NS, QT, 8:16], ACT.Ln, bias=1.0).then_inc(sx, 1)
                nc.scalar.activation(GAB[:, 0:QT, 0:24], GAB[:, 0:QT, 0:24], ACT.Sigmoid)
                nc.scalar.activation(GAB[0:NS, QT, 0:24], GAB[0:NS, QT, 0:24], ACT.Sigmoid).then_inc(smd, 1)
                nc.scalar.activation(GAB[:, 0:QT, 32:40], GAB[:, 0:QT, 32:40], ACT.Sigmoid)
                nc.scalar.activation(GAB[0:NS, QT, 32:40], GAB[0:NS, QT, 32:40], ACT.Sigmoid).then_inc(smd, 1)
                act.wait_ge(smd, 2)

            @block.vector
            def _(dve):
                dve.wait_ge(sm, 1)
                dve.wait_ge(small, 32)
                ch = Count(dve, dch)
                for rows, tiles in ((P, range(QT)), (NS, [QT])):
                    a, b = tiles[0], tiles[-1] + 1
                    src = ps[4 if rows == P else 5][0:rows, 0:40 * (b - a)].rearrange("p (t c) -> p t c", c=40)
                    dve_dt = par[0:rows, 1:2, :].broadcast_to((rows, b - a, GH))
                    nc.vector.tensor_copy(GAB[0:rows, a:b, :], src)
                    ch.link(nc.vector.tensor_tensor(tmp[0:rows, a:b, 0:8], src[:, :, 24:32], dve_dt, ALU.add))
                    ch.link(nc.vector.scalar_tensor_tensor(tmp[0:rows, a:b, 8:16], tmp[0:rows, a:b, 0:8], -1.0, tmp[0:rows, a:b, 0:8], ALU.mult, ALU.max))
                dve.wait_ge(sx, 2)
                for rows, tiles in ((P, range(QT)), (NS, [QT])):
                    a, b = tiles[0], tiles[-1] + 1
                    v = tmp[0:rows, a:b]
                    ea = par[0:rows, 0:1, :].broadcast_to((rows, b - a, GH))
                    ch.link(nc.vector.scalar_tensor_tensor(v[:, :, 0:8], v[:, :, 0:8], 0.0, v[:, :, 8:16], ALU.max, ALU.add))
                    ch.link(nc.vector.scalar_tensor_tensor(GAB[0:rows, a:b, 24:32], v[:, :, 0:8], -1.0, ea, ALU.mult, ALU.mult))

        main.close()

        with ExitStack() as ph:
            KV = sb(ph, "kv_t", [P, 12, TOK])
            NAT = sb(ph, "kv_nat", [P, QT + 1, 3 * KVC])
            ps = banks(ph, "c")
            kv_in, tr, ev_v, ev_a, out = (sem(n) for n in ("kv_in", "kv_tr", "kv_ev_v", "kv_ev_a", "kv_out"))
            block = ph.enter_context(nc.Block())

            @block.sync
            def _(sp):
                sp.dma_start(KV[:], S_proj[R_KV:R_KV + 1536].rearrange("(k p) n -> p k n", p=P)).then_inc(kv_in, 16)
                for b in range(B):
                    sp.dma_start(O[10][0, b, 0:WIN - T].rearrange("t g c d -> t (g c d)"),
                                 A["cache_win_kv"][0, b, T:WIN].rearrange("t g c d -> t (g c d)")).then_inc(out, 16)
                sp.wait_ge(ev_v, 8)
                sp.wait_ge(ev_a, 7)
                for i in range(3):
                    cols = slice(i * KVC, (i + 1) * KVC)
                    sp.dma_start(O[2 + i][0, 0].rearrange("(t p) g c d -> p t (g c d)", p=P), NAT[:, 0:QT, cols]).then_inc(out, 16)
                    if i < 2:
                        sp.dma_start(O[8 + i][0].rearrange("b t g c d -> (b t) (g c d)"), NAT[0:NS, QT, cols]).then_inc(out, 16)
                    else:
                        for b in range(B):
                            sp.dma_start(O[10][0, b, WIN - T:WIN].rearrange("t g c d -> t (g c d)"),
                                         NAT[b * T:(b + 1) * T, QT, cols]).then_inc(out, 16)
                sp.wait_ge(out, 16 * (2 * B + 5))

            @block.tensor
            def _(pe):
                pe.wait_ge(kv_in, 16)
                for u in range(15):
                    tt, i = u // 3, u % 3
                    n = P if tt < QT else NS
                    if u >= 8:
                        pe.wait_ge(ev_v if u % 2 == 0 else ev_a, (u - 8) // 2 + 1)
                    for k in range(4):
                        last = nc.tensor.transpose(ps[u % 8][0:n, k * P:(k + 1) * P], KV[:, i * 4 + k, tt * P:tt * P + n], ident)
                    last.then_inc(tr, 1)

            def evac(eng, copy, par, s):
                for u in range(par, 15, 2):
                    tt, i = u // 3, u % 3
                    n = P if tt < QT else NS
                    eng.wait_ge(tr, u + 1)
                    copy(NAT[0:n, tt, i * KVC:(i + 1) * KVC], ps[u % 8][0:n, :]).then_inc(s, 1)

            @block.vector
            def _(dve):
                evac(dve, nc.vector.tensor_copy, 0, ev_v)

            @block.scalar
            def _(act):
                evac(act, nc.scalar.copy, 1, ev_a)

        DL = HD // 2
        NPB = SEQ // BLK
        CK = sb(top, "ck", [P, B, NB, KVH])
        CV = sb(top, "cv", [NB, B, KVH, HD])
        CKP = sb(top, "ck_p", [P, NPB, KVH])
        CVP = sb(top, "cv_p", [NPB, KVH, HD])
        PT = sb(top, "pages", [1, B * NPG], I32)
        with ExitStack() as ph:
            XC = sb(ph, "xc", [P, 2, 2, NB, 4, DL])
            W1 = sb(ph, "w1", [P, 2, DL, HD])
            W2 = sb(ph, "w2", [P, 2, HD])
            XP = XC[:, 1, 0, 0:NPB + 1]
            HID = sb(ph, "hid", [P, 2, 2 * NB * KVH])
            PEB = sb(ph, "pe_bias", [P, 2])
            ps = banks(ph, "d")
            xc_in = [sem("xc_in0"), sem("xc_in1")]
            w_in4, xp_in, acc, peb, hid, ckv, out4, pt_in = (sem(n) for n in ("w1_in", "xp_in", "c_acc", "peb", "hid", "ckv", "c_out", "pt_in"))
            block = ph.enter_context(nc.Block())
            pages = A["cache_cmp_kv"][0]

            @block.sync
            def _(sp):
                sp.dma_start(PT[:, :], A["page_table"].rearrange("(o b) n -> o (b n)", o=1)).then_inc(pt_in, 16)
                src = O[2][0, 0].rearrange("(n t) g c (h l) -> h t n (g c) l", t=BLK, h=2)
                pe_src = A["cmp_pe"][0].rearrange("t c (h l) -> h t c l", h=2)
                for h in range(2):
                    rows = slice(h * BLK, (h + 1) * BLK)
                    for n in range(NPB):
                        sp.dma_start(XP[rows, n], src[h, :, n]).then_inc(xp_in, 16)
                    for g in range(2):
                        sp.dma_start(XP[rows, NPB, 2 * g:2 * g + 2], pe_src[h]).then_inc(xp_in, 16)
                for c in range(2):
                    w1 = A["cmp_w1"][0, c].rearrange("(t h l) e -> h t (l e)", t=BLK, h=2)
                    for h in range(2):
                        sp.dma_start(W1[h * BLK:(h + 1) * BLK, c].rearrange("p l e -> p (l e)"), w1[h]).then_inc(w_in4, 16)
                sp.dma_start(W2[:], A["cmp_w2"][0].rearrange("c e d -> e c d")).then_inc(w_in4, 16)
                sp.wait_ge(pt_in, 16)
                for i in range(B // 4):
                    for s in range(2):
                        if i or s:
                            sp.wait_ge(acc, i * 4 + 2 * s)
                        for bp in range(2):
                            with sp.Fori(0, NPG) as pg:
                                page = sp.value_load(PT[0:1, bass.ds(pg + (i * 4 + 2 * s + bp) * NPG, 1)], min_val=0, max_val=NPOOL - 1)
                                src = pages[bass.ds(page, 1)].rearrange("o (n t) g c (h l) -> h t (o n) (g c) l", t=BLK, h=2)
                                for h in range(2):
                                    for n in range(2):
                                        sp.dma_start(XC[h * BLK:(h + 1) * BLK, s, bp, bass.ds(pg * 2 + n, 1)].rearrange("p o c l -> p (o c) l"),
                                                     src[h, :, n]).then_inc(xc_in[s], 16)
                sp.wait_ge(ckv, 10)

            @block.tensor
            def _(pe):
                pe.wait_ge(xp_in, 16 * 2 * (NPB + 2))
                pe.wait_ge(w_in4, 80)
                n = (NPB + 1) * KVH
                for c in range(2):
                    for l in range(DL):
                        last = nc.tensor.matmul(ps[c][:, 0:n], W1[:, c, l], XP[:, :, c::2, l], start=l == 0, stop=l == DL - 1)
                    last.then_inc(acc, 1)
                pe.wait_ge(hid, 1)
                nc.tensor.matmul(ps[2][:, 0:NPB * KVH], W2[:, 0], HID[:, 0, 0:NPB * KVH], start=True, stop=True)
                for g in range(KVH):
                    last = nc.tensor.matmul(ps[3][0:NPB, g * HD:(g + 1) * HD], HID[:, 1, g:NPB * KVH:KVH], W2[:, 1], start=True, stop=True)
                last.then_inc(out4, 1)
                with pe.Fori(0, B // 4) as i:
                    for s in range(2):
                        pe.wait_ge(xc_in[s], i * 2048 + 2048)
                        for c in range(2):
                            for l in range(DL):
                                last = nc.tensor.matmul(ps[c][:, 0:2 * NB * KVH], W1[:, c, l], XC[:, s, :, :, c::2, l],
                                                        start=l == 0, stop=l == DL - 1)
                            last.then_inc(acc, 1)
                        pe.wait_ge(hid, i * 2 + s + 2)
                        pe.wait_ge(ckv, i * 4 + 2 * s + 2)
                        nc.tensor.matmul(ps[2][:, 0:2 * NB * KVH], W2[:, 0], HID[:, 0], start=True, stop=True)
                        for u in range(2 * KVH):
                            bp, g = u // KVH, u % KVH
                            last = nc.tensor.matmul(ps[3][0:NB, u * HD:(u + 1) * HD],
                                                    HID[:, 1, bp * NB * KVH + g:(bp + 1) * NB * KVH:KVH], W2[:, 1], start=True, stop=True)
                        last.then_inc(out4, 1)

            @block.scalar
            def _(act):
                act.wait_ge(acc, 2)
                act.wait_ge(peb, 2)
                for c in range(2):
                    last = nc.scalar.activation(HID[:, c, 0:NPB * KVH], ps[c][:, 0:NPB * KVH], ACT.Silu, bias=PEB[:, c:c + 1])
                last.then_inc(hid, 1)
                with act.Fori(0, B // 4) as i:
                    for s in range(2):
                        act.wait_ge(acc, i * 4 + 2 * s + 4)
                        act.wait_ge(out4, i * 2 + s + 1)
                        for c in range(2):
                            last = nc.scalar.activation(HID[:, c], ps[c][:, 0:2 * NB * KVH], ACT.Silu, bias=PEB[:, c:c + 1])
                        last.then_inc(hid, 1)

            @block.vector
            def _(dve):
                dve.wait_ge(acc, 2)
                for c in range(2):
                    nc.vector.tensor_copy(PEB[:, c:c + 1], ps[c][:, NPB * KVH:NPB * KVH + 1]).then_inc(peb, 1)
                dve.wait_ge(out4, 1)
                nc.vector.tensor_copy(CKP[:].rearrange("p n g -> p (n g)"), ps[2][:, 0:NPB * KVH]).then_inc(ckv, 1)
                nc.vector.tensor_copy(CVP[:].rearrange("p g d -> p (g d)"), ps[3][0:NPB, 0:KVH * HD]).then_inc(ckv, 1)
                with dve.Fori(0, B // 4) as i:
                    for s in range(2):
                        dve.wait_ge(out4, i * 2 + s + 2)
                        nc.vector.tensor_copy(CK[:, bass.ds(i * 4 + 2 * s, 2)].rearrange("p b n g -> p (b n g)"),
                                              ps[2][:, 0:2 * NB * KVH]).then_inc(ckv, 1)
                        nc.vector.tensor_copy(CV[:, bass.ds(i * 4 + 2 * s, 2)].rearrange("p b g d -> p (b g d)"), ps[3][0:NB, :]).then_inc(ckv, 1)

        MIX = sb(top, "mix", [P, 2 * GH, TOK])
        with ExitStack() as ph:
            lo, hi = AT["dist"][0], AT["slope"][1]
            CP = sb(ph, "consts_p", [P, hi - lo])

            def cp(name):
                return CP[:, AT[name][0] - lo:AT[name][1] - lo]

            Q = sb(ph, "q_head", [P, SEQ])
            K = sb(ph, "k_t", [P, 2, KVH, SEQ])
            V = sb(ph, "v_rows", [P, QT, 2, KVH, HD])
            BH = sb(ph, "bias", [P, SEQ])
            BC = sb(ph, "bias_c", [P, QT * NPB])
            SC = sb(ph, "scores", [P, 4, SEQ])
            NM = sb(ph, "negmax", [P, 12])
            SU = sb(ph, "sums", [P, 12])
            RI = sb(ph, "inv", [P, 12])
            DG = sb(ph, "diag", [P, 3, P])
            PTS = sb(ph, "p_t", [P, 3, SEQ])
            ps = banks(ph, "e")
            (kv_in, q_in, s_ready, s_taken, m_ready, e_ready, d_ready, pt_ready, pts_ready, o_done, o_out, ch5) = (
                sem("a_" + n) for n in ("kv_in", "q_in", "s_ready", "s_taken", "m_ready", "e_ready", "d_ready", "pt_ready",
                                        "pts_ready", "o_done", "o_out", "ch"))
            block = ph.enter_context(nc.Block())
            JOBS = [(qt, br) for qt in range(QT) for br in range(3)]
            NJ = len(JOBS)

            def width(j):
                qt, br = JOBS[j]
                return NPB if br == 0 else (qt + 1) * P

            @block.sync
            def _(sp):
                sp.dma_start(CP[:, :], C_dram[:, lo:hi]).then_inc(kv_in, 16)
                for i in range(2):
                    for g in range(KVH):
                        r = R_KV + KVC * (i + 1) + g * 2 * HD
                        sp.dma_start(K[:, i, g], S_proj[r:r + P, 0:SEQ]).then_inc(kv_in, 16)
                        sp.dma_start(V[:, :, i, g, :], O[3 + i][0, 0, :, g, 1].rearrange("(t p) d -> p t d", p=P)).then_inc(kv_in, 16)
                sp.dma_start(Q[:, :], S_proj[0:P, 0:SEQ]).then_inc(q_in, 16)
                with sp.Fori(1, H) as h:
                    sp.wait_ge(s_ready, h * NJ)
                    sp.dma_start(Q[:, :], S_proj[bass.ds(h * P, P), 0:SEQ]).then_inc(q_in, 16)
                sp.wait_ge(o_out, 2 + H * QT)

            @block.tensor
            def _(pe):
                pe.sem_inc(pt_ready, 4)
                pe.sem_inc(o_done, 3)
                pe.wait_ge(kv_in, 144)

                def scores(h, g, j):
                    qt, br = JOBS[j]
                    pe.wait_ge(s_taken, h * NJ + j + 1)
                    rhs = CKP[:, :, g] if br == 0 else K[:, br - 1, g, 0:width(j)]
                    nc.tensor.matmul(ps[j % 3][:, 0:width(j)], Q[:, qt * P:(qt + 1) * P], rhs, start=True, stop=True).then_inc(s_ready, 1)

                def turn(h, j):
                    pe.wait_ge(d_ready, h * NJ + j + 1)
                    pe.wait_ge(pts_ready, h * NJ + j + 1)
                    w = width(j)
                    for k in range(-(-w // P)):
                        n = min(P, w)
                        last = nc.tensor.matmul(ps[3 + j % 3][0:n, k * P:(k + 1) * P], SC[:, j % 4, k * P:k * P + n], DG[:, j % 3],
                                                start=True, stop=True)
                    last.then_inc(pt_ready, 1)

                def values(h, g, j):
                    qt, br = JOBS[j]
                    if br == 0:
                        pe.wait_ge(o_out, h * QT + qt + 1)
                    pe.wait_ge(pts_ready, h * NJ + j + 4)
                    o = ps[6 + qt % 2][:, 0:P]
                    if br == 0:
                        last = nc.tensor.matmul(o, CVP[:, g], PTS[0:NPB, j % 3, 0:P], start=True, stop=False)
                    else:
                        for k in range(qt + 1):
                            last = nc.tensor.matmul(o, V[:, k, br - 1, g], PTS[:, j % 3, k * P:(k + 1) * P], start=False,
                                                    stop=br == 2 and k == qt)
                    last.then_inc(o_done, 1)

                for g in range(KVH):
                    with pe.Fori(g * GRP, (g + 1) * GRP) as h:
                        pe.wait_ge(q_in, h * 16 + 16)
                        scores(h, g, 0)
                        scores(h, g, 1)
                        for j in range(NJ):
                            turn(h, j)
                            if j + 2 < NJ:
                                scores(h, g, j + 2)
                            if j:
                                values(h, g, j - 1)
                        values(h, g, NJ - 1)

            @block.scalar
            def _(act):
                act.sem_inc(pts_ready, 3)
                act.sem_inc(o_out, 2)

                def turned(h, j):
                    n = min(P, width(j))
                    w = max(P, width(j))
                    act.wait_ge(pt_ready, h * NJ + j + 5)
                    act.wait_ge(o_done, h * NJ + j + 1)
                    nc.scalar.copy(PTS[0:n, j % 3, 0:w], ps[3 + j % 3][0:n, 0:w]).then_inc(pts_ready, 1)

                def output(h, j):
                    act.wait_ge(o_done, h * NJ + j + 4)
                    nc.scalar.copy(MIX[:, bass.ds(h, 1), JOBS[j][0] * P:(JOBS[j][0] + 1) * P].rearrange("p o n -> p (o n)"),
                                   ps[6 + JOBS[j][0] % 2][:, 0:P]).then_inc(o_out, 1)

                with act.Fori(0, H) as h:
                    for j in range(NJ + 1):
                        if j < NJ:
                            act.wait_ge(m_ready, h * NJ + j + 1)
                            s = SC[:, j % 4, 0:width(j)]
                            nc.scalar.activation(s, s, ACT.Exp, bias=NM[:, j:j + 1], accum_out=SU[:, j:j + 1]).then_inc(e_ready, 1)
                        if j:
                            turned(h, j - 1)
                        if j >= 4 and (j - 4) % 3 == 0:
                            output(h, j - 2)
                    output(h, NJ - 1)

            @block.vector
            def _(dve):
                PER = 2 + NJ + QT
                dve.sem_inc(s_taken, 3)
                dve.wait_ge(kv_in, 144)

                def diag(h, j, ch):
                    qt, br = JOBS[j]
                    dve.wait_ge(e_ready, h * NJ + j + 1)
                    ch.link(nc.vector.reciprocal(RI[:, j:j + 1], SU[:, j:j + 1]))
                    if br == 0:
                        ch.link(nc.vector.tensor_tensor(RI[:, j:j + 1], RI[:, j:j + 1], cp("seen_c")[:, qt:qt + 1], ALU.mult))
                    dve.wait_ge(pt_ready, h * NJ + j + 2)
                    gate = GAB[:, qt, bass.ds(h * 3 + br, 1)]
                    nc.vector.tensor_scalar(DG[:, j % 3], ident, RI[:, j:j + 1], gate, ALU.mult, ALU.mult).then_inc(d_ready, 1)

                with dve.Fori(0, H) as h:
                    ch = Count(dve, ch5, h * PER)
                    slope = cp("slope")[:, bass.ds(h, 1)]
                    ch.link(nc.vector.tensor_scalar(BH[:], cp("dist"), slope, None, ALU.mult))
                    ch.link(nc.vector.tensor_scalar(BC[:], cp("dist_c"), slope, None, ALU.mult))
                    for j in range(NJ + 1):
                        if j < NJ:
                            qt, br = JOBS[j]
                            w = width(j)
                            dve.wait_ge(s_ready, h * NJ + j + 1)
                            dve.wait_ge(pt_ready, h * NJ + j + 1)
                            bias = BC[:, qt * NPB:(qt + 1) * NPB] if br == 0 else BH[:, SEQ - w:]
                            s = SC[:, j % 4, 0:w]
                            ins = nc.vector.scalar_tensor_tensor(s, ps[j % 3][:, 0:w], SCALE, bias, ALU.mult, ALU.add)
                            ins.then_inc(s_taken, 1)
                            dve.wait_ge(s_taken, h * NJ + j + 4)
                            nc.vector.tensor_reduce(NM[:, j:j + 1], s, AX, ALU.max, negate=True).then_inc(m_ready, 1)
                        if j:
                            diag(h, j - 1, ch)
                    assert ch.n == PER

        NG = B // 2
        UN = 2 * KVH
        RW = GRP * T
        with ExitStack() as ph:
            lo, hi = AT["ali_s"][0], AT["same_q"][1]
            CP = sb(ph, "consts_s", [P, hi - lo])

            def cp(name, a=0, b=None):
                x, y = AT[name]
                return CP[:, x - lo + a:(y - lo if b is None else x - lo + b)]

            KN = sb(ph, "k_pages", [P, 2, NPG, KVH, HD])
            VN = sb(ph, "v_pages", [P, 2, NPG, KVH, HD])
            WN = sb(ph, "win_rows", [P, 2, WIN // P, KVH, 2, HD])
            VNEW = sb(ph, "v_new", [T, 2, 2, KVH, HD])
            QA = sb(ph, "q_all", [P, H, NS])
            KA = sb(ph, "k_new", [P, 2, KVH, NS])
            GR = sb(ph, "gates_r", [P, NG * 3])
            QS = sb(ph, "q_units", [P, 2, KVH, 32])
            MK = sb(ph, "misc_keys", [P, 2, KVH, NB + 2 * T])
            CVS = sb(ph, "cv_units", [NB, 2, KVH, HD])
            KTS = sb(ph, "k_t_s", [P, 4, 512])
            SC = sb(ph, "sc_slc", [P, PAST + T])
            SW = sb(ph, "sc_win", [P, WIN + T])
            PC = sb(ph, "sc_cmp", [P, NB])
            SCR = sb(ph, "rank", [P, NBT])
            SCR2 = sb(ph, "rank2", [P, NBT])
            SB8 = sb(ph, "sel_bias", [P, NBT])
            PAD = sb(ph, "pad", [P, 1])
            M8 = sb(ph, "max8", [P, 16])
            ST6 = sb(ph, "stats6", [P, 9])
            DG = sb(ph, "diag6", [P, 3, P])
            PTS = sb(ph, "p_t6", [P, 7, 512])
            ps = banks(ph, "f")
            (c_in, k_in, v_in, w_in6, prep, misc, pc_r, imp, kt_ps, kt_a, kt_v, s_task, s_free, m_r, e_r, d_r, t_ps, pt_a, pt_v, o_r, oe,
             ch6, gz) = (
                sem("s_" + n) for n in ("c_in", "k_in", "v_in", "w_in", "prep", "misc", "pc_r", "imp", "kt_ps", "kt_a", "kt_v", "task",
                                        "free", "m_r", "e_r", "d_r", "t_ps", "pt_a", "pt_v", "o_r", "oe", "ch", "gz"))
            block = ph.enter_context(nc.Block())
            NT = 5 * UN
            slc = A["cache_slc_kv"][0]
            win = A["cache_win_kv"][0]

            @block.sync
            def _(sp):
                sp.dma_start(CP[:, :], C_dram[:, lo:hi]).then_inc(c_in, 16)
                sp.dma_start(QA[:], S_proj[0:H * HD, SEQ:TOK].rearrange("(h p) n -> p h n", p=P)).then_inc(c_in, 16)
                for i in range(2):
                    for g in range(KVH):
                        r = R_KV + KVC * (i + 1) + g * 2 * HD
                        sp.dma_start(KA[:, i, g], S_proj[r:r + P, SEQ:TOK]).then_inc(c_in, 16)
                sp.wait_ge(gz, 1)
                for G in range(NG):
                    for j in range(UN):
                        bp, g = j // KVH, j % KVH
                        b = 2 * G + bp
                        for r in range(GRP):
                            h = g * GRP + r
                            sp.dma_start(GR[32 * j + r * T:32 * j + (r + 1) * T, G * 3:G * 3 + 3],
                                         S_gate[b * T:(b + 1) * T, h * 3:h * 3 + 3]).then_inc(c_in, 16)
                with sp.Fori(0, NG) as G:
                    sp.wait_ge(oe, G + 1)
                    for bp in range(2):
                        b1 = bass.ds(G * 2 + bp, 1)
                        sp.dma_start(WN[:, bp].rearrange("p w g c d -> p w (g c d)"),
                                     win[b1].rearrange("o (w p) g c d -> p (o w) (g c d)", p=P)).then_inc(w_in6, 16)
                        sp.dma_start(VNEW[:, 0, bp], O[9][0, b1, :, :, 1].rearrange("o t g d -> (o t) g d")).then_inc(w_in6, 16)
                        sp.dma_start(VNEW[:, 1, bp], O[10][0, b1, WIN - T:WIN, :, 1].rearrange("o t g d -> (o t) g d")).then_inc(w_in6, 16)
                    for half, dst, s in ((0, KN, k_in), (1, VN, v_in)):
                        for bp in range(2):
                            with sp.Fori(0, NPG) as pg:
                                page = sp.value_load(PT[0:1, bass.ds((G * 2 + bp) * NPG + pg, 1)], min_val=0, max_val=NPOOL - 1)
                                sp.dma_start(dst[:, bp, bass.ds(pg, 1)].rearrange("p o g d -> p (o g) d"),
                                             slc[bass.ds(page, 1), :, :, half].rearrange("o t g d -> (o t) g d")).then_inc(s, 16)
                sp.wait_ge(oe, NG + 1)

            @block.gpsimd
            def _(gp):
                nc.gpsimd.memset(GR[:], 0.0).then_inc(gz, 1)
                nc.gpsimd.memset(QS[:], 0.0).then_inc(gz, 1)

            def kv_tile(t, page):
                c, j = t // UN, t % UN
                bp, g = j // KVH, j % KVH
                return WN[:, bp, page, g, 0] if c == 0 else KN[:, bp, (c - 1) * 4 + page, g]

            @block.tensor
            def _(pe):
                pe.sem_inc(s_task, 4)
                pe.sem_inc(t_ps, 7)
                pe.sem_inc(o_r, 1)
                pe.wait_ge(c_in, 16 * (6 + NG * UN * GRP))

                def turn_keys(G, t):
                    k = t // 2
                    if t == 0:
                        pe.wait_ge(w_in6, G * 96 + 96)
                    if t == UN:
                        pe.wait_ge(k_in, G * 512 + 512)
                    pe.wait_ge(kt_v if t % 2 else kt_a, G * (NT // 2) + k + 1)
                    for page in range(4):
                        last = nc.tensor.transpose(ps[t % 2][:, page * P:(page + 1) * P], kv_tile(t, page), ident)
                    last.then_inc(kt_ps, 1)

                def scores(G, t):
                    c, j = t // UN, t % UN
                    if j == 0:
                        pe.wait_ge(s_free, G * 5 + max(c, 1))
                    pe.wait_ge(kt_v if t % 2 else kt_a, G * (NT // 2) + t // 2 + 2)
                    last = nc.tensor.matmul(ps[2 + c % 2][32 * j:32 * j + 32, :], QS[:, j // KVH, j % KVH], KTS[:, t % 4], start=True, stop=True)
                    last.then_inc(s_task, 1)

                def turn(G, u):
                    pe.wait_ge(pt_v if u % 2 else pt_a, (G * 3 if u % 2 else G * 4) + u // 2 + 1)
                    bank = ps[4 + u % 2]
                    if u == 0:
                        pe.wait_ge(d_r, G * 3 + 2)
                        for k in range(4):
                            last = nc.tensor.matmul(bank[:, k * P:(k + 1) * P], SW[:, k * P:(k + 1) * P], DG[:, 1], start=True, stop=True)
                    elif u == 1:
                        nc.tensor.matmul(bank[0:NB, 0:P], PC[:, :], DG[:, 0], start=True, stop=True)
                        last = nc.tensor.matmul(bank[0:T, P:2 * P], SW[:, WIN:WIN + T], DG[:, 1], start=True, stop=True)
                    elif u < 6:
                        if u == 2:
                            pe.wait_ge(d_r, G * 3 + 3)
                        for k in range(4):
                            a = ((u - 2) * 4 + k) * P
                            last = nc.tensor.matmul(bank[:, k * P:(k + 1) * P], SC[:, a:a + P], DG[:, 2], start=True, stop=True)
                    else:
                        last = nc.tensor.matmul(bank[0:T, 0:P], SC[:, PAST:PAST + T], DG[:, 2], start=True, stop=True)
                    last.then_inc(t_ps, 1)

                with pe.Fori(0, NG) as G:
                    pe.wait_ge(prep, G + 1)
                    for j in range(UN):
                        last = nc.tensor.matmul(ps[6][32 * j:32 * j + 32, 0:NB + 2 * T], QS[:, j // KVH, j % KVH], MK[:, j // KVH, j % KVH],
                                                start=True, stop=True)
                    last.then_inc(misc, 1)
                    turn_keys(G, 0)
                    for t in range(NT):
                        if t + 1 < NT:
                            turn_keys(G, t + 1)
                        scores(G, t)
                        if t == 2 * UN - 1:
                            pe.wait_ge(pc_r, G + 1)
                            nc.tensor.matmul(ps[7][:, 0:NB], cp("same_q"), PC[:, :], start=True, stop=True).then_inc(imp, 1)
                    for u in range(7):
                        turn(G, u)
                    pe.wait_ge(pt_a, G * 4 + 5)
                    pe.wait_ge(pt_v, G * 3 + 4)
                    pe.wait_ge(v_in, G * 512 + 512)
                    for j in range(UN):
                        bp, g = j // KVH, j % KVH
                        o = ps[7][:, j * RW:(j + 1) * RW]
                        rows = slice(32 * j, 32 * j + RW)

                        def rhs(u, k, n=P):
                            return PTS[0:n, u, k * P + 32 * j:k * P + 32 * j + RW]

                        nc.tensor.matmul(o, CVS[:, bp, g], rhs(1, 0, NB), start=True, stop=False)
                        nc.tensor.matmul(o, VNEW[:, 1, bp, g], rhs(1, 1, T), start=False, stop=False)
                        nc.tensor.matmul(o, VNEW[:, 0, bp, g], rhs(6, 0, T), start=False, stop=False)
                        for k in range(4):
                            nc.tensor.matmul(o, WN[:, bp, k, g, 1], rhs(0, k), start=False, stop=False)
                        for k in range(NPG):
                            last = nc.tensor.matmul(o, VN[:, bp, k, g], rhs(2 + k // 4, k % 4), start=False, stop=k == NPG - 1)
                    last.then_inc(o_r, 1)

            def keys_evac(eng, copy, G, t, s):
                eng.wait_ge(kt_ps, G * NT + t + 1)
                eng.wait_ge(s_task, G * NT + t + 1)
                copy(KTS[:, t % 4], ps[t % 2][:, :]).then_inc(s, 1)

            def turn_evac(eng, copy, G, u, s):
                eng.wait_ge(t_ps, G * 7 + u + 8)
                eng.wait_ge(o_r, G + 1)
                bank = ps[4 + u % 2]
                if u == 1:
                    copy(PTS[0:NB, 1, 0:P], bank[0:NB, 0:P])
                    copy(PTS[0:T, 1, P:2 * P], bank[0:T, P:2 * P]).then_inc(s, 1)
                elif u == 6:
                    copy(PTS[0:T, 6, 0:P], bank[0:T, 0:P]).then_inc(s, 1)
                else:
                    copy(PTS[:, u], bank[:, :]).then_inc(s, 1)

            @block.scalar
            def _(act):
                act.sem_inc(kt_a, 1)
                act.sem_inc(pt_a, 1)

                def expo(G, i, tile):
                    act.wait_ge(m_r, G * 3 + i + 1)
                    nc.scalar.activation(tile, tile, ACT.Exp, bias=ST6[:, i:i + 1], accum_out=ST6[:, 3 + i:4 + i]).then_inc(e_r, 1)

                with act.Fori(0, NG) as G:
                    for t in range(0, NT, 2):
                        keys_evac(act, nc.scalar.copy, G, t, kt_a)
                        if t == 0:
                            expo(G, 0, PC[:, :])
                        if t == 6:
                            expo(G, 1, SW[:, :])
                    expo(G, 2, SC[:, :])
                    for u in range(0, 7, 2):
                        turn_evac(act, nc.scalar.copy, G, u, pt_a)

            @block.vector
            def _(dve):
                dve.sem_inc(kt_v, 1)
                dve.sem_inc(pt_v, 1)
                dve.sem_inc(s_free, 1)
                dve.sem_inc(oe, 1)
                dve.wait_ge(c_in, 16 * (6 + NG * UN * GRP))
                dve.wait_ge(gz, 2)
                LINKS = 13

                def chunk(G, c):
                    dve.wait_ge(s_task, G * NT + UN * (c + 1) + 4)
                    dst = SW[:, 0:WIN] if c == 0 else SC[:, (c - 1) * 512:c * 512]
                    bias = cp("ali_w", 0, WIN) if c == 0 else cp("ali_s", (c - 1) * 512, c * 512)
                    nc.vector.scalar_tensor_tensor(dst, ps[2 + c % 2][:, :], SCALE, bias, ALU.mult, ALU.add).then_inc(s_free, 1)

                with dve.Fori(0, NG) as G:
                    ch = Count(dve, ch6, G * LINKS)
                    dve.wait_ge(o_r, G + 1)
                    for bp in range(2):
                        b1, b4 = bass.ds(G * 2 + bp, 1), bass.ds(G * 8 + bp * T, T)
                        nc.vector.tensor_copy(QS[:, bp, :, 0:RW], QA[:, :, b4].rearrange("p (g r) t -> p g r t", g=KVH))
                        nc.vector.tensor_copy(MK[:, bp, :, 0:NB], CK[:, b1].rearrange("p o n g -> p g (o n)"))
                        for i in range(2):
                            nc.vector.tensor_copy(MK[:, bp, :, NB + i * T:NB + (i + 1) * T], KA[:, i, :, b4])
                    nc.vector.tensor_copy(CVS[:].rearrange("p b g d -> p (b g d)"), CV[:, bass.ds(G * 2, 2)].rearrange("p b g d -> p (b g d)")).then_inc(prep, 1)
                    dve.wait_ge(misc, G + 1)
                    m = ps[6]
                    ch.link(nc.vector.scalar_tensor_tensor(PC[:, :], m[:, 0:NB], SCALE, cp("ali_c"), ALU.mult, ALU.add))
                    nc.vector.tensor_reduce(ST6[:, 0:1], PC[:, :], AX, ALU.max, negate=True).then_inc(m_r, 1)
                    nc.vector.scalar_tensor_tensor(SC[:, PAST:], m[:, NB:NB + T], SCALE, cp("ali_s", PAST, PAST + T), ALU.mult, ALU.add)
                    ch.link(nc.vector.scalar_tensor_tensor(SW[:, WIN:], m[:, NB + T:NB + 2 * T], SCALE, cp("ali_w", WIN, WIN + T), ALU.mult, ALU.add))
                    keys_evac(dve, nc.vector.tensor_copy, G, 1, kt_v)
                    dve.wait_ge(e_r, G * 3 + 1)
                    ch.link(nc.vector.reciprocal(ST6[:, 6:7], ST6[:, 3:4]))
                    nc.vector.tensor_scalar(PC[:, :], PC[:, :], ST6[:, 6:7], None, ALU.mult).then_inc(pc_r, 1)
                    nc.vector.tensor_scalar(DG[:, 0], ident, GR[:, bass.ds(G * 3, 1)], None, ALU.mult).then_inc(d_r, 1)
                    for t in range(3, NT, 2):
                        keys_evac(dve, nc.vector.tensor_copy, G, t, kt_v)
                        if t % UN == UN - 1:
                            chunk(G, t // UN)
                        if t == 3:
                            dve.wait_ge(s_free, G * 5 + 2)
                            nc.vector.tensor_reduce(ST6[:, 1:2], SW[:, :], AX, ALU.max, negate=True).then_inc(m_r, 1)
                        if t == 9:
                            dve.wait_ge(e_r, G * 3 + 2)
                            ch.link(nc.vector.reciprocal(ST6[:, 7:8], ST6[:, 4:5]))
                            nc.vector.tensor_scalar(DG[:, 1], ident, ST6[:, 7:8], GR[:, bass.ds(G * 3 + 2, 1)], ALU.mult, ALU.mult).then_inc(d_r, 1)
                            dve.wait_ge(imp, G + 1)
                            nc.vector.tensor_copy(SCR[:, NB:NBT], cp("forced", NB, NBT))
                            ch.link(nc.vector.tensor_tensor(SCR[:, 0:NB], ps[7][:, 0:NB], cp("unforced", 0, NB), ALU.mult))
                            ch.link(nc.vector.tensor_tensor(SCR[:, 0:NB], SCR[:, 0:NB], cp("forced", 0, NB), ALU.add))
                            nc.vector.memset(PAD[:, :], 0.0)
                            ch.link(nc.vector.max(M8[:, 0:8], SCR[:, :]))
                            nc.vector.memset(PAD[:, :], 0.0)
                            ch.link(nc.vector.match_replace(SCR2[:, :], M8[:, 0:8], SCR[:, :], -1.0))
                            nc.vector.memset(PAD[:, :], 0.0)
                            ch.link(nc.vector.max(M8[:, 8:16], SCR2[:, :]))
                            nc.vector.memset(PAD[:, :], 0.0)
                            ch.link(nc.vector.match_replace(SCR[:, :], M8[:, 8:16], SCR2[:, :], -1.0))
                            ch.link(nc.vector.tensor_scalar(SB8[:, :], SCR[:, :], 0.0, -1e30, ALU.is_ge, ALU.mult))
                    dve.wait_ge(s_free, G * 5 + 6)
                    view = SC[:, 0:PAST].rearrange("p (n k) -> p n k", k=BLK)
                    sel = SB8[:, 0:NB].rearrange("p (n o) -> p n o", o=1).broadcast_to((P, NB, BLK))
                    ch.link(nc.vector.tensor_tensor(view, view, sel, ALU.add))
                    nc.vector.tensor_reduce(ST6[:, 2:3], SC[:, :], AX, ALU.max, negate=True).then_inc(m_r, 1)
                    dve.wait_ge(e_r, G * 3 + 3)
                    ch.link(nc.vector.reciprocal(ST6[:, 8:9], ST6[:, 5:6]))
                    nc.vector.tensor_scalar(DG[:, 2], ident, ST6[:, 8:9], GR[:, bass.ds(G * 3 + 1, 1)], ALU.mult, ALU.mult).then_inc(d_r, 1)
                    for u in range(1, 7, 2):
                        turn_evac(dve, nc.vector.tensor_copy, G, u, pt_v)
                    dve.wait_ge(o_r, G + 2)
                    for bp in range(2):
                        last = nc.vector.tensor_copy(MIX[:, 0:H, bass.ds(G * 8 + (SEQ + bp * T), T)],
                                                     ps[7][:, bp * 2 * RW:(bp + 1) * 2 * RW].rearrange("p (h t) -> p h t", t=T))
                    last.then_inc(oe, 1)
                    assert ch.n == LINKS

        clear_semaphores()

        CW = 3 * GH * HD
        NL = 7
        QC = QT
        with ExitStack() as ph:
            lo, hi = AT["upto"][0], AT["s_batch"][1]
            CP = sb(ph, "consts_g", [P, hi - lo])

            def cp(name, rows=P):
                return CP[0:rows, AT[name][0] - lo:AT[name][1] - lo]

            upto, s_upto = cp("upto"), cp("s_upto", NS)
            level = cp("level").rearrange("p (l c) -> p l c", l=NL)
            ones = cst("ones")
            RAW = sb(ph, "conv_rows", [3 * B + 4, CW])
            CB = sb(ph, "conv_cols", [P, 3, GH, 3 * B + 4])
            E = sb(ph, "ext", [P, 3, SEQ + 3])
            ES = sb(ph, "ext_s", [P, 3, B, T + 3])
            CT = sb(ph, "conv_out", [P, 3, TOK])
            TAIL = sb(ph, "conv_tail", [P, 3, 3 + 3 * B])
            TO = sb(ph, "conv_tail_rows", [3 + 3 * B, 3, HD])
            ZT = sb(ph, "z_t", [P, TOK])
            NAT = sb(ph, "qkv_rows", [P, QT + 1, 3, HD])
            SQ = sb(ph, "squares", [P, QT, 2, HD])
            RN = sb(ph, "inv_norm", [P, QT + 1, 2])
            KN, KB, KG, KD, QN, QG, VB = (sb(ph, n, [P, QT + 1, HD]) for n in ("kn", "kb", "kbg", "kd", "qn", "qg", "vb"))
            TR = sb(ph, "turned", [P, QT + 1, 4, HD])
            GC = sb(ph, "g_cum", [P, QT + 1, GH])
            GTOT = sb(ph, "g_tot", [P, QT + 1, GH])
            EG = sb(ph, "exp_g", [P, QT + 1, GH])
            ED = sb(ph, "exp_rest", [P, QT + 1, GH])
            GM = sb(ph, "g_masked", [NS, B, GH])
            GLS = sb(ph, "gl_s", [P, B, GH])
            GLP = sb(ph, "gl_p", [P, QT, GH])
            NG_ = sb(ph, "norm_g", [P, 1])
            UG = sb(ph, "upto_g", [P, QT, P])
            UGS = sb(ph, "upto_g_s", [NS, NS])
            DT = sb(ph, "decay", [P, QT, P])
            DTS = sb(ph, "decay_s", [NS, NS])
            AQ = sb(ph, "aq", [P, QT, 2, P])
            AQS = sb(ph, "aq_s", [NS, 2, NS])
            M = sb(ph, "a_levels", [P, NL, QT, P])
            MS = sb(ph, "a_levels_s", [NS, 2, NS])
            TI = sb(ph, "t_inv", [P, QT, P])
            TT = sb(ph, "inv_t", [P, QT, P])
            Y = sb(ph, "y", [P, QT, P])
            TIS, TTS, YS = (sb(ph, n, [NS, NS]) for n in ("inv_s", "inv_t_s", "y_s"))
            WT = sb(ph, "w_neg", [P, QT, P])
            WQ = sb(ph, "wq_s", [P, B, 2, T])
            WS = sb(ph, "ws_s", [P, 2, NS])
            VNW = sb(ph, "v_new7", [P, QT, HD])
            VNS = sb(ph, "v_new7_s", [NS, HD])
            VM = sb(ph, "v_masked", [NS, B, HD])
            S = sb(ph, "state", [P, HD])
            SS = sb(ph, "states_s", [P, B, HD])
            SN = sb(ph, "states_new", [P, B, HD])
            ON = sb(ph, "o_rows", [P, QT + 1, HD])
            RO = sb(ph, "inv_rms", [P, QT + 1])
            PAD7 = sb(ph, "pad7", [P, 1])
            ps = banks(ph, "g")
            made = {}

            def s7(name):
                if name not in made:
                    made[name] = sem("g_" + name)
                return made[name]

            block = ph.enter_context(nc.Block())
            QKV = S_proj[R_QKV:R_QKV + CW].rearrange("(i h p) n -> p i h n", i=3, p=P)
            ZALL = S_proj[R_Z:R_Z + GH * HD].rearrange("(h p) n -> p h n", p=P)
            TILES = [(t, P) for t in range(QT)] + [(QC, NS)]

            def col(tile, rows, h, off=0, tiles=slice(0, QT)):
                c = tile[0:rows, tiles, bass.ds(h + off, 1)]
                return c.broadcast_to((rows, c.shape[1], HD))

            @block.sync
            def _(sp):
                sp.dma_start(CP[:, :], C_dram[:, lo:hi]).then_inc(s7("c_in"), 16)
                sp.dma_start(RAW[0:3 * B], A["state_gdn_conv"][0].rearrange("b r c -> (b r) c")).then_inc(s7("c_in"), 16)
                sp.dma_start(RAW[3 * B:3 * B + 4], A["gdn_conv_w"][0]).then_inc(s7("c_in"), 16)
                sp.dma_start(NG_[:, :], A["gdn_norm_g"].rearrange("o (p q) -> p (o q)", q=1)).then_inc(s7("c_in"), 16)

                with sp.Fori(0, GH) as h:
                    sp.wait_ge(s7("fin"), h + 1)
                    h1 = bass.ds(h, 1)
                    sp.dma_start(ZT[:, :], ZALL[:, h1].rearrange("p o n -> p (o n)")).then_inc(s7("z_in"), 16)
                    sp.dma_start(SS[:], A["state_gdn"][0, :, h1].rearrange("b o k v -> k (b o) v")).then_inc(s7("z_in"), 16)
                    sp.wait_ge(s7("tail"), h + 1)
                    cols = bass.ds(h * HD, HD)
                    sp.dma_start(O[6][0, 0].rearrange("r (i c) -> r i c", i=3)[:, :, cols], TO[0:3]).then_inc(s7("out"), 16)
                    sp.dma_start(O[12][0].rearrange("b r (i c) -> (b r) i c", i=3)[:, :, cols], TO[3:3 + 3 * B]).then_inc(s7("out"), 16)
                    sp.wait_ge(s7("s_fin"), h + 1)
                    sp.dma_start(O[5][0, 0, h1].rearrange("o k v -> k (o v)"), S[:, :]).then_inc(s7("out"), 16)
                    sp.dma_start(O[11][0, :, h1].rearrange("b o k v -> k (b o) v"), SN[:]).then_inc(s7("out"), 16)
                    sp.wait_ge(s7("out"), h * 64 + 64)
                    sp.sem_inc(s7("stored"), 1)
                sp.wait_ge(s7("fin"), GH + 1)

            @block.gpsimd
            def _(gp):
                nc.gpsimd.memset(E[:, :, 0:3], 0.0).then_inc(s7("zero"), 1)
                gp.wait_ge(s7("c_in"), 64)
                def load(h):
                    for i in range(3):
                        q = QKV[:, i, bass.ds(h, 1)]
                        gp.dma_start(E[:, i, 3:], q[:, :, 0:SEQ].rearrange("p o n -> p (o n)")).then_inc(s7("e_in"), 16)
                        gp.dma_start(ES[:, i, :, 3:], q[:, :, SEQ:].rearrange("p o (b t) -> p (o b) t", t=T)).then_inc(s7("e_in"), 16)

                def head(h, more):
                    gp.wait_ge(s7("levels"), h + 1)
                    g = GAB[:, 0:QT, bass.ds(h + 24, 1)].broadcast_to((P, QT, P))
                    nc.gpsimd.tensor_tensor(UG[:], upto.rearrange("p (o c) -> p o c", o=1).broadcast_to((P, QT, P)), g, ALU.mult)
                    gs = GAB[0:NS, QC:QC + 1, bass.ds(h + 24, 1)].broadcast_to((NS, 1, NS))
                    nc.gpsimd.tensor_tensor(UGS[:].rearrange("p (o c) -> p o c", o=1), s_upto.rearrange("p (o c) -> p o c", o=1), gs, ALU.mult).then_inc(s7("ug"), 1)
                    if more:
                        gp.wait_ge(s7("conv"), h + 1)
                        load(h + 1)
                    gp.wait_ge(s7("nat"), h + 1)
                    gp.wait_ge(s7("nat_a"), h + 1)
                    for a, b, rows in ((0, QT, P), (QC, QC + 1, NS)):
                        last = nc.gpsimd.tensor_tensor(VB[0:rows, a:b], NAT[0:rows, a:b, 2], col(GAB, rows, h, 32, slice(a, b)), ALU.mult)
                    last.then_inc(s7("vb"), 1)
                    gp.wait_ge(s7("qn"), h + 1)
                    for a, b, rows in ((0, QT, P), (QC, QC + 1, NS)):
                        last = nc.gpsimd.tensor_tensor(QG[0:rows, a:b], QN[0:rows, a:b], col(EG, rows, h, 0, slice(a, b)), ALU.mult)
                    last.then_inc(s7("qg"), 1)
                    for dst, src, c in ((KG, KB, EG), (KD, KN, ED)):
                        for a, b, rows in ((0, QT, P), (QC, QC + 1, NS)):
                            last = nc.gpsimd.tensor_tensor(dst[0:rows, a:b], src[0:rows, a:b], col(c, rows, h, 0, slice(a, b)), ALU.mult)
                    last.then_inc(s7("kd"), 1)
                    gp.wait_ge(s7("aq"), h + 1)
                    nc.gpsimd.tensor_tensor(MS[:, 1], AQS[:, 0], level[0:NS, 1, 0:NS], ALU.mult)
                    for l in range(1, NL):
                        nc.gpsimd.tensor_tensor(M[:, l], AQ[:, :, 0], level[:, l:l + 1].broadcast_to((P, QT, P)), ALU.mult).then_inc(s7("m"), 1)

                load(0)
                with gp.Fori(0, GH - 1) as h:
                    head(h, True)
                head(GH - 1, False)

            @block.tensor
            def _(pe):
                pe.wait_ge(s7("c_in"), 64)
                n = 3 * B + 4
                for k in range(3 * GH):
                    last = nc.tensor.transpose(ps[k // 12][:, (k % 12) * n:(k % 12 + 1) * n], RAW[:, k * P:(k + 1) * P], ident[0:n, 0:n])
                last.then_inc(s7("cb_ps"), 1)
                nc.tensor.matmul(ps[2][:, 0:QT * GH], upto, GAB[:, 0:QT, 24:32], start=True, stop=True)
                nc.tensor.matmul(ps[2][:, 32:32 + QT * GH], ones, GAB[:, 0:QT, 24:32], start=True, stop=True)
                nc.tensor.matmul(ps[3][0:NS, 0:GH], s_upto, GAB[0:NS, QC, 24:32], start=True, stop=True)
                nc.tensor.matmul(ps[3][0:NS, GH:2 * GH], cp("s_same", NS), GAB[0:NS, QC, 24:32], start=True, stop=True).then_inc(s7("gc_ps"), 1)
                pe.wait_ge(s7("gm"), 1)
                nc.tensor.matmul(ps[4][:, 0:B * GH], ones[0:NS, :], GM[:].rearrange("p b h -> p (b h)"), start=True, stop=True).then_inc(s7("gl_ps"), 1)
                pe.wait_ge(s7("pre"), 1)

                with pe.Fori(0, GH) as h:
                    pe.wait_ge(s7("ug"), h + 1)
                    nc.tensor.matmul(ps[6][:, :], ones, UG[:].rearrange("p t c -> p (t c)"), start=True, stop=True)
                    nc.tensor.matmul(ps[7][0:NS, 0:NS], ones[0:NS, 0:NS], UGS[:], start=True, stop=True).then_inc(s7("gb"), 1)
                    pe.wait_ge(s7("silu"), h + 1)
                    for t, n in TILES:
                        for i in range(3):
                            last = nc.tensor.transpose(ps[t][0:n, i * P:(i + 1) * P], CT[:, i, t * P:t * P + n], ident)
                    last.then_inc(s7("nat_ps"), 1)
                    for i in range(3):
                        last = nc.tensor.transpose(ps[5][0:3 + 3 * B, i * P:(i + 1) * P], TAIL[:, i], ident)
                    last.then_inc(s7("tail_ps"), 1)
                    pe.wait_ge(s7("qg"), h + 1)
                    for t, n in TILES:
                        for i, x in enumerate((KN, KB, QN, QG)):
                            last = nc.tensor.transpose(ps[t][:, i * n:(i + 1) * n], x[0:n, t], ident[0:n, 0:n])
                    last.then_inc(s7("tr_ps"), 1)
                    pe.wait_ge(s7("tr"), h + 1)
                    pe.wait_ge(s7("tr_a"), h + 1)
                    pe.wait_ge(s7("tail"), h + 1)
                    for t in range(QT):
                        nc.tensor.matmul(ps[5 + t // 2][:, (t % 2) * 256:(t % 2) * 256 + 256], TR[:, t, 0], TR[:, t, 1:3], start=True, stop=True)
                    nc.tensor.matmul(ps[7][0:NS, 0:2 * NS], TR[:, QC, 0, 0:NS], TR[:, QC, 1:3, 0:NS], start=True, stop=True).then_inc(s7("kk"), 1)
                    pe.wait_ge(s7("tt0"), h + 1)
                    for t in range(QT):
                        nc.tensor.transpose(ps[0][:, t * P:(t + 1) * P], TT[:, t], ident)
                    nc.tensor.transpose(ps[4][0:NS, 0:NS], TTS[:, :], ident[0:NS, 0:NS]).then_inc(s7("ti_ps"), 1)
                    for l in range(1, NL):
                        x = h * (NL - 1) + l
                        pe.wait_ge(s7("inv"), x)
                        pe.wait_ge(s7("m"), x)
                        for t in range(QT):
                            last = nc.tensor.matmul(ps[1][:, t * P:(t + 1) * P], M[:, l, t], TI[:, t], start=True, stop=True)
                        if l == 1:
                            last = nc.tensor.matmul(ps[4][0:NS, NS:2 * NS], MS[:, 1], TIS[:, :], start=True, stop=True)
                        last.then_inc(s7("y_ps"), 1)
                        pe.wait_ge(s7("y"), x)
                        if l < NL - 1:
                            for t in range(QT):
                                nc.tensor.matmul(ps[2][:, t * P:(t + 1) * P], TT[:, t], Y[:, t], start=True, stop=True)
                        for t in range(QT):
                            last = nc.tensor.matmul(ps[3][:, t * P:(t + 1) * P], Y[:, t], TT[:, t], start=True, stop=True)
                        if l == 1:
                            last = nc.tensor.matmul(ps[4][0:NS, 2 * NS:3 * NS], YS[:, :], TTS[:, :], start=True, stop=True)
                        last.then_inc(s7("d_ps"), 1)
                    pe.wait_ge(s7("kd"), h + 1)
                    pe.wait_ge(s7("inv_end"), h + 1)
                    for t in range(QT):
                        nc.tensor.matmul(ps[5][:, t * P:(t + 1) * P], KG[:, t], TT[:, t], start=True, stop=True)
                    nc.tensor.matmul(ps[7][:, 0:NS], KG[0:NS, QC], TTS[:, :], start=True, stop=True).then_inc(s7("w_ps"), 1)
                    pe.wait_ge(s7("vb"), h + 1)
                    pe.wait_ge(s7("w"), h + 1)
                    pe.wait_ge(s7("z_in"), h * 32 + 32)
                    for b in range(B):
                        last = nc.tensor.matmul(ps[4][:, b * 8:b * 8 + 8], SS[:, b], WQ[:, b].rearrange("p i t -> p (i t)"), start=True, stop=True)
                    last.then_inc(s7("ws_ps"), 1)
                    for t in range(QT):
                        x = h * QT + t
                        if t:
                            pe.wait_ge(s7("state"), x)
                        else:
                            pe.wait_ge(s7("szero"), h + 1)
                        v = ps[0][:, t * P:(t + 1) * P]
                        nc.tensor.matmul(v, TT[:, t], VB[:, t], start=True, stop=False)
                        nc.tensor.matmul(v, WT[:, t], S[:, :], start=False, stop=True).then_inc(s7("v_ps"), 1)
                        o = ps[1][:, t * P:(t + 1) * P]
                        nc.tensor.matmul(o, TR[:, t, 3], S[:, :], start=True, stop=False)
                        pe.wait_ge(s7("vn"), x + 1)
                        nc.tensor.matmul(ps[2][:, 0:P], KD[:, t], VNW[:, t], start=True, stop=True).then_inc(s7("s_ps"), 1)
                        last = nc.tensor.matmul(o, AQ[:, t, 1], VNW[:, t], start=False, stop=True)
                        if t == 0:
                            pe.wait_ge(s7("ws"), h + 1)
                            v = ps[7][0:NS, P:2 * P]
                            nc.tensor.matmul(v, WS[:, 0], ident, start=True, stop=False)
                            nc.tensor.matmul(v, TTS[:, :], VB[0:NS, QC], start=False, stop=True).then_inc(s7("vs_ps"), 1)
                        if t == 1:
                            pe.wait_ge(s7("vns"), h + 1)
                            v = ps[6][0:NS, 0:P]
                            nc.tensor.matmul(v, WS[:, 1], ident, start=True, stop=False)
                            nc.tensor.matmul(v, AQS[:, 1], VNS[:, :], start=False, stop=True).then_inc(s7("os_ps"), 1)
                        if t == 2:
                            pe.wait_ge(s7("vm"), h + 1)
                            for k in range(2):
                                last2 = nc.tensor.matmul(ps[3 + 2 * k][:, :], KD[0:NS, QC], VM[:, 4 * k:4 * k + 4].rearrange("p b v -> p (b v)"), start=True, stop=True)
                            last2.then_inc(s7("ss_ps"), 1)
                    last.then_inc(s7("o_ps"), 1)
                    pe.wait_ge(s7("on"), h + 1)
                    for t in range(QT):
                        nc.tensor.transpose(ps[0][:, t * P:(t + 1) * P], ON[:, t], ident)
                    nc.tensor.transpose(ps[4][:, 0:NS], ON[0:NS, QC], ident[0:NS, 0:NS]).then_inc(s7("ot_ps"), 1)

            @block.scalar
            def _(act):
                act.wait_ge(s7("gcs"), 1)
                nc.scalar.activation(EG[:, 0:QT], GC[:, 0:QT], ACT.Exp)
                nc.scalar.activation(EG[0:NS, QC], GC[0:NS, QC], ACT.Exp)
                nc.scalar.activation(GLP[:].rearrange("p t h -> p (t h)"), ps[2][:, 32:32 + QT * GH], ACT.Exp)
                nc.scalar.activation(ED[:, 0:QT], GTOT[:, 0:QT], ACT.Exp)
                nc.scalar.activation(ED[0:NS, QC], GTOT[0:NS, QC], ACT.Exp)
                act.wait_ge(s7("gl_ps"), 1)
                nc.scalar.activation(GLS[:].rearrange("p b h -> p (b h)"), ps[4][:, 0:B * GH], ACT.Exp).then_inc(s7("pre"), 1)
                with act.Fori(0, GH) as h:
                    act.wait_ge(s7("conv"), h + 1)
                    nc.scalar.activation(CT[:], CT[:], ACT.Silu).then_inc(s7("silu"), 1)
                    act.wait_ge(s7("nat_ps"), h + 1)
                    for t in (0, 1):
                        last = nc.scalar.copy(NAT[:, t].rearrange("p i d -> p (i d)"), ps[t][:, 0:3 * HD])
                    last.then_inc(s7("nat_a"), 1)
                    act.wait_ge(s7("rn_v"), h * 2 + 2)
                    nc.scalar.activation(RN[:, 0:QT], RN[:, 0:QT], ACT.Sqrt)
                    nc.scalar.activation(RN[0:NS, QC], RN[0:NS, QC], ACT.Sqrt).then_inc(s7("rn"), 1)
                    act.wait_ge(s7("tail_ps"), h + 1)
                    act.wait_ge(s7("stored"), h + 1)
                    nc.scalar.copy(TO[:].rearrange("p i d -> p (i d)"), ps[5][0:3 + 3 * B, 0:3 * HD]).then_inc(s7("tail"), 1)
                    act.wait_ge(s7("tr_ps"), h + 1)
                    for t in (0, 1):
                        last = nc.scalar.copy(TR[:, t].rearrange("p i d -> p (i d)"), ps[t][:, :])
                    last.then_inc(s7("tr_a"), 1)
                    act.wait_ge(s7("dec"), h + 1)
                    nc.scalar.activation(DT[:], DT[:], ACT.Exp)
                    nc.scalar.activation(DTS[:], DTS[:], ACT.Exp).then_inc(s7("dexp"), 1)
                    for l in range(1, NL):
                        x = h * (NL - 1) + l
                        act.wait_ge(s7("y_ps"), x)
                        last = nc.scalar.copy(Y[:].rearrange("p t c -> p (t c)"), ps[1][:, :])
                        if l == 1:
                            last = nc.scalar.copy(YS[:, :], ps[4][0:NS, NS:2 * NS])
                        last.then_inc(s7("y"), 1)
                    act.wait_ge(s7("w_ps"), h + 1)
                    nc.scalar.mul(WT[:].rearrange("p t c -> p (t c)"), ps[5][:, :], -1.0)
                    nc.scalar.mul(WQ[:, :, 0], ps[7][:, 0:NS].rearrange("p (b t) -> p b t", t=T), -1.0)
                    nc.scalar.copy(WQ[:, :, 1], TR[:, QC, 3, 0:NS].rearrange("p (b t) -> p b t", t=T)).then_inc(s7("w"), 1)
                    act.wait_ge(s7("ws_ps"), h + 1)
                    nc.scalar.copy(WS[:].rearrange("p i (b t) -> p i b t", t=T), ps[4][:, 0:64].rearrange("p (b i t) -> p i b t", i=2, t=T)).then_inc(s7("ws"), 1)
                    act.wait_ge(s7("z_in"), h * 32 + 32)
                    nc.scalar.activation(ZT[:, :], ZT[:, :], ACT.Silu).then_inc(s7("z"), 1)
                    act.wait_ge(s7("os_ps"), h + 1)
                    nc.scalar.activation(ON[0:NS, QC], ps[6][0:NS, 0:P], ACT.Square, accum_out=RO[0:NS, QC:QC + 1])
                    act.wait_ge(s7("o_ps"), h + 1)
                    for t in range(QT):
                        last = nc.scalar.activation(ON[:, t], ps[1][:, t * P:(t + 1) * P], ACT.Square, accum_out=RO[:, t:t + 1])
                    last.then_inc(s7("osq"), 1)
                    act.wait_ge(s7("ro_v"), h + 1)
                    nc.scalar.activation(RO[:, 0:QT], RO[:, 0:QT], ACT.Sqrt)
                    nc.scalar.activation(RO[0:NS, QC:QC + 1], RO[0:NS, QC:QC + 1], ACT.Sqrt).then_inc(s7("ro"), 1)

            @block.vector
            def _(dve):
                dve.sem_inc(s7("fin"), 1)
                dve.sem_inc(s7("stored"), 1)
                dve.sem_inc(s7("levels"), 1)
                dve.wait_ge(s7("cb_ps"), 1)
                n = 3 * B + 4
                for k in range(2):
                    nc.vector.tensor_copy(CB[:].rearrange("p i h n -> p (i h n)")[:, k * 12 * n:(k + 1) * 12 * n], ps[k][:, 0:12 * n])
                dve.wait_ge(s7("gc_ps"), 1)
                pre = Count(dve, s7("pre_v"))
                nc.vector.tensor_copy(GC[:, 0:QT].rearrange("p t h -> p (t h)"), ps[2][:, 0:QT * GH])
                pre.link(nc.vector.tensor_copy(GC[0:NS, QC], ps[3][0:NS, 0:GH]))
                nc.vector.tensor_tensor(GTOT[:, 0:QT].rearrange("p t h -> p (t h)"), ps[2][:, 32:32 + QT * GH], GC[:, 0:QT].rearrange("p t h -> p (t h)"), ALU.subtract)
                nc.vector.tensor_tensor(GTOT[0:NS, QC], ps[3][0:NS, GH:2 * GH], GC[0:NS, QC], ALU.subtract).then_inc(s7("gcs"), 1)
                nc.vector.tensor_tensor(GM[:], cp("s_batch", NS).rearrange("p (b o) -> p b o", o=1).broadcast_to((NS, B, GH)),
                                        GAB[0:NS, QC:QC + 1, 24:32].broadcast_to((NS, B, GH)), ALU.mult).then_inc(s7("gm"), 1)
                dve.wait_ge(s7("zero"), 1)
                dve.wait_ge(s7("pre"), 1)
                LINKS = 15
                with dve.Fori(0, GH) as h:
                    ch = Count(dve, s7("ch"), h * LINKS)
                    h1 = bass.ds(h, 1)
                    dve.wait_ge(s7("e_in"), h * 96 + 96)
                    ch.link(nc.vector.tensor_copy(ES[:, :, :, 0:3], CB[:, :, h1, 0:3 * B].rearrange("p i o (b j) -> p i (o b) j", j=3)))
                    for j in range(4):
                        for i in range(3):
                            w = CB[:, i, h1, 3 * B + j]
                            o, x = CT[:, i, 0:SEQ], E[:, i, j:j + SEQ]
                            os_, xs = CT[:, i, SEQ:].rearrange("p (b t) -> p b t", t=T), ES[:, i, :, j:j + T]
                            if j == 0:
                                nc.vector.tensor_scalar(o, x, w, None, ALU.mult)
                                last = nc.vector.tensor_scalar(os_, xs, w, None, ALU.mult)
                            else:
                                nc.vector.scalar_tensor_tensor(o, x, w, o, ALU.mult, ALU.add)
                                last = nc.vector.scalar_tensor_tensor(os_, xs, w, os_, ALU.mult, ALU.add)
                        if j < 3:
                            ch.link(last)
                    nc.vector.tensor_copy(TAIL[:, :, 0:3], E[:, :, SEQ:SEQ + 3])
                    nc.vector.tensor_copy(TAIL[:, :, 3:].rearrange("p i (b j) -> p i b j", j=3), ES[:, :, :, T:T + 3]).then_inc(s7("conv"), 1)
                    dve.wait_ge(s7("gb"), h + 1)
                    for t in range(QT):
                        nc.vector.tensor_scalar(DT[:, t], ps[6][:, t * P:(t + 1) * P], GC[:, t, h1], 0.0, ALU.subtract, ALU.min)
                    nc.vector.tensor_scalar(DTS[:], ps[7][0:NS, 0:NS], GC[0:NS, QC, h1], 0.0, ALU.subtract, ALU.min).then_inc(s7("dec"), 1)
                    dve.wait_ge(s7("nat_ps"), h + 1)
                    for t, n in TILES[2:]:
                        last = nc.vector.tensor_copy(NAT[0:n, t].rearrange("p i d -> p (i d)"), ps[t][0:n, 0:3 * HD])
                    last.then_inc(s7("nat"), 1)
                    dve.wait_ge(s7("nat"), h + 1)
                    dve.wait_ge(s7("nat_a"), h + 1)
                    for a, b, rows in ((0, QT, P), (QC, QC + 1, NS)):
                        x = NAT[0:rows, a:b, 0:2]
                        q = SQ[0:rows, 0:b - a]
                        ch.link(nc.vector.tensor_tensor(q, x, x, ALU.mult))
                        ch.link(nc.vector.tensor_reduce(RN[0:rows, a:b], q, AX, ALU.add))
                        ch.link(nc.vector.tensor_scalar(RN[0:rows, a:b], RN[0:rows, a:b], 1e-6, None, ALU.add))
                        nc.vector.reciprocal(RN[0:rows, a:b], RN[0:rows, a:b]).then_inc(s7("rn_v"), 1)
                    dve.wait_ge(s7("rn"), h + 1)
                    for a, b, rows in ((0, QT, P), (QC, QC + 1, NS)):
                        def rn(i):
                            return RN[0:rows, a:b, i:i + 1].broadcast_to((rows, b - a, HD))
                        nc.vector.scalar_tensor_tensor(QN[0:rows, a:b], NAT[0:rows, a:b, 0], SCALE, rn(0), ALU.mult, ALU.mult)
                        last = nc.vector.tensor_tensor(KN[0:rows, a:b], NAT[0:rows, a:b, 1], rn(1), ALU.mult)
                    ch.link(last)
                    for a, b, rows in ((0, QT, P), (QC, QC + 1, NS)):
                        last = nc.vector.tensor_tensor(KB[0:rows, a:b], KN[0:rows, a:b], col(GAB, rows, h, 32, slice(a, b)), ALU.mult)
                    last.then_inc(s7("qn"), 1)
                    dve.wait_ge(s7("tr_ps"), h + 1)
                    for t in (2, 3):
                        nc.vector.tensor_copy(TR[:, t].rearrange("p i d -> p (i d)"), ps[t][:, :])
                    nc.vector.tensor_copy(TR[:, QC, :, 0:NS], ps[4][:, 0:4 * NS].rearrange("p (i n) -> p i n", n=NS)).then_inc(s7("tr"), 1)
                    dve.wait_ge(s7("dexp"), h + 1)
                    nc.vector.tensor_tensor(DT[:], DT[:], upto.rearrange("p (o c) -> p o c", o=1).broadcast_to((P, QT, P)), ALU.mult)
                    ch.link(nc.vector.tensor_tensor(DTS[:], DTS[:], s_upto, ALU.mult))
                    dve.wait_ge(s7("kk"), h + 1)
                    for k in range(2):
                        for i in range(2):
                            nc.vector.tensor_tensor(AQ[:, 2 * k:2 * k + 2, i], ps[5 + k][:, :].rearrange("p (t i c) -> p t i c", t=2, i=2)[:, :, i],
                                                    DT[:, 2 * k:2 * k + 2], ALU.mult)
                    for i in range(2):
                        last = nc.vector.tensor_tensor(AQS[:, i], ps[7][0:NS, i * NS:(i + 1) * NS], DTS[:, :], ALU.mult)
                    last.then_inc(s7("aq"), 1)
                    dve.wait_ge(s7("aq"), h + 1)
                    nc.vector.tensor_tensor(TT[:], AQ[:, :, 0], level[:, 0:1].broadcast_to((P, QT, P)), ALU.mult)
                    ch.link(nc.vector.tensor_tensor(TTS[:], AQS[:, 0], level[0:NS, 0, 0:NS], ALU.mult))
                    nc.vector.tensor_tensor(TT[:], ident.rearrange("p (o c) -> p o c", o=1).broadcast_to((P, QT, P)), TT[:], ALU.subtract)
                    nc.vector.tensor_tensor(TTS[:], ident[0:NS, 0:NS], TTS[:], ALU.subtract).then_inc(s7("tt0"), 1)
                    dve.wait_ge(s7("ti_ps"), h + 1)
                    nc.vector.tensor_copy(TIS[:, :], ps[4][0:NS, 0:NS])
                    nc.vector.tensor_copy(TI[:].rearrange("p t c -> p (t c)"), ps[0][:, :]).then_inc(s7("inv"), 1)
                    for l in range(1, NL):
                        x = h * (NL - 1) + l
                        dve.wait_ge(s7("d_ps"), x)
                        ttf, tif = TT[:].rearrange("p t c -> p (t c)"), TI[:].rearrange("p t c -> p (t c)")
                        if l == 1:
                            nc.vector.tensor_tensor(TTS[:], TTS[:], ps[4][0:NS, 2 * NS:3 * NS], ALU.subtract)
                        if l < NL - 1:
                            nc.vector.tensor_tensor(ttf, ttf, ps[3][:, :], ALU.subtract)
                            nc.vector.tensor_tensor(tif, tif, ps[2][:, :], ALU.subtract).then_inc(s7("inv"), 1)
                        else:
                            nc.vector.tensor_tensor(ttf, ttf, ps[3][:, :], ALU.subtract).then_inc(s7("inv_end"), 1)
                    dve.wait_ge(s7("stored"), h + 1)
                    nc.vector.memset(S[:, :], 0.0).then_inc(s7("szero"), 1)
                    for t in range(QT):
                        x = h * QT + t
                        dve.wait_ge(s7("v_ps"), x + 1)
                        nc.vector.tensor_copy(VNW[:, t], ps[0][:, t * P:(t + 1) * P]).then_inc(s7("vn"), 1)
                        dve.wait_ge(s7("s_ps"), x + 1)
                        last = nc.vector.scalar_tensor_tensor(S[:, :], S[:, :], GLP[:, t, h1], ps[2][:, 0:P], ALU.mult, ALU.add)
                        last.then_inc(s7("state"), 1)
                        if t == 0:
                            dve.wait_ge(s7("vs_ps"), h + 1)
                            nc.vector.tensor_copy(VNS[:, :], ps[7][0:NS, P:2 * P]).then_inc(s7("vns"), 1)
                            dve.wait_ge(s7("vns"), h + 1)
                            nc.vector.tensor_tensor(VM[:], VNS[:].rearrange("p (o v) -> p o v", o=1).broadcast_to((NS, B, HD)),
                                                    cp("s_batch", NS).rearrange("p (b o) -> p b o", o=1).broadcast_to((NS, B, HD)), ALU.mult).then_inc(s7("vm"), 1)
                    ch.link(nc.vector.tensor_tensor(SN[:], SS[:], GLS[:, :, h1].broadcast_to((P, B, HD)), ALU.mult))
                    dve.wait_ge(s7("ss_ps"), h + 1)
                    for k in range(2):
                        half = SN[:, 4 * k:4 * k + 4].rearrange("p b v -> p (b v)")
                        last = nc.vector.tensor_tensor(half, half, ps[3 + 2 * k][:, :], ALU.add)
                    last.then_inc(s7("s_fin"), 1)
                    dve.wait_ge(s7("osq"), h + 1)
                    nc.vector.tensor_scalar(RO[:, 0:QT], RO[:, 0:QT], 1.0 / HD, 1e-6, ALU.mult, ALU.add)
                    ch.link(nc.vector.tensor_scalar(RO[0:NS, QC:QC + 1], RO[0:NS, QC:QC + 1], 1.0 / HD, 1e-6, ALU.mult, ALU.add))
                    nc.vector.reciprocal(RO[:, 0:QT], RO[:, 0:QT])
                    nc.vector.reciprocal(RO[0:NS, QC:QC + 1], RO[0:NS, QC:QC + 1]).then_inc(s7("ro_v"), 1)
                    dve.wait_ge(s7("ro"), h + 1)
                    nc.vector.tensor_tensor(ON[:, 0:QT], ps[1][:, :].rearrange("p (t v) -> p t v", t=QT),
                                            RO[:, 0:QT].rearrange("p (t o) -> p t o", o=1).broadcast_to((P, QT, HD)), ALU.mult)
                    nc.vector.tensor_scalar(ON[0:NS, QC], ps[6][0:NS, 0:P], RO[0:NS, QC:QC + 1], None, ALU.mult).then_inc(s7("on"), 1)
                    dve.wait_ge(s7("ot_ps"), h + 1)
                    dve.wait_ge(s7("z"), h + 1)
                    out = MIX[:, bass.ds(h + H, 1)]
                    nc.vector.scalar_tensor_tensor(out[:, :, 0:SEQ].rearrange("p o n -> p (o n)"), ps[0][:, :], NG_[:, 0:1], ZT[:, 0:SEQ], ALU.mult, ALU.mult)
                    nc.vector.scalar_tensor_tensor(out[:, :, SEQ:].rearrange("p o n -> p (o n)"), ps[4][:, 0:NS], NG_[:, 0:1], ZT[:, SEQ:], ALU.mult, ALU.mult).then_inc(s7("fin"), 1)
                    nc.vector.memset(PAD7[:, :], 0.0).then_inc(s7("levels"), 1)
                    assert ch.n == LINKS, ch.n

        def layer_norm(tag, X, OUT, g_name, b_name):
            with ExitStack() as ph:
                NQ = 4
                SQ = sb(ph, tag + "_sq", [P, NQ, TOK])
                MU = sb(ph, tag + "_mu", [P, TOK])
                RS = sb(ph, tag + "_rs", [P, TOK])
                GB = sb(ph, tag + "_gb", [P, 2, KT])
                ps = banks(ph, tag)
                gb_in, su, ce, sq, vs, va, rs, sc, fin, ch = (sem(f"{tag}_{n}") for n in (
                    "gb_in", "sum", "centred", "squared", "sq_sum", "var", "rstd", "scaled", "fin", "ch"))
                block = ph.enter_context(nc.Block())

                @block.sync
                def _(sp):
                    with nc.allow_non_contiguous_dma("small columns"):
                        for i, name in enumerate((g_name, b_name)):
                            sp.dma_start(GB[:, i, :], A[name][0].rearrange("(k p) -> p k", p=P)).then_inc(gb_in, 16)
                    sp.wait_ge(fin, KT)

                @block.tensor
                def _(pe):
                    for k in range(KT):
                        nc.tensor.matmul(ps[0][:, :], cst("ones"), X[:, k, 0:SEQ], start=k == 0, stop=k == KT - 1)
                        last = nc.tensor.matmul(ps[1][:, 0:NS], cst("ones"), X[:, k, SEQ:], start=k == 0, stop=k == KT - 1)
                    last.then_inc(su, 1)
                    for k in range(KT):
                        pe.wait_ge(sq, k + 1)
                        nc.tensor.matmul(ps[2][:, :], cst("ones"), SQ[:, k % NQ, 0:SEQ], start=k == 0, stop=k == KT - 1)
                        nc.tensor.matmul(ps[3][:, 0:NS], cst("ones"), SQ[:, k % NQ, SEQ:], start=k == 0, stop=k == KT - 1).then_inc(vs, 1)

                @block.vector
                def _(dve):
                    c = Count(dve, ch)
                    dve.wait_ge(su, 1)
                    nc.vector.tensor_scalar(MU[:, 0:SEQ], ps[0][:, :], 1.0 / DM, None, ALU.mult)
                    c.link(nc.vector.tensor_scalar(MU[:, SEQ:], ps[1][:, 0:NS], 1.0 / DM, None, ALU.mult))
                    for k in range(KT):
                        nc.vector.tensor_tensor(X[:, k], X[:, k], MU[:], ALU.subtract).then_inc(ce, 1)
                    dve.wait_ge(vs, KT)
                    nc.vector.tensor_scalar(RS[:, 0:SEQ], ps[2][:, :], 1.0 / DM, 1e-5, ALU.mult, ALU.add)
                    c.link(nc.vector.tensor_scalar(RS[:, SEQ:], ps[3][:, 0:NS], 1.0 / DM, 1e-5, ALU.mult, ALU.add))
                    nc.vector.reciprocal(RS[:], RS[:]).then_inc(va, 1)
                    dve.wait_ge(rs, 1)
                    for k in range(KT):
                        nc.vector.tensor_tensor(X[:, k], X[:, k], RS[:], ALU.mult).then_inc(sc, 1)

                @block.scalar
                def _(act):
                    for k in range(KT):
                        act.wait_ge(ce, k + 1)
                        if k >= NQ:
                            act.wait_ge(vs, k - NQ + 1)
                        nc.scalar.activation(SQ[:, k % NQ], X[:, k], ACT.Square).then_inc(sq, 1)
                    act.wait_ge(va, 1)
                    nc.scalar.activation(RS[:], RS[:], ACT.Sqrt).then_inc(rs, 1)
                    act.wait_ge(gb_in, 32)
                    for k in range(KT):
                        act.wait_ge(sc, k + 1)
                        nc.scalar.activation(OUT[:, k], X[:, k], ACT.Identity, scale=GB[:, 0, k:k + 1], bias=GB[:, 1, k:k + 1]).then_inc(fin, 1)

        res = ExitStack()
        top.enter_context(res)
        XR = sb(res, "x_res", [P, KT, TOK])
        with ExitStack() as ph:
            W = sb(ph, "wo_ring", [P, 4, KT, P])
            ps = banks(ph, "h")
            w_in = [sem(f"wo_in{i}") for i in range(4)]
            x_in, acc, ev = sem("xr_in"), sem("o_acc"), sem("o_ev")
            W_o = A["w_o"][0].rearrange("(k p) n -> p k n", p=P)
            block = ph.enter_context(nc.Block())
            NGO = DM // 512

            @block.sync
            def _(sp):
                for n in range(4):
                    sp.dma_start(W[:, n], W_o[:, :, n * P:(n + 1) * P]).then_inc(w_in[n], 16)
                sp.dma_start(XR[:], S_xt.rearrange("k p n -> p k n")).then_inc(x_in, 16)
                with sp.Fori(1, NGO) as g:
                    for n in range(4):
                        sp.wait_ge(acc, g * 4 + n - 3)
                        sp.dma_start(W[:, n], W_o[:, :, bass.ds(g * 512 + n * P, P)]).then_inc(w_in[n], 16)
                sp.wait_ge(ev, NGO * 4 + 2)

            @block.tensor
            def _(pe):
                with pe.Fori(0, NGO) as g:
                    for n in range(4):
                        pe.wait_ge(w_in[n], g * 16 + 16)
                        pe.wait_ge(ev, g * 4 + n + 1)
                        a, b = ps[2 * (n % 2)], ps[2 * (n % 2) + 1]
                        for k in range(KT):
                            nc.tensor.matmul(a[:, :], W[:, n, k], MIX[:, k, 0:SEQ], start=k == 0, stop=k == KT - 1)
                            last = nc.tensor.matmul(b[:, 0:NS], W[:, n, k], MIX[:, k, SEQ:TOK], start=k == 0, stop=k == KT - 1)
                        last.then_inc(acc, 1)

            @block.vector
            def _(dve):
                dve.sem_inc(ev, 2)
                dve.wait_ge(x_in, 16)
                with dve.Fori(0, NGO) as g:
                    for n in range(4):
                        dve.wait_ge(acc, g * 4 + n + 1)
                        x = XR[:, bass.ds(g * 4 + n, 1)].rearrange("p o n -> p (o n)")
                        nc.vector.scalar_tensor_tensor(x[:, 0:SEQ], x[:, 0:SEQ], ALPHA, ps[2 * (n % 2)][:, :], ALU.mult, ALU.add)
                        nc.vector.scalar_tensor_tensor(x[:, SEQ:], x[:, SEQ:], ALPHA, ps[2 * (n % 2) + 1][:, 0:NS], ALU.mult, ALU.add).then_inc(ev, 1)

        layer_norm("ln1", XR, MIX, "ln1_g", "ln1_b")
        res.close()
        HT = MIX

        ffn = ExitStack()
        top.enter_context(ffn)
        AC = sb(ffn, "act_t", [P, FT, TOK])
        NF = FT // 4
        SR = 2 * B
        with ExitStack() as ph:
            W = sb(ph, "up_ring", [P, 4, KT, P])
            FB = sb(ph, "ffn_cols", [P, FT, SR + 3])
            UE = sb(ph, "u_ext", [P, 2, SEQ + 2])
            US = sb(ph, "u_ext_s", [P, 2, B, T + 2])
            UC = sb(ph, "u_conv", [P, 2, TOK])
            TL = sb(ph, "u_tail", [P, FT, 2 + SR])
            RAW = AC[0:SR + 3].rearrange("p f n -> p (f n)")[:, 0:FF]
            TO = W[0:2 + SR].rearrange("p s k c -> p (s k c)")[:, 0:FF]
            ps = banks(ph, "i")
            w_in = [sem(f"up_in{i}") for i in range(4)]
            raw_in, fb_ps, fb, acc, ue, cv, ge, uv, z9, tl, tev, tout, ch = (sem("f_" + n) for n in (
                "raw_in", "fb_ps", "fb", "acc", "ue", "conv", "gelu", "prod", "zero", "tail_ps", "tail_ev", "tail_out", "ch"))
            W_up = A["ffn_w_up"][0].rearrange("(k p) n -> p k n", p=P)
            block = ph.enter_context(nc.Block())
            NTR = FT // 4

            @block.sync
            def _(sp):
                sp.dma_start(RAW[0:SR], A["state_ffn_conv"][0].rearrange("b r c -> (b r) c")).then_inc(raw_in, 16)
                sp.dma_start(RAW[SR:SR + 3], A["ffn_conv_w"][0]).then_inc(raw_in, 16)
                for s in range(4):
                    c = (s % 2) * FF + (s // 2) * P
                    sp.dma_start(W[:, s], W_up[:, :, c:c + P]).then_inc(w_in[s], 16)
                with sp.Fori(1, FT // 2) as i:
                    for s in range(4):
                        sp.wait_ge(acc, i * 4 + s - 3)
                        sp.dma_start(W[:, s], W_up[:, :, bass.ds(i * 256 + ((s % 2) * FF + (s // 2) * P), P)]).then_inc(w_in[s], 16)
                sp.wait_ge(tev, NTR)
                sp.dma_start(O[7][0, 0], TO[0:2]).then_inc(tout, 16)
                sp.dma_start(O[13][0].rearrange("b r c -> (b r) c"), TO[2:2 + SR]).then_inc(tout, 16)
                sp.wait_ge(tout, 32)

            @block.tensor
            def _(pe):
                pe.wait_ge(raw_in, 32)
                n = SR + 3
                for q in range(NTR):
                    if q >= 2:
                        pe.wait_ge(fb, q - 1)
                    for k in range(4):
                        j = q * 4 + k
                        last = nc.tensor.transpose(ps[6 + q % 2][:, k * n:(k + 1) * n], RAW[:, j * P:(j + 1) * P], ident[0:n, 0:n])
                    last.then_inc(fb_ps, 1)
                with pe.Fori(0, FT // 2) as i:
                    for n in range(2):
                        pe.wait_ge(uv, i * 2 + n + 1)
                        for v in range(2):
                            s = 2 * n + v
                            pe.wait_ge(w_in[s], i * 16 + 16)
                            a, b = ps[3 * n + v], ps[3 * n + 2]
                            for k in range(KT):
                                nc.tensor.matmul(a[:, :], W[:, s, k], HT[:, k, 0:SEQ], start=k == 0, stop=k == KT - 1)
                                last = nc.tensor.matmul(b[:, v * NS:(v + 1) * NS], W[:, s, k], HT[:, k, SEQ:TOK], start=k == 0, stop=k == KT - 1)
                            last.then_inc(acc, 1)
                pe.wait_ge(uv, FT + 2)
                for q in range(NTR):
                    if q >= 2:
                        pe.wait_ge(tev, q - 1)
                    for k in range(4):
                        last = nc.tensor.transpose(ps[6 + q % 2][0:2 + SR, k * P:(k + 1) * P], TL[:, q * 4 + k], ident)
                    last.then_inc(tl, 1)

            @block.scalar
            def _(act):
                with act.Fori(0, FT // 2) as i:
                    for n in range(2):
                        act.wait_ge(acc, i * 4 + 2 * n + 2)
                        act.wait_ge(cv, i * 2 + n + 1)
                        nc.scalar.copy(UE[:, n, 2:], ps[3 * n][:, :])
                        nc.scalar.copy(US[:, n, :, 2:], ps[3 * n + 2][:, 0:NS].rearrange("p (b t) -> p b t", t=T)).then_inc(ue, 1)
                        act.wait_ge(cv, i * 2 + n + 3)
                        nc.scalar.activation(UC[:, n], UC[:, n], ACT.Gelu_apprx_tanh).then_inc(ge, 1)
                for q in range(NTR):
                    act.wait_ge(tl, q + 1)
                    nc.scalar.copy(TO[:, q * 512:(q + 1) * 512], ps[6 + q % 2][0:2 + SR, :]).then_inc(tev, 1)

            @block.vector
            def _(dve):
                dve.sem_inc(uv, 2)
                dve.sem_inc(cv, 2)
                n = SR + 3
                nc.vector.memset(UE[:, :, 0:2], 0.0)
                for q in range(NTR):
                    dve.wait_ge(fb_ps, q + 1)
                    nc.vector.tensor_copy(FB[:].rearrange("p f n -> p (f n)")[:, q * 4 * n:(q + 1) * 4 * n], ps[6 + q % 2][:, 0:4 * n]).then_inc(fb, 1)
                dve.wait_ge(fb, NTR)
                with dve.Fori(0, FT // 2) as i:
                    c = Count(dve, ch, i * 6)
                    for n in range(2):
                        j1 = bass.ds(i * 2 + n, 1)
                        dve.wait_ge(ue, i * 2 + n + 1)
                        c.link(nc.vector.tensor_copy(US[:, n, :, 0:2], FB[:, j1, 0:SR].rearrange("p o (b j) -> p (o b) j", j=2)))
                        for j in range(3):
                            w = FB[:, j1, SR + j]
                            o, x = UC[:, n, 0:SEQ], UE[:, n, j:j + SEQ]
                            os_, xs = UC[:, n, SEQ:].rearrange("p (b t) -> p b t", t=T), US[:, n, :, j:j + T]
                            if j == 0:
                                nc.vector.tensor_scalar(o, x, w, None, ALU.mult)
                                last = nc.vector.tensor_scalar(os_, xs, w, None, ALU.mult)
                            else:
                                nc.vector.scalar_tensor_tensor(o, x, w, o, ALU.mult, ALU.add)
                                last = nc.vector.scalar_tensor_tensor(os_, xs, w, os_, ALU.mult, ALU.add)
                            if j < 2:
                                c.link(last)
                        nc.vector.tensor_copy(TL[:, j1, 0:2].rearrange("p o r -> p (o r)"), UE[:, n, SEQ:SEQ + 2])
                        nc.vector.tensor_copy(TL[:, j1, 2:].rearrange("p o (b j) -> p (o b) j", j=2), US[:, n, :, T:T + 2]).then_inc(cv, 1)
                        dve.wait_ge(ge, i * 2 + n + 1)
                        out = AC[:, j1].rearrange("p o n -> p (o n)")
                        nc.vector.tensor_tensor(out[:, 0:SEQ], UC[:, n, 0:SEQ], ps[3 * n + 1][:, :], ALU.mult)
                        nc.vector.tensor_tensor(out[:, SEQ:], UC[:, n, SEQ:], ps[3 * n + 2][:, NS:2 * NS], ALU.mult).then_inc(uv, 1)

        with ExitStack() as ph:
            CH = 4
            KC = FT // CH
            W = sb(ph, "down_ring", [P, 8, KC, P])
            ps = banks(ph, "j")
            w_in = [sem(f"dn_in{i}") for i in range(8)]
            used, acc, ev = sem("d_used"), sem("d_acc"), sem("d_ev")
            W_dn = A["ffn_w_down"][0].rearrange("(k p) n -> p k n", p=P)
            block = ph.enter_context(nc.Block())
            NGD = DM // 256

            @block.sync
            def _(sp):
                for s in range(8):
                    sp.dma_start(W[:, s], W_dn[:, (s % CH) * KC:(s % CH + 1) * KC, (s // CH) * P:(s // CH + 1) * P]).then_inc(w_in[s], 16)
                with sp.Fori(1, NGD) as i:
                    for s in range(8):
                        sp.wait_ge(used, i * 8 + s - 7)
                        sp.dma_start(W[:, s], W_dn[:, (s % CH) * KC:(s % CH + 1) * KC, bass.ds(i * 256 + (s // CH) * P, P)]).then_inc(w_in[s], 16)
                sp.wait_ge(ev, NGD * 2 + 2)

            @block.tensor
            def _(pe):
                with pe.Fori(0, NGD) as i:
                    for n in range(2):
                        pe.wait_ge(ev, i * 2 + n + 1)
                        a, b = ps[2 * n], ps[2 * n + 1]
                        for c in range(CH):
                            s = n * CH + c
                            pe.wait_ge(w_in[s], i * 16 + 16)
                            for k in range(KC):
                                f = c * KC + k
                                nc.tensor.matmul(a[:, :], W[:, s, k], AC[:, f, 0:SEQ], start=f == 0, stop=f == FT - 1)
                                last = nc.tensor.matmul(b[:, 0:NS], W[:, s, k], AC[:, f, SEQ:TOK], start=f == 0, stop=f == FT - 1)
                            last.then_inc(used, 1)

            @block.vector
            def _(dve):
                dve.sem_inc(ev, 2)
                with dve.Fori(0, NGD) as i:
                    for n in range(2):
                        dve.wait_ge(used, i * 8 + 4 * n + 4)
                        x = HT[:, bass.ds(i * 2 + n, 1)].rearrange("p o n -> p (o n)")
                        nc.vector.scalar_tensor_tensor(x[:, 0:SEQ], x[:, 0:SEQ], ALPHA, ps[2 * n][:, :], ALU.mult, ALU.add)
                        nc.vector.scalar_tensor_tensor(x[:, SEQ:], x[:, SEQ:], ALPHA, ps[2 * n + 1][:, 0:NS], ALU.mult, ALU.add).then_inc(ev, 1)
        ffn.close()
        layer_norm("ln2", HT, HT, "ln2_g", "ln2_b")

        with ExitStack() as ph:
            YN = sb(ph, "y_rows", [P, QT + 1, DM])
            ps = banks(ph, "k")
            tr, ev_v, ev_a, out = (sem("y_" + n) for n in ("tr", "ev_v", "ev_a", "out"))
            block = ph.enter_context(nc.Block())

            @block.sync
            def _(sp):
                for t in range(QT + 1):
                    sp.wait_ge(ev_v, 2 * t + 2)
                    sp.wait_ge(ev_a, 2 * t + 2)
                    if t < QT:
                        sp.dma_start(O[0][0, t * P:(t + 1) * P, :], YN[:, t]).then_inc(out, 16)
                    else:
                        sp.dma_start(O[1].rearrange("b t d -> (b t) d"), YN[0:NS, t]).then_inc(out, 16)
                sp.wait_ge(out, 16 * (QT + 1))

            @block.tensor
            def _(pe):
                for u in range(20):
                    tt, kg = u // 4, u % 4
                    n = P if tt < QT else NS
                    if u >= 8:
                        pe.wait_ge(ev_v if u % 2 == 0 else ev_a, (u - 8) // 2 + 1)
                    for k in range(4):
                        last = nc.tensor.transpose(ps[u % 8][0:n, k * P:(k + 1) * P], HT[:, kg * 4 + k, tt * P:tt * P + n], ident)
                    last.then_inc(tr, 1)

            def rows_evac(eng, copy, par, s):
                for u in range(par, 20, 2):
                    tt, kg = u // 4, u % 4
                    n = P if tt < QT else NS
                    eng.wait_ge(tr, u + 1)
                    copy(YN[0:n, tt, kg * 512:(kg + 1) * 512], ps[u % 8][0:n, :]).then_inc(s, 1)

            @block.vector
            def _(dve):
                rows_evac(dve, nc.vector.tensor_copy, 0, ev_v)

            @block.scalar
            def _(act):
                rows_evac(act, nc.scalar.copy, 1, ev_a)
_INS = ['x_prompt','x_sample','cache_cmp_kv','cache_slc_kv','cache_win_kv','state_gdn','state_gdn_conv','state_ffn_conv','page_table','w_in','w_o','cmp_pe','cmp_w1','cmp_w2','gdn_conv_w','gdn_a_log','gdn_dt_bias','gdn_norm_g','ln1_g','ln1_b','ffn_w_up','ffn_conv_w','ffn_w_down','ln2_g','ln2_b']
_OUTS = [(1,512,2048),(8,4,2048),(1,1,512,2,2,128),(1,1,512,2,2,128),(1,1,512,2,2,128),(1,1,8,128,128),(1,1,3,3072),(1,1,2,5632),
         (1,8,4,2,2,128),(1,8,4,2,2,128),(1,8,512,2,2,128),(1,8,8,128,128),(1,8,3,3072),(1,8,2,5632)]


def kernel(**inputs):
    import numpy as _np
    import concourse.bacc as _bacc
    from concourse import mybir as _mybir
    from concourse.bass_utils import run_bass_kernel_spmd as _run

    nc = _bacc.Bacc("TRN2", target_bir_lowering=False, num_devices=1)
    arrays, args = {}, {}
    for name in _INS:
        a = _np.ascontiguousarray(inputs[name])
        arrays[f"in_{name}_dram"] = a
        args[name] = nc.dram_tensor(f"in_{name}_dram", a.shape, _mybir.dt.from_np(a.dtype), kind="ExternalInput").ap()
    table, at = shape_constants()
    arrays['in_consts_dram'] = table
    consts = nc.dram_tensor('in_consts_dram', table.shape, _mybir.dt.float32, kind='ExternalInput').ap()
    outs = []
    for i, shape in enumerate(_OUTS):
        outs.append(nc.dram_tensor(f"out_{i}_dram", shape, _mybir.dt.float32, kind="ExternalOutput").ap())
    build(nc, args, outs, consts, at)
    r = _run(nc, [arrays], core_ids=[0])
    return tuple(r.results[0][f"out_{i}_dram"] for i in range(len(_OUTS)))
```

```python
import numpy as np
import concourse.bass as bass
from concourse import mybir
from contextlib import ExitStack

F32 = mybir.dt.float32
F32R = mybir.dt.float32r
I32 = mybir.dt.int32
ACT = mybir.ActivationFunctionType
ALU = mybir.AluOpType
AX = mybir.AxisListType.X

P = 128
DM = 2048
SEQ = 512
B, T = 8, 4
NS = B * T
TOK = SEQ + NS
HT2 = TOK // 2
SP2 = SEQ - HT2
PAST, PAGE = 2048, 128
NPG = PAST // PAGE
NPOOL = B * NPG * 5 // 4
HD = 128
H, KVH = 8, 2
GRP = H // KVH
BLK = 64
NB = PAST // BLK
NBT = NB + 1
WIN = 512
GH = 8
KT = DM // P
FF = 11 * DM // 4
FT = FF // P
QT = SEQ // P
KVC = KVH * 2 * HD
O_KV = H * HD
O_GATE = O_KV + 3 * KVC
O_QKV = O_GATE + 3 * H
O_Z = O_QKV + 3 * GH * HD
O_AB = O_Z + GH * HD
G_FIRST = O_GATE // 512
G_ALL = (O_AB - 3 * H) // 512
ALPHA = 2.0 ** 0.25
SCALE = HD ** -0.5
BIG = 1e33
R_Q, R_KV, R_QKV = 0, O_KV, O_GATE
R_Z = R_QKV + 3 * GH * HD


def shape_constants():
    i = np.arange(P)
    c = {"ident": np.eye(P), "ones": np.ones((P, P)), "upto": (i[:, None] <= i[None, :])}
    lv = []
    for l in range(7):
        s = 1 << l
        same = (i[:, None] // (2 * s)) == (i[None, :] // (2 * s))
        lv.append(same & ((i[:, None] // s) % 2 == 0) & ((i[None, :] // s) % 2 == 1))
    c["level"] = np.concatenate(lv, 1)
    same = (i[:, None] // T == i[None, :NS] // T) & (i[:, None] < NS)
    c["s_upto"] = same & (i[:, None] <= i[None, :NS])
    c["s_same"] = same
    c["s_batch"] = (i[:, None] // T == np.arange(B)[None, :])
    d = i[:, None] - np.arange(SEQ)[None, :] + SEQ - P
    c["dist"] = np.where(d >= 0, d, BIG)
    q = i[:, None, None] + P * np.arange(QT)[None, :, None]
    d = q - (BLK * np.arange(SEQ // BLK)[None, None, :] + BLK - 1)
    c["dist_c"] = np.where(d >= 0, d, BIG).reshape(P, -1)
    c["seen_c"] = (q[:, :, 0] >= BLK - 1)
    slope = 2.0 ** -(np.arange(H) + 1.0)
    c["slope"] = np.broadcast_to(-slope, (P, H))
    j, r, t = i // 32, (i % 32) // T, i % T
    real = (i % 32) < GRP * T
    sl = np.where(real, slope[(j % 2) * GRP + r % GRP], 0)[:, None]
    key = np.arange(PAST + T)[None, :]
    d = PAST + t[:, None] - key
    c["ali_s"] = np.where(d >= 0, -sl * d, -1e30)
    d = d[:, PAST - WIN:]
    c["ali_w"] = np.where((d >= 0) & (d < WIN), -sl * d, -1e30)
    c["ali_c"] = -sl * (PAST + t[:, None] - (BLK * np.arange(NB)[None, :] + BLK - 1))
    forced = np.zeros(NBT)
    forced[[0, NBT - 2, NBT - 1]] = 1
    c["unforced"] = np.broadcast_to(1 - forced, (P, NBT))
    c["forced"] = np.broadcast_to(1e4 * forced, (P, NBT))
    c["same_q"] = (j[:, None] == j[None, :]) & (t[:, None] == t[None, :]) & real[:, None] & real[None, :]
    at, parts, n = {}, [], 0
    for k, v in c.items():
        at[k] = (n, n + v.shape[1])
        n += v.shape[1]
        parts.append(np.asarray(v, np.float32))
    return np.concatenate(parts, 1), at


class Count:

    def __init__(self, eng, sem, base=0):
        self.eng, self.sem, self.base, self.n = eng, sem, base, 0

    def link(self, ins):
        self.n += 1
        ins.then_inc(self.sem, 1)
        self.eng.wait_ge(self.sem, self.base + self.n)


def product(nc, banks2, wh, wl, xh, xl, start, stop):
    for i, (w, x) in enumerate(((wh, xh), (wh, xl), (wl, xh))):
        for half in range(2):
            last = nc.tensor.matmul(banks2[half][:, 0:HT2], w, x[:, half * HT2:(half + 1) * HT2],
                                    start=start and i == 0, stop=stop and i == 2)
    return last


def build(nc, A, O, C_dram, AT):
    top = ExitStack()
    with top:
        held = []

        def sem(name):
            held.append(nc.alloc_semaphore(name=name))
            return held[-1]

        def clear_semaphores():
            nc.clear_and_free_semaphores(held)
            held.clear()
            nc.all_engine_barrier()

        def sb(ctx, name, shape, dt=F32):
            return ctx.enter_context(nc.sbuf_tensor(name, shape, dt))

        def banks(ctx, name):
            return [ctx.enter_context(nc.psum_tensor(f"{name}{i}", [P, 512], F32)) for i in range(8)]

        S_proj = nc.dram_tensor("s_proj", (G_ALL * 512, TOK), F32, kind="Internal").ap()
        S_xt = nc.dram_tensor("s_xt", (KT, P, TOK), F32, kind="Internal").ap()
        S_gate = nc.dram_tensor("s_gate", (NS, 3 * H), F32, kind="Internal").ap()

        C_N = AT["upto"][0]
        CS = sb(top, "consts", [P, C_N])
        GAB = sb(top, "gab", [P, QT + 1, 40])

        def cst(name, rows=P):
            a, b = AT[name]
            return CS[0:rows, a:b]

        ident = cst("ident")

        SR = 2 * B
        FB = sb(top, "ffn_cols", [P, FT, SR + 3])

        main = ExitStack()
        top.enter_context(main)
        XT = sb(main, "xt", [P, KT, TOK])
        c_sem = sem("consts_in")
        with ExitStack() as ph:
            xn = sb(ph, "x_nat", [P, QT + 1, DM])
            ps = banks(ph, "a")
            x_in, tr, ev_v, ev_a = (sem(n) for n in ("x_in", "x_tr", "x_ev_v", "x_ev_a"))
            block = ph.enter_context(nc.Block())

            @block.sync
            def _(sp):
                sp.dma_start(CS[:, :], C_dram[:, 0:C_N]).then_inc(c_sem, 16)
                sp.dma_start(xn[:, 0:QT, :], A["x_prompt"][0].rearrange("(t p) d -> p t d", p=P)).then_inc(x_in, 16)
                sp.dma_start(xn[0:NS, QT, :], A["x_sample"].rearrange("b t d -> (b t) d")).then_inc(x_in, 16)
                sp.wait_ge(ev_v, 10)
                sp.wait_ge(ev_a, 10)

            @block.tensor
            def _(pe):
                pe.wait_ge(c_sem, 16)
                pe.wait_ge(x_in, 32)
                for u in range(20):
                    tt, kg = u // 4, u % 4
                    n = P if tt < QT else NS
                    if u >= 8:
                        pe.wait_ge(ev_v if u % 2 == 0 else ev_a, (u - 8) // 2 + 1)
                    for k in range(4):
                        last = nc.tensor.transpose(ps[u % 8][:, k * n:(k + 1) * n],
                                                   xn[0:n, tt, (kg * 4 + k) * P:(kg * 4 + k + 1) * P],
                                                   ident[0:n, 0:n])
                    last.then_inc(tr, 1)

            def evac(eng, copy, par, s):
                for u in range(par, 20, 2):
                    tt, kg = u // 4, u % 4
                    n = P if tt < QT else NS
                    eng.wait_ge(tr, u + 1)
                    copy(XT[:, kg * 4:kg * 4 + 4, tt * P:tt * P + n],
                         ps[u % 8][:, 0:4 * n].rearrange("p (k n) -> p k n", k=4)).then_inc(s, 1)

            @block.vector
            def _(dve):
                evac(dve, nc.vector.tensor_copy, 0, ev_v)

            @block.scalar
            def _(act):
                evac(act, nc.scalar.copy, 1, ev_a)

        W_in = A["w_in"][0].rearrange("(k p) n -> p k n", p=P)
        with ExitStack() as ph:
            W = sb(ph, "w_ring", [P, 4, KT, P])
            WH = sb(ph, "w_hi", [P, 2, KT, P], F32R)
            WL = sb(ph, "w_lo", [P, 2, KT, P], F32R)
            XH = sb(ph, "x_hi", [P, KT, TOK], F32R)
            XL = sb(ph, "x_lo", [P, KT, TOK], F32R)
            WG = sb(ph, "w_small", [P, KT, 40])
            ST = sb(ph, "stage", [P, 4, TOK])
            tmp = sb(ph, "g_tmp", [P, QT + 1, 16])
            par = sb(ph, "g_par", [P, 2, GH])
            ps = banks(ph, "b")
            w_in = [sem(f"w_in{i}") for i in range(4)]
            wh, wl, xh, xl = (sem(n) for n in ("w_hi_r", "w_lo_r", "x_hi_r", "x_lo_r"))
            st_out = [sem(f"st_out{i}") for i in range(4)]
            acc, ev, wg, sm, smd, small, gs = (sem(n) for n in ("acc", "acc_ev", "wg_in", "sm_ps", "sm_done", "par_in", "gs_out"))
            dch, ach, sx = (sem(n) for n in ("ch2_v", "ch2_a", "sm_exp"))
            block = ph.enter_context(nc.Block())

            @block.sync
            def _(sp):
                for n in range(4):
                    sp.dma_start(W[:, n], W_in[:, :, n * P:(n + 1) * P]).then_inc(w_in[n], 16)
                sp.dma_start(S_xt.rearrange("k p n -> p k n"), XT[:]).then_inc(gs, 16)
                sp.dma_start(WG[:, :, 0:24], W_in[:, :, O_GATE:O_QKV]).then_inc(wg, 16)
                sp.dma_start(WG[:, :, 24:40], W_in[:, :, O_AB:O_AB + 16]).then_inc(wg, 16)
                sp.dma_start(par[:, 0, :], A["gdn_a_log"].partition_broadcast(P)[:, 0, :]).then_inc(small, 16)
                sp.dma_start(par[:, 1, :], A["gdn_dt_bias"].partition_broadcast(P)[:, 0, :]).then_inc(small, 16)
                for lo, hi, off in ((1, G_FIRST, 0), (G_FIRST, G_ALL, 24)):
                    with sp.Fori(lo, hi) as g:
                        for n in range(4):
                            sp.wait_ge(wl, g * 4 + n - 3)
                            sp.dma_start(W[:, n], W_in[:, :, bass.ds(g * 512 + (n * P + off), P)]).then_inc(w_in[n], 16)
                sp.wait_ge(smd, 1)
                sp.dma_start(S_gate[:, :], GAB[0:NS, QT, 0:24]).then_inc(gs, 16)
                sp.wait_ge(gs, 32)

            @block.tensor
            def _(pe):
                pe.sem_inc(acc, 2)
                pe.wait_ge(xl, 1)
                with pe.Fori(0, G_ALL) as g:
                    for n in range(4):
                        pe.wait_ge(wl, g * 4 + n + 1)
                        pe.wait_ge(ev, g * 4 + n + 1)
                        for k in range(KT):
                            last = product(nc, ps[2 * (n % 2):2 * (n % 2) + 2], WH[:, n % 2, k], WL[:, n % 2, k], XH[:, k], XL[:, k],
                                           k == 0, k == KT - 1)
                        last.then_inc(acc, 1)
                pe.wait_ge(wg, 32)
                for tt in range(QT + 1):
                    n = P if tt < QT else NS
                    for k in range(KT):
                        last = nc.tensor.matmul(ps[4 if tt < QT else 5][0:n, (tt % QT) * 40:(tt % QT) * 40 + 40], XT[:, k, tt * P:tt * P + n], WG[:, k],
                                                start=k == 0, stop=k == KT - 1)
                last.then_inc(sm, 1)

            @block.scalar
            def _(act):
                nc.scalar.copy(XH[:, 0:KT // 2], XT[:, 0:KT // 2]).then_inc(xh, 1)
                act.sem_inc(ev, 2)
                for n in range(4):
                    act.sem_inc(st_out[n], 16)
                with act.Fori(0, G_ALL) as g:
                    for n in range(4):
                        act.wait_ge(acc, g * 4 + n + 3)
                        act.wait_ge(st_out[n], g * 16 + 16)
                        nc.scalar.copy(ST[:, n, 0:HT2], ps[2 * (n % 2)][:, 0:HT2])
                        nc.scalar.copy(ST[:, n, HT2:TOK], ps[2 * (n % 2) + 1][:, 0:HT2]).then_inc(ev, 1)
                        act.wait_ge(ev, g * 4 + n + 3)
                        act.dma_start(S_proj[bass.ds(g * 512 + n * P, P), :], ST[:, n]).then_inc(st_out[n], 16)
                for n in range(4):
                    act.wait_ge(st_out[n], 16 * G_ALL + 16)
                ch = Count(act, ach)
                act.wait_ge(small, 32)
                nc.scalar.activation(par[:, 0, :], par[:, 0, :], ACT.Exp).then_inc(sx, 1)
                act.wait_ge(dch, 4)
                nc.scalar.activation(tmp[:, 0:QT, 8:16], tmp[:, 0:QT, 8:16], ACT.Exp, scale=-1.0)
                ch.link(nc.scalar.activation(tmp[0:NS, QT, 8:16], tmp[0:NS, QT, 8:16], ACT.Exp, scale=-1.0))
                nc.scalar.activation(tmp[:, 0:QT, 8:16], tmp[:, 0:QT, 8:16], ACT.Ln, bias=1.0)
                nc.scalar.activation(tmp[0:NS, QT, 8:16], tmp[0:NS, QT, 8:16], ACT.Ln, bias=1.0).then_inc(sx, 1)
                nc.scalar.activation(GAB[:, 0:QT, 0:24], GAB[:, 0:QT, 0:24], ACT.Sigmoid)
                nc.scalar.activation(GAB[0:NS, QT, 0:24], GAB[0:NS, QT, 0:24], ACT.Sigmoid).then_inc(smd, 1)
                nc.scalar.activation(GAB[:, 0:QT, 32:40], GAB[:, 0:QT, 32:40], ACT.Sigmoid)
                nc.scalar.activation(GAB[0:NS, QT, 32:40], GAB[0:NS, QT, 32:40], ACT.Sigmoid).then_inc(smd, 1)
                act.wait_ge(smd, 2)

            @block.gpsimd
            def _(gp):
                with gp.Fori(0, G_ALL) as g:
                    for n in range(4):
                        gp.wait_ge(wh, g * 4 + n + 1)
                        nc.gpsimd.tensor_tensor(WL[:, n % 2], W[:, n], WH[:, n % 2].bitcast(F32), ALU.subtract).then_inc(wl, 1)

            @block.vector
            def _(dve):
                nc.vector.tensor_copy(XH[:, KT // 2:], XT[:, KT // 2:]).then_inc(xh, 1)
                dve.wait_ge(xh, 2)
                nc.vector.tensor_tensor(XL[:], XT[:], XH[:].bitcast(F32), ALU.subtract).then_inc(xl, 1)
                with dve.Fori(0, G_ALL) as g:
                    for n in range(4):
                        dve.wait_ge(w_in[n], g * 16 + 16)
                        dve.wait_ge(acc, g * 4 + n + 1)
                        nc.vector.tensor_copy(WH[:, n % 2], W[:, n]).then_inc(wh, 1)
                dve.wait_ge(sm, 1)
                dve.wait_ge(small, 32)
                ch = Count(dve, dch)
                for rows, tiles in ((P, range(QT)), (NS, [QT])):
                    a, b = tiles[0], tiles[-1] + 1
                    src = ps[4 if rows == P else 5][0:rows, 0:40 * (b - a)].rearrange("p (t c) -> p t c", c=40)
                    dve_dt = par[0:rows, 1:2, :].broadcast_to((rows, b - a, GH))
                    nc.vector.tensor_copy(GAB[0:rows, a:b, :], src)
                    ch.link(nc.vector.tensor_tensor(tmp[0:rows, a:b, 0:8], src[:, :, 24:32], dve_dt, ALU.add))
                    ch.link(nc.vector.scalar_tensor_tensor(tmp[0:rows, a:b, 8:16], tmp[0:rows, a:b, 0:8], -1.0, tmp[0:rows, a:b, 0:8], ALU.mult, ALU.max))
                dve.wait_ge(sx, 2)
                for rows, tiles in ((P, range(QT)), (NS, [QT])):
                    a, b = tiles[0], tiles[-1] + 1
                    v = tmp[0:rows, a:b]
                    ea = par[0:rows, 0:1, :].broadcast_to((rows, b - a, GH))
                    ch.link(nc.vector.scalar_tensor_tensor(v[:, :, 0:8], v[:, :, 0:8], 0.0, v[:, :, 8:16], ALU.max, ALU.add))
                    ch.link(nc.vector.scalar_tensor_tensor(GAB[0:rows, a:b, 24:32], v[:, :, 0:8], -1.0, ea, ALU.mult, ALU.mult))

        main.close()

        with ExitStack() as ph:
            KV = sb(ph, "kv_t", [P, 12, TOK])
            NAT = sb(ph, "kv_nat", [P, QT + 1, 3 * KVC])
            RAW3 = sb(ph, "ffn_rows", [SR + 3, FF])
            ps = banks(ph, "c")
            kv_in, tr, ev_v, ev_a, out = (sem(n) for n in ("kv_in", "kv_tr", "kv_ev_v", "kv_ev_a", "kv_out"))
            raw_in, fb_ps, fb_a = (sem(n) for n in ("raw3_in", "fb_ps", "fb_a"))
            NF3, RF = 8, SR + 3
            FBS = [(q * FT // NF3, (q + 1) * FT // NF3) for q in range(NF3)]
            block = ph.enter_context(nc.Block())

            @block.sync
            def _(sp):
                sp.dma_start(KV[:], S_proj[R_KV:R_KV + 1536].rearrange("(k p) n -> p k n", p=P)).then_inc(kv_in, 16)
                sp.dma_start(RAW3[0:SR], A["state_ffn_conv"][0].rearrange("b r c -> (b r) c")).then_inc(raw_in, 16)
                sp.dma_start(RAW3[SR:RF], A["ffn_conv_w"][0]).then_inc(raw_in, 16)
                for b in range(B):
                    sp.dma_start(O[10][0, b, 0:WIN - T].rearrange("t g c d -> t (g c d)"),
                                 A["cache_win_kv"][0, b, T:WIN].rearrange("t g c d -> t (g c d)")).then_inc(out, 16)
                sp.wait_ge(ev_v, 8)
                sp.wait_ge(ev_a, 7)
                for i in range(3):
                    cols = slice(i * KVC, (i + 1) * KVC)
                    sp.dma_start(O[2 + i][0, 0].rearrange("(t p) g c d -> p t (g c d)", p=P), NAT[:, 0:QT, cols]).then_inc(out, 16)
                    if i < 2:
                        sp.dma_start(O[8 + i][0].rearrange("b t g c d -> (b t) (g c d)"), NAT[0:NS, QT, cols]).then_inc(out, 16)
                    else:
                        for b in range(B):
                            sp.dma_start(O[10][0, b, WIN - T:WIN].rearrange("t g c d -> t (g c d)"),
                                         NAT[b * T:(b + 1) * T, QT, cols]).then_inc(out, 16)
                sp.wait_ge(out, 16 * (2 * B + 5))

            @block.tensor
            def _(pe):
                pe.wait_ge(kv_in, 16)
                for u in range(15):
                    tt, i = u // 3, u % 3
                    n = P if tt < QT else NS
                    if u >= 8:
                        pe.wait_ge(ev_v if u % 2 == 0 else ev_a, (u - 8) // 2 + 1)
                    for k in range(4):
                        last = nc.tensor.transpose(ps[u % 8][0:n, k * P:(k + 1) * P], KV[:, i * 4 + k, tt * P:tt * P + n], ident)
                    last.then_inc(tr, 1)
                pe.wait_ge(raw_in, 32)
                pe.wait_ge(ev_v, 8)
                pe.wait_ge(ev_a, 7)
                for q, (lo, hi) in enumerate(FBS):
                    for k in range(lo, hi):
                        last = nc.tensor.transpose(ps[q][:, (k - lo) * RF:(k - lo + 1) * RF], RAW3[:, k * P:(k + 1) * P], ident[0:RF, 0:RF])
                    last.then_inc(fb_ps, 1)

            def evac(eng, copy, par, s):
                for u in range(par, 15, 2):
                    tt, i = u // 3, u % 3
                    n = P if tt < QT else NS
                    eng.wait_ge(tr, u + 1)
                    copy(NAT[0:n, tt, i * KVC:(i + 1) * KVC], ps[u % 8][0:n, :]).then_inc(s, 1)

            @block.vector
            def _(dve):
                evac(dve, nc.vector.tensor_copy, 0, ev_v)

            @block.scalar
            def _(act):
                evac(act, nc.scalar.copy, 1, ev_a)
                for q, (lo, hi) in enumerate(FBS):
                    act.wait_ge(fb_ps, q + 1)
                    nc.scalar.copy(FB[:, lo:hi].rearrange("p f n -> p (f n)"), ps[q][:, 0:(hi - lo) * RF]).then_inc(fb_a, 1)

        NPB = SEQ // BLK
        MIX = sb(top, "mix", [P, 2 * GH, TOK])
        att = ExitStack()
        top.enter_context(att)
        CK = sb(att, "ck", [P, B, NB, KVH])
        CV = sb(att, "cv", [NB, B, KVH, HD])
        CKP = sb(att, "ck_p", [P, NPB, KVH])
        CVP = sb(att, "cv_p", [NPB, KVH, HD])
        PT = sb(att, "pages", [1, B * NPG], I32)
        with ExitStack() as ph:
            RG = 8
            PP = 2 * NPG
            XN = sb(ph, "xn", [P, RG, 2 * KVC // 2])
            XTR = sb(ph, "xtr", [P, PP, 4, PAGE])
            W1 = sb(ph, "w1", [P, 2, BLK, HD])
            W2 = sb(ph, "w2", [P, 2, HD])
            HID = sb(ph, "hid", [P, 2, 2 * NB * KVH])
            PEB = sb(ph, "pe_bias", [P, 2])
            ps = banks(ph, "d")
            xn_in = [sem(f"xn_in{i}") for i in range(RG)]
            w_in4, pn_in, tr, ev_a, ev_v, acc, peb, hid, ckv, out4, pt_in = (sem("c_" + n) for n in (
                "w1_in", "pn_in", "tr", "ev_a", "ev_v", "acc", "peb", "hid", "ckv", "out", "pt_in"))
            block = ph.enter_context(nc.Block())
            pages = A["cache_cmp_kv"][0]
            NX = NPB // 2 + 1
            KV_T = XTR[:].rearrange("p q (g c) (n t) -> p c t (q g) n", c=2, n=2)

            @block.sync
            def _(sp):
                sp.dma_start(PT[:, :], A["page_table"].rearrange("(o b) n -> o (b n)", o=1)).then_inc(pt_in, 16)
                sp.dma_start(XN[:, 0:NX - 1], O[2][0, 0].rearrange("(q t) g c d -> t q (g c d)", t=PAGE)).then_inc(pn_in, 16)
                for n in range(2):
                    for g in range(KVH):
                        sp.dma_start(XN[n * BLK:(n + 1) * BLK, NX - 1, g * 2 * HD:(g + 1) * 2 * HD],
                                     A["cmp_pe"][0].rearrange("t c d -> t (c d)")).then_inc(pn_in, 16)
                for c in range(2):
                    sp.dma_start(W1[:, c], A["cmp_w1"][0, c].rearrange("(t d) e -> d t e", d=HD)).then_inc(w_in4, 16)
                sp.dma_start(W2[:], A["cmp_w2"][0].rearrange("c e d -> e c d")).then_inc(w_in4, 16)
                sp.wait_ge(pt_in, 16)
                with sp.Fori(0, B * NPG // RG) as i:
                    for r in range(RG):
                        page = sp.value_load(PT[0:1, bass.ds(i * RG + r, 1)], min_val=0, max_val=NPOOL - 1)
                        sp.wait_ge(tr, i * RG + (r + 1 if r >= NX else RG))
                        sp.dma_start(XN[:, r], pages[bass.ds(page, 1)].rearrange("o t g c d -> (o t) (g c d)")).then_inc(xn_in[r], 16)
                sp.wait_ge(ckv, 10)

            def turn(q, s):
                for j in range(4):
                    last = nc.tensor.transpose(ps[q % 4][:, j * P:(j + 1) * P], XN[:, s, j * P:(j + 1) * P], ident)
                last.then_inc(tr, 1)

            @block.tensor
            def _(pe):
                pe.sem_inc(tr, RG - NX)
                pe.wait_ge(pn_in, 80)
                for q in range(NX):
                    if q == 4:
                        pe.wait_ge(ev_a, 1)
                    turn(q, q)
                pe.wait_ge(w_in4, 48)
                pe.wait_ge(ev_a, 3)
                pe.wait_ge(ev_v, 2)
                for c in range(2):
                    for t in range(BLK):
                        last = nc.tensor.matmul(ps[4 + c][:, 0:NX * 4], W1[:, c, t], KV_T[:, c, t, 0:NX * KVH], start=t == 0, stop=t == BLK - 1)
                    last.then_inc(acc, 1)
                pe.wait_ge(hid, 1)
                nc.tensor.matmul(ps[6][:, 0:NPB * KVH], W2[:, 0], HID[:, 0, 0:NPB * KVH], start=True, stop=True)
                for g in range(KVH):
                    last = nc.tensor.matmul(ps[7][0:NPB, g * HD:(g + 1) * HD], HID[:, 1, g:NPB * KVH:KVH], W2[:, 1], start=True, stop=True)
                last.then_inc(out4, 1)
                with pe.Fori(0, B // 2) as i:
                    for q in range(PP):
                        if q < RG:
                            pe.wait_ge(xn_in[q % RG], i * (16 * PP // RG) + 16)
                        else:
                            pe.wait_ge(xn_in[q % RG], i * (16 * PP // RG) + 16 * (q // RG) + 16)
                        if q % 2 == 0:
                            pe.wait_ge(ev_a, i * (PP // 2) + q // 2 + 2)
                        else:
                            pe.wait_ge(ev_v, i * (PP // 2) + q // 2 + 1)
                        turn(q, q % RG)
                    pe.wait_ge(ev_a, (i + 1) * (PP // 2) + 3)
                    pe.wait_ge(ev_v, (i + 1) * (PP // 2) + 2)
                    for c in range(2):
                        for t in range(BLK):
                            last = nc.tensor.matmul(ps[4 + c][:, 0:2 * NB * KVH], W1[:, c, t], KV_T[:, c, t], start=t == 0, stop=t == BLK - 1)
                        last.then_inc(acc, 1)
                    pe.wait_ge(hid, i + 2)
                    pe.wait_ge(ckv, i * 2 + 2)
                    nc.tensor.matmul(ps[6][:, 0:2 * NB * KVH], W2[:, 0], HID[:, 0], start=True, stop=True)
                    for u in range(2 * KVH):
                        bp, g = u // KVH, u % KVH
                        last = nc.tensor.matmul(ps[7][0:NB, u * HD:(u + 1) * HD],
                                                HID[:, 1, bp * NB * KVH + g:(bp + 1) * NB * KVH:KVH], W2[:, 1], start=True, stop=True)
                    last.then_inc(out4, 1)

            def hidden(c, nq):
                n = nq * 4
                return nc.scalar.activation(HID[:, c, 0:n].rearrange("p (q n g) -> p q g n", n=2, g=KVH),
                                            ps[4 + c][:, 0:n].rearrange("p (q g n) -> p q g n", n=2, g=KVH), ACT.Silu, bias=PEB[:, c:c + 1])

            def pages_evac(eng, copy, par, s, i):
                for q in range(par, PP, 2):
                    eng.wait_ge(tr, i * PP + (RG + q + 1))
                    if q == par:
                        eng.wait_ge(acc, i * 2 + 2)
                    copy(XTR[:, q].rearrange("p j n -> p (j n)"), ps[q % 4][:, :]).then_inc(s, 1)

            @block.scalar
            def _(act):
                for q in range(0, NX, 2):
                    act.wait_ge(tr, q + 1 + RG - NX)
                    nc.scalar.copy(XTR[:, q].rearrange("p j n -> p (j n)"), ps[q % 4][:, :]).then_inc(ev_a, 1)
                act.wait_ge(peb, 2)
                for c in range(2):
                    last = hidden(c, NX - 1)
                last.then_inc(hid, 1)
                with act.Fori(0, B // 2) as i:
                    pages_evac(act, nc.scalar.copy, 0, ev_a, i)
                    act.wait_ge(acc, i * 2 + 4)
                    act.wait_ge(out4, i + 1)
                    for c in range(2):
                        last = hidden(c, PP)
                    last.then_inc(hid, 1)

            @block.vector
            def _(dve):
                for q in range(1, NX, 2):
                    dve.wait_ge(tr, q + 1 + RG - NX)
                    nc.vector.tensor_copy(XTR[:, q].rearrange("p j n -> p (j n)"), ps[q % 4][:, :]).then_inc(ev_v, 1)
                dve.wait_ge(acc, 2)
                n = (NX - 1) * 4
                for c in range(2):
                    nc.vector.tensor_copy(PEB[:, c:c + 1], ps[4 + c][:, n:n + 1]).then_inc(peb, 1)
                dve.wait_ge(out4, 1)
                nc.vector.tensor_copy(CKP[:].rearrange("p n g -> p (n g)"), ps[6][:, 0:NPB * KVH]).then_inc(ckv, 1)
                nc.vector.tensor_copy(CVP[:].rearrange("p g d -> p (g d)"), ps[7][0:NPB, 0:KVH * HD]).then_inc(ckv, 1)
                with dve.Fori(0, B // 2) as i:
                    pages_evac(dve, nc.vector.tensor_copy, 1, ev_v, i)
                    dve.wait_ge(out4, i + 2)
                    nc.vector.tensor_copy(CK[:, bass.ds(i * 2, 2)].rearrange("p b n g -> p (b n g)"), ps[6][:, 0:2 * NB * KVH]).then_inc(ckv, 1)
                    nc.vector.tensor_copy(CV[:, bass.ds(i * 2, 2)].rearrange("p b g d -> p (b g d)"), ps[7][0:NB, :]).then_inc(ckv, 1)

        with ExitStack() as ph:
            lo, hi = AT["dist"][0], AT["slope"][1]
            CP = sb(ph, "consts_p", [P, hi - lo])

            def cp(name):
                return CP[:, AT[name][0] - lo:AT[name][1] - lo]

            Q = sb(ph, "q_head", [P, SEQ])
            K = sb(ph, "k_t", [P, 2, KVH, SEQ])
            V = sb(ph, "v_rows", [P, QT, 2, KVH, HD])
            BH = sb(ph, "bias", [P, SEQ])
            BC = sb(ph, "bias_c", [P, QT * NPB])
            SC = sb(ph, "scores", [P, 4, SEQ])
            NM = sb(ph, "negmax", [P, 12])
            SU = sb(ph, "sums", [P, 12])
            RI = sb(ph, "inv", [P, 12])
            DG = sb(ph, "diag", [P, 3, P])
            PTS = sb(ph, "p_t", [P, 3, SEQ])
            ps = banks(ph, "e")
            (kv_in, q_in, s_ready, s_taken, m_ready, e_ready, d_ready, pt_ready, pts_ready, o_done, o_out, ch5) = (
                sem("a_" + n) for n in ("kv_in", "q_in", "s_ready", "s_taken", "m_ready", "e_ready", "d_ready", "pt_ready",
                                        "pts_ready", "o_done", "o_out", "ch"))
            block = ph.enter_context(nc.Block())
            JOBS = [(qt, br) for qt in range(QT) for br in range(3)]
            NJ = len(JOBS)

            def width(j):
                qt, br = JOBS[j]
                return NPB if br == 0 else (qt + 1) * P

            @block.sync
            def _(sp):
                sp.dma_start(CP[:, :], C_dram[:, lo:hi]).then_inc(kv_in, 16)
                for i in range(2):
                    for g in range(KVH):
                        r = R_KV + KVC * (i + 1) + g * 2 * HD
                        sp.dma_start(K[:, i, g], S_proj[r:r + P, 0:SEQ]).then_inc(kv_in, 16)
                        sp.dma_start(V[:, :, i, g, :], O[3 + i][0, 0, :, g, 1].rearrange("(t p) d -> p t d", p=P)).then_inc(kv_in, 16)
                sp.dma_start(Q[:, :], S_proj[0:P, 0:SEQ]).then_inc(q_in, 16)
                with sp.Fori(1, H) as h:
                    sp.wait_ge(s_ready, h * NJ)
                    sp.dma_start(Q[:, :], S_proj[bass.ds(h * P, P), 0:SEQ]).then_inc(q_in, 16)
                sp.wait_ge(o_out, 2 + H * QT)

            @block.tensor
            def _(pe):
                pe.sem_inc(pt_ready, 4)
                pe.sem_inc(o_done, 3)
                pe.wait_ge(kv_in, 144)

                def scores(h, g, j):
                    qt, br = JOBS[j]
                    pe.wait_ge(s_taken, h * NJ + j + 1)
                    rhs = CKP[:, :, g] if br == 0 else K[:, br - 1, g, 0:width(j)]
                    nc.tensor.matmul(ps[j % 3][:, 0:width(j)], Q[:, qt * P:(qt + 1) * P], rhs, start=True, stop=True).then_inc(s_ready, 1)

                def turn(h, j):
                    pe.wait_ge(d_ready, h * NJ + j + 1)
                    pe.wait_ge(pts_ready, h * NJ + j + 1)
                    w = width(j)
                    for k in range(-(-w // P)):
                        n = min(P, w)
                        last = nc.tensor.matmul(ps[3 + j % 3][0:n, k * P:(k + 1) * P], SC[:, j % 4, k * P:k * P + n], DG[:, j % 3],
                                                start=True, stop=True)
                    last.then_inc(pt_ready, 1)

                def values(h, g, j):
                    qt, br = JOBS[j]
                    if br == 0:
                        pe.wait_ge(o_out, h * QT + qt + 1)
                    pe.wait_ge(pts_ready, h * NJ + j + 4)
                    o = ps[6 + qt % 2][:, 0:P]
                    if br == 0:
                        last = nc.tensor.matmul(o, CVP[:, g], PTS[0:NPB, j % 3, 0:P], start=True, stop=False)
                    else:
                        for k in range(qt + 1):
                            last = nc.tensor.matmul(o, V[:, k, br - 1, g], PTS[:, j % 3, k * P:(k + 1) * P], start=False,
                                                    stop=br == 2 and k == qt)
                    last.then_inc(o_done, 1)

                for g in range(KVH):
                    with pe.Fori(g * GRP, (g + 1) * GRP) as h:
                        pe.wait_ge(q_in, h * 16 + 16)
                        scores(h, g, 0)
                        scores(h, g, 1)
                        for j in range(NJ):
                            turn(h, j)
                            if j + 2 < NJ:
                                scores(h, g, j + 2)
                            if j:
                                values(h, g, j - 1)
                        values(h, g, NJ - 1)

            @block.scalar
            def _(act):
                act.sem_inc(pts_ready, 3)
                act.sem_inc(o_out, 2)

                def turned(h, j):
                    n = min(P, width(j))
                    w = max(P, width(j))
                    act.wait_ge(pt_ready, h * NJ + j + 5)
                    act.wait_ge(o_done, h * NJ + j + 1)
                    nc.scalar.copy(PTS[0:n, j % 3, 0:w], ps[3 + j % 3][0:n, 0:w]).then_inc(pts_ready, 1)

                def output(h, j):
                    act.wait_ge(o_done, h * NJ + j + 4)
                    nc.scalar.copy(MIX[:, bass.ds(h, 1), JOBS[j][0] * P:(JOBS[j][0] + 1) * P].rearrange("p o n -> p (o n)"),
                                   ps[6 + JOBS[j][0] % 2][:, 0:P]).then_inc(o_out, 1)

                with act.Fori(0, H) as h:
                    for j in range(NJ + 1):
                        if j < NJ:
                            act.wait_ge(m_ready, h * NJ + j + 1)
                            s = SC[:, j % 4, 0:width(j)]
                            nc.scalar.activation(s, s, ACT.Exp, bias=NM[:, j:j + 1], accum_out=SU[:, j:j + 1]).then_inc(e_ready, 1)
                        if j:
                            turned(h, j - 1)
                        if j >= 4 and (j - 4) % 3 == 0:
                            output(h, j - 2)
                    output(h, NJ - 1)

            @block.vector
            def _(dve):
                PER = 2 + NJ + QT
                dve.sem_inc(s_taken, 3)
                dve.wait_ge(kv_in, 144)

                def diag(h, j, ch):
                    qt, br = JOBS[j]
                    dve.wait_ge(e_ready, h * NJ + j + 1)
                    ch.link(nc.vector.reciprocal(RI[:, j:j + 1], SU[:, j:j + 1]))
                    if br == 0:
                        ch.link(nc.vector.tensor_tensor(RI[:, j:j + 1], RI[:, j:j + 1], cp("seen_c")[:, qt:qt + 1], ALU.mult))
                    dve.wait_ge(pt_ready, h * NJ + j + 2)
                    gate = GAB[:, qt, bass.ds(h * 3 + br, 1)]
                    nc.vector.tensor_scalar(DG[:, j % 3], ident, RI[:, j:j + 1], gate, ALU.mult, ALU.mult).then_inc(d_ready, 1)

                with dve.Fori(0, H) as h:
                    ch = Count(dve, ch5, h * PER)
                    slope = cp("slope")[:, bass.ds(h, 1)]
                    ch.link(nc.vector.tensor_scalar(BH[:], cp("dist"), slope, None, ALU.mult))
                    ch.link(nc.vector.tensor_scalar(BC[:], cp("dist_c"), slope, None, ALU.mult))
                    for j in range(NJ + 1):
                        if j < NJ:
                            qt, br = JOBS[j]
                            w = width(j)
                            dve.wait_ge(s_ready, h * NJ + j + 1)
                            dve.wait_ge(pt_ready, h * NJ + j + 1)
                            bias = BC[:, qt * NPB:(qt + 1) * NPB] if br == 0 else BH[:, SEQ - w:]
                            s = SC[:, j % 4, 0:w]
                            ins = nc.vector.scalar_tensor_tensor(s, ps[j % 3][:, 0:w], SCALE, bias, ALU.mult, ALU.add)
                            ins.then_inc(s_taken, 1)
                            dve.wait_ge(s_taken, h * NJ + j + 4)
                            nc.vector.tensor_reduce(NM[:, j:j + 1], s, AX, ALU.max, negate=True).then_inc(m_ready, 1)
                        if j:
                            diag(h, j - 1, ch)
                    assert ch.n == PER

        NG = B // 2
        UN = 2 * KVH
        RW = GRP * T
        with ExitStack() as ph:
            lo, hi = AT["ali_s"][0], AT["same_q"][1]
            CP = sb(ph, "consts_s", [P, hi - lo])

            def cp(name, a=0, b=None):
                x, y = AT[name]
                return CP[:, x - lo + a:(y - lo if b is None else x - lo + b)]

            KN = sb(ph, "k_pages", [P, 2, NPG, KVH, HD])
            VN = sb(ph, "v_pages", [P, 2, NPG, KVH, HD])
            WN = sb(ph, "win_rows", [P, 2, WIN // P, KVH, 2, HD])
            VNEW = sb(ph, "v_new", [T, 2, 2, KVH, HD])
            QA = sb(ph, "q_all", [P, H, NS])
            KA = sb(ph, "k_new", [P, 2, KVH, NS])
            GR = sb(ph, "gates_r", [P, NG * 3])
            QS = sb(ph, "q_units", [P, 2, KVH, 32])
            MK = sb(ph, "misc_keys", [P, 2, KVH, NB + 2 * T])
            CVS = sb(ph, "cv_units", [NB, 2, KVH, HD])
            KTS = sb(ph, "k_t_s", [P, 4, 512])
            SC = sb(ph, "sc_slc", [P, PAST + T])
            SW = sb(ph, "sc_win", [P, WIN + T])
            PC = sb(ph, "sc_cmp", [P, NB])
            SCR = sb(ph, "rank", [P, NBT])
            SCR2 = sb(ph, "rank2", [P, NBT])
            SB8 = sb(ph, "sel_bias", [P, NBT])
            PAD = sb(ph, "pad", [P, 1])
            M8 = sb(ph, "max8", [P, 16])
            ST6 = sb(ph, "stats6", [P, 9])
            DG = sb(ph, "diag6", [P, 3, P])
            PTS = sb(ph, "p_t6", [P, 7, 512])
            ps = banks(ph, "f")
            (c_in, k_in, v_in, w_in6, prep, misc, pc_r, imp, kt_ps, kt_a, kt_v, s_task, s_free, m_r, e_r, d_r, t_ps, pt_a, pt_v, o_r, oe,
             ch6, gz) = (
                sem("s_" + n) for n in ("c_in", "k_in", "v_in", "w_in", "prep", "misc", "pc_r", "imp", "kt_ps", "kt_a", "kt_v", "task",
                                        "free", "m_r", "e_r", "d_r", "t_ps", "pt_a", "pt_v", "o_r", "oe", "ch", "gz"))
            block = ph.enter_context(nc.Block())
            NT = 5 * UN
            slc = A["cache_slc_kv"][0]
            win = A["cache_win_kv"][0]

            def gate_rows(eng, groups):
                eng.wait_ge(gz, 1)
                for G in groups:
                    for j in range(UN):
                        bp, g = j // KVH, j % KVH
                        b = 2 * G + bp
                        for r in range(GRP):
                            h = g * GRP + r
                            eng.dma_start(GR[32 * j + r * T:32 * j + (r + 1) * T, G * 3:G * 3 + 3],
                                          S_gate[b * T:(b + 1) * T, h * 3:h * 3 + 3]).then_inc(c_in, 16)

            def slc_rows(eng, G, half, dst, s, free, value):
                for bp in range(2):
                    with eng.Fori(0, NPG) as pg:
                        page = eng.value_load(PT[0:1, bass.ds((G * 2 + bp) * NPG + pg, 1)], min_val=0, max_val=NPOOL - 1)
                        eng.wait_ge(free, value)
                        eng.dma_start(dst[:, bp, bass.ds(pg, 1)].rearrange("p o g d -> p (o g) d"),
                                      slc[bass.ds(page, 1), :, :, half].rearrange("o t g d -> (o t) g d")).then_inc(s, 16)

            @block.sync
            def _(sp):
                sp.dma_start(CP[:, :], C_dram[:, lo:hi]).then_inc(c_in, 16)
                sp.dma_start(QA[:], S_proj[0:H * HD, SEQ:TOK].rearrange("(h p) n -> p h n", p=P)).then_inc(c_in, 16)
                for i in range(2):
                    for g in range(KVH):
                        r = R_KV + KVC * (i + 1) + g * 2 * HD
                        sp.dma_start(KA[:, i, g], S_proj[r:r + P, SEQ:TOK]).then_inc(c_in, 16)
                gate_rows(sp, range(0, NG // 2))

                with sp.Fori(0, NG) as G:
                    slc_rows(sp, G, 0, KN, k_in, s_task, G * NT + 4)
                    sp.wait_ge(oe, G + 1)
                    for bp in range(2):
                        b1 = bass.ds(G * 2 + bp, 1)
                        sp.dma_start(WN[:, bp].rearrange("p w g c d -> p w (g c d)"),
                                     win[b1].rearrange("o (w p) g c d -> p (o w) (g c d)", p=P)).then_inc(w_in6, 16)
                        sp.dma_start(VNEW[:, 0, bp], O[9][0, b1, :, :, 1].rearrange("o t g d -> (o t) g d")).then_inc(w_in6, 16)
                        sp.dma_start(VNEW[:, 1, bp], O[10][0, b1, WIN - T:WIN, :, 1].rearrange("o t g d -> (o t) g d")).then_inc(w_in6, 16)
                sp.wait_ge(oe, NG + 1)

            @block.gpsimd
            def _(gp):
                nc.gpsimd.memset(GR[:], 0.0).then_inc(gz, 1)
                nc.gpsimd.memset(QS[:], 0.0).then_inc(gz, 1)
                with gp.Fori(0, NG) as G:
                    slc_rows(gp, G, 1, VN, v_in, oe, G + 1)

            def kv_tile(t, page):
                c, j = t // UN, t % UN
                bp, g = j // KVH, j % KVH
                return WN[:, bp, page, g, 0] if c == 4 else KN[:, bp, c * 4 + page, g]

            @block.tensor
            def _(pe):
                pe.sem_inc(s_task, 4)
                pe.sem_inc(t_ps, 7)
                pe.sem_inc(o_r, 1)
                pe.wait_ge(c_in, 16 * (6 + NG * UN * GRP))

                def turn_keys(G, t):
                    k = t // 2
                    if t == 0:
                        pe.wait_ge(k_in, G * 512 + 512)
                    if t == 4 * UN:
                        pe.wait_ge(w_in6, G * 96 + 96)
                    pe.wait_ge(kt_v if t % 2 else kt_a, G * (NT // 2) + k + 1)
                    for page in range(4):
                        last = nc.tensor.transpose(ps[t % 2][:, page * P:(page + 1) * P], kv_tile(t, page), ident)
                    last.then_inc(kt_ps, 1)

                def scores(G, t):
                    c, j = t // UN, t % UN
                    if j == 0:
                        pe.wait_ge(s_free, G * 5 + max(c, 1))
                    pe.wait_ge(kt_v if t % 2 else kt_a, G * (NT // 2) + t // 2 + 2)
                    last = nc.tensor.matmul(ps[2 + c % 2][32 * j:32 * j + 32, :], QS[:, j // KVH, j % KVH], KTS[:, t % 4], start=True, stop=True)
                    last.then_inc(s_task, 1)

                def turn(G, u):
                    pe.wait_ge(pt_v if u % 2 else pt_a, (G * 3 if u % 2 else G * 4) + u // 2 + 1)
                    bank = ps[4 + u % 2]
                    if u < 4:
                        if u == 0:
                            pe.wait_ge(d_r, G * 3 + 2)
                        for k in range(4):
                            a = (u * 4 + k) * P
                            last = nc.tensor.matmul(bank[:, k * P:(k + 1) * P], SC[:, a:a + P], DG[:, 2], start=True, stop=True)
                    elif u == 4:
                        last = nc.tensor.matmul(bank[0:T, 0:P], SC[:, PAST:PAST + T], DG[:, 2], start=True, stop=True)
                    elif u == 5:
                        pe.wait_ge(d_r, G * 3 + 3)
                        for k in range(4):
                            last = nc.tensor.matmul(bank[:, k * P:(k + 1) * P], SW[:, k * P:(k + 1) * P], DG[:, 1], start=True, stop=True)
                    else:
                        nc.tensor.matmul(bank[0:NB, 0:P], PC[:, :], DG[:, 0], start=True, stop=True)
                        last = nc.tensor.matmul(bank[0:T, P:2 * P], SW[:, WIN:WIN + T], DG[:, 1], start=True, stop=True)
                    last.then_inc(t_ps, 1)

                with pe.Fori(0, NG) as G:
                    pe.wait_ge(prep, G + 1)
                    for j in range(UN):
                        last = nc.tensor.matmul(ps[6][32 * j:32 * j + 32, 0:NB + 2 * T], QS[:, j // KVH, j % KVH], MK[:, j // KVH, j % KVH],
                                                start=True, stop=True)
                    last.then_inc(misc, 1)
                    turn_keys(G, 0)
                    for t in range(NT):
                        if t + 1 < NT:
                            turn_keys(G, t + 1)
                        scores(G, t)
                        if t == 2 * UN - 1:
                            pe.wait_ge(pc_r, G + 1)
                            nc.tensor.matmul(ps[7][:, 0:NB], cp("same_q"), PC[:, :], start=True, stop=True).then_inc(imp, 1)
                    for u in range(7):
                        turn(G, u)
                    pe.wait_ge(pt_a, G * 4 + 5)
                    pe.wait_ge(pt_v, G * 3 + 4)
                    pe.wait_ge(v_in, G * 512 + 512)
                    for j in range(UN):
                        bp, g = j // KVH, j % KVH
                        o = ps[7][:, j * RW:(j + 1) * RW]
                        rows = slice(32 * j, 32 * j + RW)

                        def rhs(u, k, n=P):
                            return PTS[0:n, u, k * P + 32 * j:k * P + 32 * j + RW]

                        nc.tensor.matmul(o, CVS[:, bp, g], rhs(6, 0, NB), start=True, stop=False)
                        nc.tensor.matmul(o, VNEW[:, 1, bp, g], rhs(6, 1, T), start=False, stop=False)
                        nc.tensor.matmul(o, VNEW[:, 0, bp, g], rhs(4, 0, T), start=False, stop=False)
                        for k in range(4):
                            nc.tensor.matmul(o, WN[:, bp, k, g, 1], rhs(5, k), start=False, stop=False)
                        for k in range(NPG):
                            last = nc.tensor.matmul(o, VN[:, bp, k, g], rhs(k // 4, k % 4), start=False, stop=k == NPG - 1)
                    last.then_inc(o_r, 1)

            def keys_evac(eng, copy, G, t, s):
                eng.wait_ge(kt_ps, G * NT + t + 1)
                eng.wait_ge(s_task, G * NT + t + 1)
                copy(KTS[:, t % 4], ps[t % 2][:, :]).then_inc(s, 1)

            def turn_evac(eng, copy, G, u, s):
                eng.wait_ge(t_ps, G * 7 + u + 8)
                eng.wait_ge(o_r, G + 1)
                bank = ps[4 + u % 2]
                if u == 6:
                    copy(PTS[0:NB, 6, 0:P], bank[0:NB, 0:P])
                    copy(PTS[0:T, 6, P:2 * P], bank[0:T, P:2 * P]).then_inc(s, 1)
                elif u == 4:
                    copy(PTS[0:T, 4, 0:P], bank[0:T, 0:P]).then_inc(s, 1)
                else:
                    copy(PTS[:, u], bank[:, :]).then_inc(s, 1)

            @block.scalar
            def _(act):
                gate_rows(act, range(NG // 2, NG))
                act.sem_inc(kt_a, 1)
                act.sem_inc(pt_a, 1)

                def expo(G, i, order, tile):
                    act.wait_ge(m_r, G * 3 + order + 1)
                    nc.scalar.activation(tile, tile, ACT.Exp, bias=ST6[:, i:i + 1], accum_out=ST6[:, 3 + i:4 + i]).then_inc(e_r, 1)

                with act.Fori(0, NG) as G:
                    for t in range(0, NT, 2):
                        keys_evac(act, nc.scalar.copy, G, t, kt_a)
                        if t == 0:
                            expo(G, 0, 0, PC[:, :])
                    expo(G, 2, 1, SC[:, :])
                    expo(G, 1, 2, SW[:, :])
                    for u in range(0, 7, 2):
                        turn_evac(act, nc.scalar.copy, G, u, pt_a)

            @block.vector
            def _(dve):
                dve.sem_inc(kt_v, 1)
                dve.sem_inc(pt_v, 1)
                dve.sem_inc(s_free, 1)
                dve.sem_inc(oe, 1)
                dve.wait_ge(c_in, 16 * (6 + NG * UN * GRP))
                dve.wait_ge(gz, 2)
                LINKS = 13

                def chunk(G, c):
                    dve.wait_ge(s_task, G * NT + UN * (c + 1) + 4)
                    dst = SW[:, 0:WIN] if c == 4 else SC[:, c * 512:(c + 1) * 512]
                    bias = cp("ali_w", 0, WIN) if c == 4 else cp("ali_s", c * 512, (c + 1) * 512)
                    nc.vector.scalar_tensor_tensor(dst, ps[2 + c % 2][:, :], SCALE, bias, ALU.mult, ALU.add).then_inc(s_free, 1)

                with dve.Fori(0, NG) as G:
                    ch = Count(dve, ch6, G * LINKS)
                    dve.wait_ge(o_r, G + 1)
                    for bp in range(2):
                        b1, b4 = bass.ds(G * 2 + bp, 1), bass.ds(G * 8 + bp * T, T)
                        nc.vector.tensor_copy(QS[:, bp, :, 0:RW], QA[:, :, b4].rearrange("p (g r) t -> p g r t", g=KVH))
                        nc.vector.tensor_copy(MK[:, bp, :, 0:NB], CK[:, b1].rearrange("p o n g -> p g (o n)"))
                        for i in range(2):
                            nc.vector.tensor_copy(MK[:, bp, :, NB + i * T:NB + (i + 1) * T], KA[:, i, :, b4])
                    nc.vector.tensor_copy(CVS[:].rearrange("p b g d -> p (b g d)"), CV[:, bass.ds(G * 2, 2)].rearrange("p b g d -> p (b g d)")).then_inc(prep, 1)
                    dve.wait_ge(misc, G + 1)
                    m = ps[6]
                    ch.link(nc.vector.scalar_tensor_tensor(PC[:, :], m[:, 0:NB], SCALE, cp("ali_c"), ALU.mult, ALU.add))
                    nc.vector.tensor_reduce(ST6[:, 0:1], PC[:, :], AX, ALU.max, negate=True).then_inc(m_r, 1)
                    nc.vector.scalar_tensor_tensor(SC[:, PAST:], m[:, NB:NB + T], SCALE, cp("ali_s", PAST, PAST + T), ALU.mult, ALU.add)
                    ch.link(nc.vector.scalar_tensor_tensor(SW[:, WIN:], m[:, NB + T:NB + 2 * T], SCALE, cp("ali_w", WIN, WIN + T), ALU.mult, ALU.add))
                    keys_evac(dve, nc.vector.tensor_copy, G, 1, kt_v)
                    dve.wait_ge(e_r, G * 3 + 1)
                    ch.link(nc.vector.reciprocal(ST6[:, 6:7], ST6[:, 3:4]))
                    nc.vector.tensor_scalar(PC[:, :], PC[:, :], ST6[:, 6:7], None, ALU.mult).then_inc(pc_r, 1)
                    nc.vector.tensor_scalar(DG[:, 0], ident, GR[:, bass.ds(G * 3, 1)], None, ALU.mult).then_inc(d_r, 1)
                    for t in range(3, NT, 2):
                        keys_evac(dve, nc.vector.tensor_copy, G, t, kt_v)
                        if t % UN == UN - 1:
                            chunk(G, t // UN)
                        if t == 9:
                            dve.wait_ge(imp, G + 1)
                            nc.vector.tensor_copy(SCR[:, NB:NBT], cp("forced", NB, NBT))
                            ch.link(nc.vector.tensor_tensor(SCR[:, 0:NB], ps[7][:, 0:NB], cp("unforced", 0, NB), ALU.mult))
                            ch.link(nc.vector.tensor_tensor(SCR[:, 0:NB], SCR[:, 0:NB], cp("forced", 0, NB), ALU.add))
                            nc.vector.memset(PAD[:, :], 0.0)
                            ch.link(nc.vector.max(M8[:, 0:8], SCR[:, :]))
                            nc.vector.memset(PAD[:, :], 0.0)
                            ch.link(nc.vector.match_replace(SCR2[:, :], M8[:, 0:8], SCR[:, :], -1.0))
                            nc.vector.memset(PAD[:, :], 0.0)
                            ch.link(nc.vector.max(M8[:, 8:16], SCR2[:, :]))
                            nc.vector.memset(PAD[:, :], 0.0)
                            ch.link(nc.vector.match_replace(SCR[:, :], M8[:, 8:16], SCR2[:, :], -1.0))
                            ch.link(nc.vector.tensor_scalar(SB8[:, :], SCR[:, :], 0.0, -1e30, ALU.is_ge, ALU.mult))
                    dve.wait_ge(s_free, G * 5 + 6)
                    view = SC[:, 0:PAST].rearrange("p (n k) -> p n k", k=BLK)
                    sel = SB8[:, 0:NB].rearrange("p (n o) -> p n o", o=1).broadcast_to((P, NB, BLK))
                    ch.link(nc.vector.tensor_tensor(view, view, sel, ALU.add))
                    nc.vector.tensor_reduce(ST6[:, 2:3], SC[:, :], AX, ALU.max, negate=True).then_inc(m_r, 1)
                    nc.vector.tensor_reduce(ST6[:, 1:2], SW[:, :], AX, ALU.max, negate=True).then_inc(m_r, 1)
                    dve.wait_ge(e_r, G * 3 + 2)
                    ch.link(nc.vector.reciprocal(ST6[:, 8:9], ST6[:, 5:6]))
                    nc.vector.tensor_scalar(DG[:, 2], ident, ST6[:, 8:9], GR[:, bass.ds(G * 3 + 1, 1)], ALU.mult, ALU.mult).then_inc(d_r, 1)
                    dve.wait_ge(e_r, G * 3 + 3)
                    ch.link(nc.vector.reciprocal(ST6[:, 7:8], ST6[:, 4:5]))
                    nc.vector.tensor_scalar(DG[:, 1], ident, ST6[:, 7:8], GR[:, bass.ds(G * 3 + 2, 1)], ALU.mult, ALU.mult).then_inc(d_r, 1)
                    for u in range(1, 7, 2):
                        turn_evac(dve, nc.vector.tensor_copy, G, u, pt_v)
                    dve.wait_ge(o_r, G + 2)
                    for bp in range(2):
                        last = nc.vector.tensor_copy(MIX[:, 0:H, bass.ds(G * 8 + (SEQ + bp * T), T)],
                                                     ps[7][:, bp * 2 * RW:(bp + 1) * 2 * RW].rearrange("p (h t) -> p h t", t=T))
                    last.then_inc(oe, 1)
                    assert ch.n == LINKS

        att.close()
        clear_semaphores()

        CW = 3 * GH * HD
        NL = 7
        QC = QT
        with ExitStack() as ph:
            lo, hi = AT["upto"][0], AT["s_batch"][1]
            CP = sb(ph, "consts_g", [P, hi - lo])

            def cp(name, rows=P):
                return CP[0:rows, AT[name][0] - lo:AT[name][1] - lo]

            upto, s_upto = cp("upto"), cp("s_upto", NS)
            level = cp("level").rearrange("p (l c) -> p l c", l=NL)
            ones = cst("ones")
            RAW = sb(ph, "conv_rows", [3 * B + 4, CW])
            CB = sb(ph, "conv_cols", [P, 3, GH, 3 * B + 4])
            E = sb(ph, "ext", [P, 3, SEQ + 3])
            ES = sb(ph, "ext_s", [P, 3, B, T + 3])
            CT = sb(ph, "conv_out", [P, 3, TOK])
            TAIL = sb(ph, "conv_tail", [P, 3, 3 + 3 * B])
            TO = sb(ph, "conv_tail_rows", [3 + 3 * B, 3, HD])
            ZT = sb(ph, "z_t", [P, TOK])
            NAT = sb(ph, "qkv_rows", [P, QT + 1, 3, HD])
            SQ = sb(ph, "squares", [P, QT, 2, HD])
            RN = sb(ph, "inv_norm", [P, QT + 1, 2])
            KN, KB, KG, KD, QN, QG, VB = (sb(ph, n, [P, QT + 1, HD]) for n in ("kn", "kb", "kbg", "kd", "qn", "qg", "vb"))
            TR = sb(ph, "turned", [P, QT + 1, 4, HD])
            GC = sb(ph, "g_cum", [P, QT + 1, GH])
            GTOT = sb(ph, "g_tot", [P, QT + 1, GH])
            EG = sb(ph, "exp_g", [P, QT + 1, GH])
            ED = sb(ph, "exp_rest", [P, QT + 1, GH])
            GM = sb(ph, "g_masked", [NS, B, GH])
            GLS = sb(ph, "gl_s", [P, B, GH])
            GLP = sb(ph, "gl_p", [P, QT, GH])
            NG_ = sb(ph, "norm_g", [P, 1])
            UG = sb(ph, "upto_g", [P, QT, P])
            UGS = sb(ph, "upto_g_s", [NS, NS])
            DT = sb(ph, "decay", [P, QT, P])
            DTS = sb(ph, "decay_s", [NS, NS])
            AQ = sb(ph, "aq", [P, QT, 2, P])
            AQS = sb(ph, "aq_s", [NS, 2, NS])
            M = sb(ph, "a_levels", [P, NL, QT, P])
            MS = sb(ph, "a_levels_s", [NS, 2, NS])
            TI = sb(ph, "t_inv", [P, QT, P])
            TT = sb(ph, "inv_t", [P, QT, P])
            Y = sb(ph, "y", [P, QT, P])
            TIS, TTS, YS = (sb(ph, n, [NS, NS]) for n in ("inv_s", "inv_t_s", "y_s"))
            WT = sb(ph, "w_neg", [P, QT, P])
            WQ = sb(ph, "wq_s", [P, B, 2, T])
            WS = sb(ph, "ws_s", [P, 2, NS])
            VNW = sb(ph, "v_new7", [P, QT, HD])
            VNS = sb(ph, "v_new7_s", [NS, HD])
            VM = sb(ph, "v_masked", [NS, B, HD])
            S = sb(ph, "state", [P, HD])
            SS = sb(ph, "states_s", [P, B, HD])
            SN = sb(ph, "states_new", [P, B, HD])
            ON = sb(ph, "o_rows", [P, QT + 1, HD])
            RO = sb(ph, "inv_rms", [P, QT + 1])
            PAD7 = sb(ph, "pad7", [P, 1])
            ps = banks(ph, "g")
            made = {}

            def s7(name):
                if name not in made:
                    made[name] = sem("g_" + name)
                return made[name]

            block = ph.enter_context(nc.Block())
            QKV = S_proj[R_QKV:R_QKV + CW].rearrange("(i h p) n -> p i h n", i=3, p=P)
            ZALL = S_proj[R_Z:R_Z + GH * HD].rearrange("(h p) n -> p h n", p=P)
            TILES = [(t, P) for t in range(QT)] + [(QC, NS)]

            def col(tile, rows, h, off=0, tiles=slice(0, QT)):
                c = tile[0:rows, tiles, bass.ds(h + off, 1)]
                return c.broadcast_to((rows, c.shape[1], HD))

            @block.sync
            def _(sp):
                sp.dma_start(CP[:, :], C_dram[:, lo:hi]).then_inc(s7("c_in"), 16)
                sp.dma_start(RAW[0:3 * B], A["state_gdn_conv"][0].rearrange("b r c -> (b r) c")).then_inc(s7("c_in"), 16)
                sp.dma_start(RAW[3 * B:3 * B + 4], A["gdn_conv_w"][0]).then_inc(s7("c_in"), 16)
                sp.dma_start(NG_[:, :], A["gdn_norm_g"].rearrange("o (p q) -> p (o q)", q=1)).then_inc(s7("c_in"), 16)

                with sp.Fori(0, GH) as h:
                    sp.wait_ge(s7("fin"), h + 1)
                    h1 = bass.ds(h, 1)
                    sp.dma_start(ZT[:, :], ZALL[:, h1].rearrange("p o n -> p (o n)")).then_inc(s7("z_in"), 16)
                    sp.dma_start(SS[:], A["state_gdn"][0, :, h1].rearrange("b o k v -> k (b o) v")).then_inc(s7("z_in"), 16)
                    sp.wait_ge(s7("tail"), h + 1)
                    cols = bass.ds(h * HD, HD)
                    sp.dma_start(O[6][0, 0].rearrange("r (i c) -> r i c", i=3)[:, :, cols], TO[0:3]).then_inc(s7("out"), 16)
                    sp.dma_start(O[12][0].rearrange("b r (i c) -> (b r) i c", i=3)[:, :, cols], TO[3:3 + 3 * B]).then_inc(s7("out"), 16)
                    sp.wait_ge(s7("s_fin"), h + 1)
                    sp.dma_start(O[5][0, 0, h1].rearrange("o k v -> k (o v)"), S[:, :]).then_inc(s7("out"), 16)
                    sp.dma_start(O[11][0, :, h1].rearrange("b o k v -> k (b o) v"), SN[:]).then_inc(s7("out"), 16)
                    sp.wait_ge(s7("out"), h * 64 + 64)
                    sp.sem_inc(s7("stored"), 1)
                sp.wait_ge(s7("fin"), GH + 1)

            @block.gpsimd
            def _(gp):
                nc.gpsimd.memset(E[:, :, 0:3], 0.0).then_inc(s7("zero"), 1)
                gp.wait_ge(s7("c_in"), 64)
                def load(h):
                    for i in range(3):
                        q = QKV[:, i, bass.ds(h, 1)]
                        gp.dma_start(E[:, i, 3:], q[:, :, 0:SEQ].rearrange("p o n -> p (o n)")).then_inc(s7("e_in"), 16)
                        gp.dma_start(ES[:, i, :, 3:], q[:, :, SEQ:].rearrange("p o (b t) -> p (o b) t", t=T)).then_inc(s7("e_in"), 16)

                def head(h, more):
                    gp.wait_ge(s7("levels"), h + 1)
                    g = GAB[:, 0:QT, bass.ds(h + 24, 1)].broadcast_to((P, QT, P))
                    nc.gpsimd.tensor_tensor(UG[:], upto.rearrange("p (o c) -> p o c", o=1).broadcast_to((P, QT, P)), g, ALU.mult)
                    gs = GAB[0:NS, QC:QC + 1, bass.ds(h + 24, 1)].broadcast_to((NS, 1, NS))
                    nc.gpsimd.tensor_tensor(UGS[:].rearrange("p (o c) -> p o c", o=1), s_upto.rearrange("p (o c) -> p o c", o=1), gs, ALU.mult).then_inc(s7("ug"), 1)
                    if more:
                        gp.wait_ge(s7("conv"), h + 1)
                        load(h + 1)
                    gp.wait_ge(s7("nat"), h + 1)
                    gp.wait_ge(s7("nat_a"), h + 1)
                    for a, b, rows in ((0, QT, P), (QC, QC + 1, NS)):
                        last = nc.gpsimd.tensor_tensor(VB[0:rows, a:b], NAT[0:rows, a:b, 2], col(GAB, rows, h, 32, slice(a, b)), ALU.mult)
                    last.then_inc(s7("vb"), 1)
                    gp.wait_ge(s7("qn"), h + 1)
                    for a, b, rows in ((0, QT, P), (QC, QC + 1, NS)):
                        last = nc.gpsimd.tensor_tensor(QG[0:rows, a:b], QN[0:rows, a:b], col(EG, rows, h, 0, slice(a, b)), ALU.mult)
                    last.then_inc(s7("qg"), 1)
                    for dst, src, c in ((KG, KB, EG), (KD, KN, ED)):
                        for a, b, rows in ((0, QT, P), (QC, QC + 1, NS)):
                            last = nc.gpsimd.tensor_tensor(dst[0:rows, a:b], src[0:rows, a:b], col(c, rows, h, 0, slice(a, b)), ALU.mult)
                    last.then_inc(s7("kd"), 1)
                    gp.wait_ge(s7("aq"), h + 1)
                    nc.gpsimd.tensor_tensor(MS[:, 1], AQS[:, 0], level[0:NS, 1, 0:NS], ALU.mult)
                    for l in range(1, NL):
                        nc.gpsimd.tensor_tensor(M[:, l], AQ[:, :, 0], level[:, l:l + 1].broadcast_to((P, QT, P)), ALU.mult).then_inc(s7("m"), 1)

                load(0)
                with gp.Fori(0, GH - 1) as h:
                    head(h, True)
                head(GH - 1, False)

            @block.tensor
            def _(pe):
                pe.wait_ge(s7("c_in"), 64)
                n = 3 * B + 4
                for k in range(3 * GH):
                    last = nc.tensor.transpose(ps[k // 12][:, (k % 12) * n:(k % 12 + 1) * n], RAW[:, k * P:(k + 1) * P], ident[0:n, 0:n])
                last.then_inc(s7("cb_ps"), 1)
                nc.tensor.matmul(ps[2][:, 0:QT * GH], upto, GAB[:, 0:QT, 24:32], start=True, stop=True)
                nc.tensor.matmul(ps[2][:, 32:32 + QT * GH], ones, GAB[:, 0:QT, 24:32], start=True, stop=True)
                nc.tensor.matmul(ps[3][0:NS, 0:GH], s_upto, GAB[0:NS, QC, 24:32], start=True, stop=True)
                nc.tensor.matmul(ps[3][0:NS, GH:2 * GH], cp("s_same", NS), GAB[0:NS, QC, 24:32], start=True, stop=True).then_inc(s7("gc_ps"), 1)
                pe.wait_ge(s7("gm"), 1)
                nc.tensor.matmul(ps[4][:, 0:B * GH], ones[0:NS, :], GM[:].rearrange("p b h -> p (b h)"), start=True, stop=True).then_inc(s7("gl_ps"), 1)
                pe.wait_ge(s7("pre"), 1)

                with pe.Fori(0, GH) as h:
                    pe.wait_ge(s7("ug"), h + 1)
                    nc.tensor.matmul(ps[6][:, :], ones, UG[:].rearrange("p t c -> p (t c)"), start=True, stop=True)
                    nc.tensor.matmul(ps[7][0:NS, 0:NS], ones[0:NS, 0:NS], UGS[:], start=True, stop=True).then_inc(s7("gb"), 1)
                    pe.wait_ge(s7("silu"), h + 1)
                    for t, n in TILES:
                        for i in range(3):
                            last = nc.tensor.transpose(ps[t][0:n, i * P:(i + 1) * P], CT[:, i, t * P:t * P + n], ident)
                    last.then_inc(s7("nat_ps"), 1)
                    for i in range(3):
                        last = nc.tensor.transpose(ps[5][0:3 + 3 * B, i * P:(i + 1) * P], TAIL[:, i], ident)
                    last.then_inc(s7("tail_ps"), 1)
                    pe.wait_ge(s7("qg"), h + 1)
                    for t, n in TILES:
                        for i, x in enumerate((KN, KB, QN, QG)):
                            last = nc.tensor.transpose(ps[t][:, i * n:(i + 1) * n], x[0:n, t], ident[0:n, 0:n])
                    last.then_inc(s7("tr_ps"), 1)
                    pe.wait_ge(s7("tr"), h + 1)
                    pe.wait_ge(s7("tr_a"), h + 1)
                    pe.wait_ge(s7("tail"), h + 1)
                    for t in range(QT):
                        nc.tensor.matmul(ps[5 + t // 2][:, (t % 2) * 256:(t % 2) * 256 + 256], TR[:, t, 0], TR[:, t, 1:3], start=True, stop=True)
                    nc.tensor.matmul(ps[7][0:NS, 0:2 * NS], TR[:, QC, 0, 0:NS], TR[:, QC, 1:3, 0:NS], start=True, stop=True).then_inc(s7("kk"), 1)
                    pe.wait_ge(s7("tt0"), h + 1)
                    for t in range(QT):
                        nc.tensor.transpose(ps[0][:, t * P:(t + 1) * P], TT[:, t], ident)
                    nc.tensor.transpose(ps[4][0:NS, 0:NS], TTS[:, :], ident[0:NS, 0:NS]).then_inc(s7("ti_ps"), 1)
                    for l in range(1, NL):
                        x = h * (NL - 1) + l
                        pe.wait_ge(s7("inv"), x)
                        pe.wait_ge(s7("m"), x)
                        for t in range(QT):
                            last = nc.tensor.matmul(ps[1][:, t * P:(t + 1) * P], M[:, l, t], TI[:, t], start=True, stop=True)
                        if l == 1:
                            last = nc.tensor.matmul(ps[4][0:NS, NS:2 * NS], MS[:, 1], TIS[:, :], start=True, stop=True)
                        last.then_inc(s7("y_ps"), 1)
                        pe.wait_ge(s7("y"), x)
                        if l < NL - 1:
                            for t in range(QT):
                                nc.tensor.matmul(ps[2][:, t * P:(t + 1) * P], TT[:, t], Y[:, t], start=True, stop=True)
                        for t in range(QT):
                            last = nc.tensor.matmul(ps[3][:, t * P:(t + 1) * P], Y[:, t], TT[:, t], start=True, stop=True)
                        if l == 1:
                            last = nc.tensor.matmul(ps[4][0:NS, 2 * NS:3 * NS], YS[:, :], TTS[:, :], start=True, stop=True)
                        last.then_inc(s7("d_ps"), 1)
                    pe.wait_ge(s7("kd"), h + 1)
                    pe.wait_ge(s7("inv_end"), h + 1)
                    for t in range(QT):
                        nc.tensor.matmul(ps[5][:, t * P:(t + 1) * P], KG[:, t], TT[:, t], start=True, stop=True)
                    nc.tensor.matmul(ps[7][:, 0:NS], KG[0:NS, QC], TTS[:, :], start=True, stop=True).then_inc(s7("w_ps"), 1)
                    pe.wait_ge(s7("vb"), h + 1)
                    pe.wait_ge(s7("w"), h + 1)
                    pe.wait_ge(s7("z_in"), h * 32 + 32)
                    for b in range(B):
                        last = nc.tensor.matmul(ps[4][:, b * 8:b * 8 + 8], SS[:, b], WQ[:, b].rearrange("p i t -> p (i t)"), start=True, stop=True)
                    last.then_inc(s7("ws_ps"), 1)
                    for t in range(QT):
                        x = h * QT + t
                        if t:
                            pe.wait_ge(s7("state"), x)
                        else:
                            pe.wait_ge(s7("szero"), h + 1)
                        v = ps[0][:, t * P:(t + 1) * P]
                        nc.tensor.matmul(v, TT[:, t], VB[:, t], start=True, stop=False)
                        nc.tensor.matmul(v, WT[:, t], S[:, :], start=False, stop=True).then_inc(s7("v_ps"), 1)
                        o = ps[1][:, t * P:(t + 1) * P]
                        nc.tensor.matmul(o, TR[:, t, 3], S[:, :], start=True, stop=False)
                        pe.wait_ge(s7("vn"), x + 1)
                        nc.tensor.matmul(ps[2][:, 0:P], KD[:, t], VNW[:, t], start=True, stop=True).then_inc(s7("s_ps"), 1)
                        last = nc.tensor.matmul(o, AQ[:, t, 1], VNW[:, t], start=False, stop=True)
                        if t == 0:
                            pe.wait_ge(s7("ws"), h + 1)
                            v = ps[7][0:NS, P:2 * P]
                            nc.tensor.matmul(v, WS[:, 0], ident, start=True, stop=False)
                            nc.tensor.matmul(v, TTS[:, :], VB[0:NS, QC], start=False, stop=True).then_inc(s7("vs_ps"), 1)
                        if t == 1:
                            pe.wait_ge(s7("vns"), h + 1)
                            v = ps[6][0:NS, 0:P]
                            nc.tensor.matmul(v, WS[:, 1], ident, start=True, stop=False)
                            nc.tensor.matmul(v, AQS[:, 1], VNS[:, :], start=False, stop=True).then_inc(s7("os_ps"), 1)
                        if t == 2:
                            pe.wait_ge(s7("vm"), h + 1)
                            for k in range(2):
                                last2 = nc.tensor.matmul(ps[3 + 2 * k][:, :], KD[0:NS, QC], VM[:, 4 * k:4 * k + 4].rearrange("p b v -> p (b v)"), start=True, stop=True)
                            last2.then_inc(s7("ss_ps"), 1)
                    last.then_inc(s7("o_ps"), 1)
                    pe.wait_ge(s7("on"), h + 1)
                    for t in range(QT):
                        nc.tensor.transpose(ps[0][:, t * P:(t + 1) * P], ON[:, t], ident)
                    nc.tensor.transpose(ps[4][:, 0:NS], ON[0:NS, QC], ident[0:NS, 0:NS]).then_inc(s7("ot_ps"), 1)

            @block.scalar
            def _(act):
                act.wait_ge(s7("gcs"), 1)
                nc.scalar.activation(EG[:, 0:QT], GC[:, 0:QT], ACT.Exp)
                nc.scalar.activation(EG[0:NS, QC], GC[0:NS, QC], ACT.Exp)
                nc.scalar.activation(GLP[:].rearrange("p t h -> p (t h)"), ps[2][:, 32:32 + QT * GH], ACT.Exp)
                nc.scalar.activation(ED[:, 0:QT], GTOT[:, 0:QT], ACT.Exp)
                nc.scalar.activation(ED[0:NS, QC], GTOT[0:NS, QC], ACT.Exp)
                act.wait_ge(s7("gl_ps"), 1)
                nc.scalar.activation(GLS[:].rearrange("p b h -> p (b h)"), ps[4][:, 0:B * GH], ACT.Exp).then_inc(s7("pre"), 1)
                with act.Fori(0, GH) as h:
                    act.wait_ge(s7("conv"), h + 1)
                    nc.scalar.activation(CT[:], CT[:], ACT.Silu).then_inc(s7("silu"), 1)
                    act.wait_ge(s7("nat_ps"), h + 1)
                    for t in (0, 1):
                        last = nc.scalar.copy(NAT[:, t].rearrange("p i d -> p (i d)"), ps[t][:, 0:3 * HD])
                    last.then_inc(s7("nat_a"), 1)
                    act.wait_ge(s7("rn_v"), h * 2 + 2)
                    nc.scalar.activation(RN[:, 0:QT], RN[:, 0:QT], ACT.Sqrt)
                    nc.scalar.activation(RN[0:NS, QC], RN[0:NS, QC], ACT.Sqrt).then_inc(s7("rn"), 1)
                    act.wait_ge(s7("tail_ps"), h + 1)
                    act.wait_ge(s7("stored"), h + 1)
                    nc.scalar.copy(TO[:].rearrange("p i d -> p (i d)"), ps[5][0:3 + 3 * B, 0:3 * HD]).then_inc(s7("tail"), 1)
                    act.wait_ge(s7("tr_ps"), h + 1)
                    for t in (0, 1):
                        last = nc.scalar.copy(TR[:, t].rearrange("p i d -> p (i d)"), ps[t][:, :])
                    last.then_inc(s7("tr_a"), 1)
                    act.wait_ge(s7("dec"), h + 1)
                    nc.scalar.activation(DT[:], DT[:], ACT.Exp)
                    nc.scalar.activation(DTS[:], DTS[:], ACT.Exp).then_inc(s7("dexp"), 1)
                    for l in range(1, NL):
                        x = h * (NL - 1) + l
                        act.wait_ge(s7("y_ps"), x)
                        last = nc.scalar.copy(Y[:].rearrange("p t c -> p (t c)"), ps[1][:, :])
                        if l == 1:
                            last = nc.scalar.copy(YS[:, :], ps[4][0:NS, NS:2 * NS])
                        last.then_inc(s7("y"), 1)
                    act.wait_ge(s7("w_ps"), h + 1)
                    nc.scalar.mul(WT[:].rearrange("p t c -> p (t c)"), ps[5][:, :], -1.0)
                    nc.scalar.mul(WQ[:, :, 0], ps[7][:, 0:NS].rearrange("p (b t) -> p b t", t=T), -1.0)
                    nc.scalar.copy(WQ[:, :, 1], TR[:, QC, 3, 0:NS].rearrange("p (b t) -> p b t", t=T)).then_inc(s7("w"), 1)
                    act.wait_ge(s7("ws_ps"), h + 1)
                    nc.scalar.copy(WS[:].rearrange("p i (b t) -> p i b t", t=T), ps[4][:, 0:64].rearrange("p (b i t) -> p i b t", i=2, t=T)).then_inc(s7("ws"), 1)
                    act.wait_ge(s7("z_in"), h * 32 + 32)
                    nc.scalar.activation(ZT[:, :], ZT[:, :], ACT.Silu).then_inc(s7("z"), 1)
                    act.wait_ge(s7("os_ps"), h + 1)
                    nc.scalar.activation(ON[0:NS, QC], ps[6][0:NS, 0:P], ACT.Square, accum_out=RO[0:NS, QC:QC + 1])
                    act.wait_ge(s7("o_ps"), h + 1)
                    for t in range(QT):
                        last = nc.scalar.activation(ON[:, t], ps[1][:, t * P:(t + 1) * P], ACT.Square, accum_out=RO[:, t:t + 1])
                    last.then_inc(s7("osq"), 1)
                    act.wait_ge(s7("ro_v"), h + 1)
                    nc.scalar.activation(RO[:, 0:QT], RO[:, 0:QT], ACT.Sqrt)
                    nc.scalar.activation(RO[0:NS, QC:QC + 1], RO[0:NS, QC:QC + 1], ACT.Sqrt).then_inc(s7("ro"), 1)

            @block.vector
            def _(dve):
                dve.sem_inc(s7("fin"), 1)
                dve.sem_inc(s7("stored"), 1)
                dve.sem_inc(s7("levels"), 1)
                dve.wait_ge(s7("cb_ps"), 1)
                n = 3 * B + 4
                for k in range(2):
                    nc.vector.tensor_copy(CB[:].rearrange("p i h n -> p (i h n)")[:, k * 12 * n:(k + 1) * 12 * n], ps[k][:, 0:12 * n])
                dve.wait_ge(s7("gc_ps"), 1)
                pre = Count(dve, s7("pre_v"))
                nc.vector.tensor_copy(GC[:, 0:QT].rearrange("p t h -> p (t h)"), ps[2][:, 0:QT * GH])
                pre.link(nc.vector.tensor_copy(GC[0:NS, QC], ps[3][0:NS, 0:GH]))
                nc.vector.tensor_tensor(GTOT[:, 0:QT].rearrange("p t h -> p (t h)"), ps[2][:, 32:32 + QT * GH], GC[:, 0:QT].rearrange("p t h -> p (t h)"), ALU.subtract)
                nc.vector.tensor_tensor(GTOT[0:NS, QC], ps[3][0:NS, GH:2 * GH], GC[0:NS, QC], ALU.subtract).then_inc(s7("gcs"), 1)
                nc.vector.tensor_tensor(GM[:], cp("s_batch", NS).rearrange("p (b o) -> p b o", o=1).broadcast_to((NS, B, GH)),
                                        GAB[0:NS, QC:QC + 1, 24:32].broadcast_to((NS, B, GH)), ALU.mult).then_inc(s7("gm"), 1)
                dve.wait_ge(s7("zero"), 1)
                dve.wait_ge(s7("pre"), 1)
                LINKS = 15
                with dve.Fori(0, GH) as h:
                    ch = Count(dve, s7("ch"), h * LINKS)
                    h1 = bass.ds(h, 1)
                    dve.wait_ge(s7("e_in"), h * 96 + 96)
                    ch.link(nc.vector.tensor_copy(ES[:, :, :, 0:3], CB[:, :, h1, 0:3 * B].rearrange("p i o (b j) -> p i (o b) j", j=3)))
                    for j in range(4):
                        for i in range(3):
                            w = CB[:, i, h1, 3 * B + j]
                            o, x = CT[:, i, 0:SEQ], E[:, i, j:j + SEQ]
                            os_, xs = CT[:, i, SEQ:].rearrange("p (b t) -> p b t", t=T), ES[:, i, :, j:j + T]
                            if j == 0:
                                nc.vector.tensor_scalar(o, x, w, None, ALU.mult)
                                last = nc.vector.tensor_scalar(os_, xs, w, None, ALU.mult)
                            else:
                                nc.vector.scalar_tensor_tensor(o, x, w, o, ALU.mult, ALU.add)
                                last = nc.vector.scalar_tensor_tensor(os_, xs, w, os_, ALU.mult, ALU.add)
                        if j < 3:
                            ch.link(last)
                    nc.vector.tensor_copy(TAIL[:, :, 0:3], E[:, :, SEQ:SEQ + 3])
                    nc.vector.tensor_copy(TAIL[:, :, 3:].rearrange("p i (b j) -> p i b j", j=3), ES[:, :, :, T:T + 3]).then_inc(s7("conv"), 1)
                    dve.wait_ge(s7("gb"), h + 1)
                    for t in range(QT):
                        nc.vector.tensor_scalar(DT[:, t], ps[6][:, t * P:(t + 1) * P], GC[:, t, h1], 0.0, ALU.subtract, ALU.min)
                    nc.vector.tensor_scalar(DTS[:], ps[7][0:NS, 0:NS], GC[0:NS, QC, h1], 0.0, ALU.subtract, ALU.min).then_inc(s7("dec"), 1)
                    dve.wait_ge(s7("nat_ps"), h + 1)
                    for t, n in TILES[2:]:
                        last = nc.vector.tensor_copy(NAT[0:n, t].rearrange("p i d -> p (i d)"), ps[t][0:n, 0:3 * HD])
                    last.then_inc(s7("nat"), 1)
                    dve.wait_ge(s7("nat"), h + 1)
                    dve.wait_ge(s7("nat_a"), h + 1)
                    for a, b, rows in ((0, QT, P), (QC, QC + 1, NS)):
                        x = NAT[0:rows, a:b, 0:2]
                        q = SQ[0:rows, 0:b - a]
                        ch.link(nc.vector.tensor_tensor(q, x, x, ALU.mult))
                        ch.link(nc.vector.tensor_reduce(RN[0:rows, a:b], q, AX, ALU.add))
                        ch.link(nc.vector.tensor_scalar(RN[0:rows, a:b], RN[0:rows, a:b], 1e-6, None, ALU.add))
                        nc.vector.reciprocal(RN[0:rows, a:b], RN[0:rows, a:b]).then_inc(s7("rn_v"), 1)
                    dve.wait_ge(s7("rn"), h + 1)
                    for a, b, rows in ((0, QT, P), (QC, QC + 1, NS)):
                        def rn(i):
                            return RN[0:rows, a:b, i:i + 1].broadcast_to((rows, b - a, HD))
                        nc.vector.scalar_tensor_tensor(QN[0:rows, a:b], NAT[0:rows, a:b, 0], SCALE, rn(0), ALU.mult, ALU.mult)
                        last = nc.vector.tensor_tensor(KN[0:rows, a:b], NAT[0:rows, a:b, 1], rn(1), ALU.mult)
                    ch.link(last)
                    for a, b, rows in ((0, QT, P), (QC, QC + 1, NS)):
                        last = nc.vector.tensor_tensor(KB[0:rows, a:b], KN[0:rows, a:b], col(GAB, rows, h, 32, slice(a, b)), ALU.mult)
                    last.then_inc(s7("qn"), 1)
                    dve.wait_ge(s7("tr_ps"), h + 1)
                    for t in (2, 3):
                        nc.vector.tensor_copy(TR[:, t].rearrange("p i d -> p (i d)"), ps[t][:, :])
                    nc.vector.tensor_copy(TR[:, QC, :, 0:NS], ps[4][:, 0:4 * NS].rearrange("p (i n) -> p i n", n=NS)).then_inc(s7("tr"), 1)
                    dve.wait_ge(s7("dexp"), h + 1)
                    nc.vector.tensor_tensor(DT[:], DT[:], upto.rearrange("p (o c) -> p o c", o=1).broadcast_to((P, QT, P)), ALU.mult)
                    ch.link(nc.vector.tensor_tensor(DTS[:], DTS[:], s_upto, ALU.mult))
                    dve.wait_ge(s7("kk"), h + 1)
                    for k in range(2):
                        for i in range(2):
                            nc.vector.tensor_tensor(AQ[:, 2 * k:2 * k + 2, i], ps[5 + k][:, :].rearrange("p (t i c) -> p t i c", t=2, i=2)[:, :, i],
                                                    DT[:, 2 * k:2 * k + 2], ALU.mult)
                    for i in range(2):
                        last = nc.vector.tensor_tensor(AQS[:, i], ps[7][0:NS, i * NS:(i + 1) * NS], DTS[:, :], ALU.mult)
                    last.then_inc(s7("aq"), 1)
                    dve.wait_ge(s7("aq"), h + 1)
                    nc.vector.tensor_tensor(TT[:], AQ[:, :, 0], level[:, 0:1].broadcast_to((P, QT, P)), ALU.mult)
                    ch.link(nc.vector.tensor_tensor(TTS[:], AQS[:, 0], level[0:NS, 0, 0:NS], ALU.mult))
                    nc.vector.tensor_tensor(TT[:], ident.rearrange("p (o c) -> p o c", o=1).broadcast_to((P, QT, P)), TT[:], ALU.subtract)
                    nc.vector.tensor_tensor(TTS[:], ident[0:NS, 0:NS], TTS[:], ALU.subtract).then_inc(s7("tt0"), 1)
                    dve.wait_ge(s7("ti_ps"), h + 1)
                    nc.vector.tensor_copy(TIS[:, :], ps[4][0:NS, 0:NS])
                    nc.vector.tensor_copy(TI[:].rearrange("p t c -> p (t c)"), ps[0][:, :]).then_inc(s7("inv"), 1)
                    for l in range(1, NL):
                        x = h * (NL - 1) + l
                        dve.wait_ge(s7("d_ps"), x)
                        ttf, tif = TT[:].rearrange("p t c -> p (t c)"), TI[:].rearrange("p t c -> p (t c)")
                        if l == 1:
                            nc.vector.tensor_tensor(TTS[:], TTS[:], ps[4][0:NS, 2 * NS:3 * NS], ALU.subtract)
                        if l < NL - 1:
                            nc.vector.tensor_tensor(ttf, ttf, ps[3][:, :], ALU.subtract)
                            nc.vector.tensor_tensor(tif, tif, ps[2][:, :], ALU.subtract).then_inc(s7("inv"), 1)
                        else:
                            nc.vector.tensor_tensor(ttf, ttf, ps[3][:, :], ALU.subtract).then_inc(s7("inv_end"), 1)
                    dve.wait_ge(s7("stored"), h + 1)
                    nc.vector.memset(S[:, :], 0.0).then_inc(s7("szero"), 1)
                    for t in range(QT):
                        x = h * QT + t
                        dve.wait_ge(s7("v_ps"), x + 1)
                        nc.vector.tensor_copy(VNW[:, t], ps[0][:, t * P:(t + 1) * P]).then_inc(s7("vn"), 1)
                        dve.wait_ge(s7("s_ps"), x + 1)
                        last = nc.vector.scalar_tensor_tensor(S[:, :], S[:, :], GLP[:, t, h1], ps[2][:, 0:P], ALU.mult, ALU.add)
                        last.then_inc(s7("state"), 1)
                        if t == 0:
                            dve.wait_ge(s7("vs_ps"), h + 1)
                            nc.vector.tensor_copy(VNS[:, :], ps[7][0:NS, P:2 * P]).then_inc(s7("vns"), 1)
                            dve.wait_ge(s7("vns"), h + 1)
                            nc.vector.tensor_tensor(VM[:], VNS[:].rearrange("p (o v) -> p o v", o=1).broadcast_to((NS, B, HD)),
                                                    cp("s_batch", NS).rearrange("p (b o) -> p b o", o=1).broadcast_to((NS, B, HD)), ALU.mult).then_inc(s7("vm"), 1)
                    ch.link(nc.vector.tensor_tensor(SN[:], SS[:], GLS[:, :, h1].broadcast_to((P, B, HD)), ALU.mult))
                    dve.wait_ge(s7("ss_ps"), h + 1)
                    for k in range(2):
                        half = SN[:, 4 * k:4 * k + 4].rearrange("p b v -> p (b v)")
                        last = nc.vector.tensor_tensor(half, half, ps[3 + 2 * k][:, :], ALU.add)
                    last.then_inc(s7("s_fin"), 1)
                    dve.wait_ge(s7("osq"), h + 1)
                    nc.vector.tensor_scalar(RO[:, 0:QT], RO[:, 0:QT], 1.0 / HD, 1e-6, ALU.mult, ALU.add)
                    ch.link(nc.vector.tensor_scalar(RO[0:NS, QC:QC + 1], RO[0:NS, QC:QC + 1], 1.0 / HD, 1e-6, ALU.mult, ALU.add))
                    nc.vector.reciprocal(RO[:, 0:QT], RO[:, 0:QT])
                    nc.vector.reciprocal(RO[0:NS, QC:QC + 1], RO[0:NS, QC:QC + 1]).then_inc(s7("ro_v"), 1)
                    dve.wait_ge(s7("ro"), h + 1)
                    nc.vector.tensor_tensor(ON[:, 0:QT], ps[1][:, :].rearrange("p (t v) -> p t v", t=QT),
                                            RO[:, 0:QT].rearrange("p (t o) -> p t o", o=1).broadcast_to((P, QT, HD)), ALU.mult)
                    nc.vector.tensor_scalar(ON[0:NS, QC], ps[6][0:NS, 0:P], RO[0:NS, QC:QC + 1], None, ALU.mult).then_inc(s7("on"), 1)
                    dve.wait_ge(s7("ot_ps"), h + 1)
                    dve.wait_ge(s7("z"), h + 1)
                    out = MIX[:, bass.ds(h + H, 1)]
                    nc.vector.scalar_tensor_tensor(out[:, :, 0:SEQ].rearrange("p o n -> p (o n)"), ps[0][:, :], NG_[:, 0:1], ZT[:, 0:SEQ], ALU.mult, ALU.mult)
                    nc.vector.scalar_tensor_tensor(out[:, :, SEQ:].rearrange("p o n -> p (o n)"), ps[4][:, 0:NS], NG_[:, 0:1], ZT[:, SEQ:], ALU.mult, ALU.mult).then_inc(s7("fin"), 1)
                    nc.vector.memset(PAD7[:, :], 0.0).then_inc(s7("levels"), 1)
                    assert ch.n == LINKS, ch.n

        def layer_norm(tag, X, OUT, g_name, b_name, split):
            with ExitStack() as ph:
                NQ = 4
                SQ = sb(ph, tag + "_sq", [P, NQ, TOK])
                MU = sb(ph, tag + "_mu", [P, TOK])
                RS = sb(ph, tag + "_rs", [P, TOK])
                GB = sb(ph, tag + "_gb", [P, 2, KT])
                ps = banks(ph, tag)
                gb_in, su, ce, sq, vs, va, rs, sc, fin, ch = (sem(f"{tag}_{n}") for n in (
                    "gb_in", "sum", "centred", "squared", "sq_sum", "var", "rstd", "scaled", "fin", "ch"))
                hi, lo_s, al = (sem(f"{tag}_{n}") for n in ("hi", "lo", "alpha"))
                block = ph.enter_context(nc.Block())

                @block.sync
                def _(sp):
                    with nc.allow_non_contiguous_dma("small columns"):
                        for i, name in enumerate((g_name, b_name)):
                            sp.dma_start(GB[:, i, :], A[name][0].rearrange("(k p) -> p k", p=P)).then_inc(gb_in, 16)
                    sp.wait_ge(fin, KT)

                if split:
                    @block.gpsimd
                    def _(gp):
                        for k in range(KT):
                            gp.wait_ge(hi, k + 1)
                            nc.gpsimd.tensor_tensor(XL[:, k], OUT[:, k], XH[:, k].bitcast(F32), ALU.subtract).then_inc(lo_s, 1)

                @block.tensor
                def _(pe):
                    for k in range(KT):
                        nc.tensor.matmul(ps[0][:, :], cst("ones"), X[:, k, 0:SEQ], start=k == 0, stop=k == KT - 1)
                        last = nc.tensor.matmul(ps[1][:, 0:NS], cst("ones"), X[:, k, SEQ:], start=k == 0, stop=k == KT - 1)
                    last.then_inc(su, 1)
                    for k in range(KT):
                        pe.wait_ge(sq, k + 1)
                        nc.tensor.matmul(ps[2][:, :], cst("ones"), SQ[:, k % NQ, 0:SEQ], start=k == 0, stop=k == KT - 1)
                        nc.tensor.matmul(ps[3][:, 0:NS], cst("ones"), SQ[:, k % NQ, SEQ:], start=k == 0, stop=k == KT - 1).then_inc(vs, 1)

                @block.vector
                def _(dve):
                    c = Count(dve, ch)
                    dve.wait_ge(su, 1)
                    nc.vector.tensor_scalar(MU[:, 0:SEQ], ps[0][:, :], 1.0 / DM, None, ALU.mult)
                    c.link(nc.vector.tensor_scalar(MU[:, SEQ:], ps[1][:, 0:NS], 1.0 / DM, None, ALU.mult))
                    for k in range(KT):
                        nc.vector.tensor_tensor(X[:, k], X[:, k], MU[:], ALU.subtract).then_inc(ce, 1)
                    dve.wait_ge(vs, KT)
                    nc.vector.tensor_scalar(RS[:, 0:SEQ], ps[2][:, :], 1.0 / DM, 1e-5, ALU.mult, ALU.add)
                    c.link(nc.vector.tensor_scalar(RS[:, SEQ:], ps[3][:, 0:NS], 1.0 / DM, 1e-5, ALU.mult, ALU.add))
                    nc.vector.reciprocal(RS[:], RS[:]).then_inc(va, 1)
                    dve.wait_ge(rs, 1)
                    for k in range(KT):
                        nc.vector.tensor_tensor(X[:, k], X[:, k], RS[:], ALU.mult).then_inc(sc, 1)
                    if split:
                        for k in range(KT):
                            dve.wait_ge(lo_s, k + 1)
                            nc.vector.tensor_scalar(OUT[:, k], OUT[:, k], ALPHA, None, ALU.mult).then_inc(al, 1)

                @block.scalar
                def _(act):
                    for k in range(KT):
                        act.wait_ge(ce, k + 1)
                        if k >= NQ:
                            act.wait_ge(vs, k - NQ + 1)
                        nc.scalar.activation(SQ[:, k % NQ], X[:, k], ACT.Square).then_inc(sq, 1)
                    act.wait_ge(va, 1)
                    nc.scalar.activation(RS[:], RS[:], ACT.Sqrt).then_inc(rs, 1)
                    act.wait_ge(gb_in, 32)
                    for k in range(KT):
                        act.wait_ge(sc, k + 1)
                        nc.scalar.activation(OUT[:, k], X[:, k], ACT.Identity, scale=GB[:, 0, k:k + 1], bias=GB[:, 1, k:k + 1]).then_inc(fin, 1)
                        if split:
                            act.wait_ge(fin, k + 1)
                            nc.scalar.copy(XH[:, k], OUT[:, k]).then_inc(hi, 1)

        XH = sb(top, "m_hi", [P, KT, TOK], F32R)
        XL = sb(top, "m_lo", [P, KT, TOK], F32R)
        res = ExitStack()
        top.enter_context(res)
        XR = sb(res, "x_res", [P, KT, TOK])
        with ExitStack() as ph:
            W = sb(ph, "wo_ring", [P, 2, KT, P])
            WH = sb(ph, "wo_hi", [P, 2, KT, P], F32R)
            WL = sb(ph, "wo_lo", [P, 2, KT, P], F32R)
            ps = banks(ph, "h")
            w_in = [sem(f"wo_in{i}") for i in range(2)]
            x_in, acc, ev, wh, wl, xh, xl = (sem("o_" + n) for n in ("xr_in", "acc", "ev", "wh", "wl", "xh", "xl"))
            W_o = A["w_o"][0].rearrange("(k p) n -> p k n", p=P)
            block = ph.enter_context(nc.Block())
            NGO = DM // 256

            @block.sync
            def _(sp):
                for n in range(2):
                    sp.dma_start(W[:, n], W_o[:, :, n * P:(n + 1) * P]).then_inc(w_in[n], 16)
                sp.dma_start(XR[:], S_xt.rearrange("k p n -> p k n")).then_inc(x_in, 16)
                with sp.Fori(1, NGO) as g:
                    for n in range(2):
                        sp.wait_ge(wl, g * 2 + n - 1)
                        sp.dma_start(W[:, n], W_o[:, :, bass.ds(g * 256 + n * P, P)]).then_inc(w_in[n], 16)
                sp.wait_ge(ev, NGO * 2 + 2)

            @block.tensor
            def _(pe):
                pe.sem_inc(acc, 2)
                pe.wait_ge(xl, 1)
                with pe.Fori(0, NGO) as g:
                    for n in range(2):
                        pe.wait_ge(wl, g * 2 + n + 1)
                        pe.wait_ge(ev, g * 2 + n + 1)
                        for k in range(KT):
                            last = product(nc, ps[2 * n:2 * n + 2], WH[:, n, k], WL[:, n, k], XH[:, k], XL[:, k], k == 0, k == KT - 1)
                        last.then_inc(acc, 1)

            @block.scalar
            def _(act):
                nc.scalar.copy(XH[:], MIX[:]).then_inc(xh, 1)
                with act.Fori(0, NGO) as g:
                    for n in range(2):
                        act.wait_ge(w_in[n], g * 16 + 16)
                        act.wait_ge(acc, g * 2 + n + 1)
                        nc.scalar.copy(WH[:, n], W[:, n]).then_inc(wh, 1)

            @block.gpsimd
            def _(gp):
                with gp.Fori(0, NGO) as g:
                    for n in range(2):
                        gp.wait_ge(wh, g * 2 + n + 1)
                        nc.gpsimd.tensor_tensor(WL[:, n], W[:, n], WH[:, n].bitcast(F32), ALU.subtract).then_inc(wl, 1)

            @block.vector
            def _(dve):
                dve.sem_inc(ev, 2)
                dve.wait_ge(xh, 1)
                nc.vector.tensor_tensor(XL[:], MIX[:], XH[:].bitcast(F32), ALU.subtract).then_inc(xl, 1)
                dve.wait_ge(x_in, 16)
                with dve.Fori(0, NGO) as g:
                    for n in range(2):
                        dve.wait_ge(acc, g * 2 + n + 3)
                        x = XR[:, bass.ds(g * 2 + n, 1)].rearrange("p o n -> p (o n)")
                        for half in range(2):
                            c = slice(half * HT2, (half + 1) * HT2)
                            last = nc.vector.scalar_tensor_tensor(x[:, c], x[:, c], ALPHA, ps[2 * n + half][:, 0:HT2], ALU.mult, ALU.add)
                        last.then_inc(ev, 1)

        layer_norm("ln1", XR, MIX, "ln1_g", "ln1_b", True)
        res.close()
        HT = MIX

        with ExitStack() as ph:
            NF = 4
            NCH = FT // NF
            NTASK, NUSE = 12, 12
            FREED = {0: 1, 1: 3, 10: 5, 11: 7}
            W = sb(ph, "f_ring", [P, 4, KT * P])
            WH = sb(ph, "f_hi", [P, 2, KT * P], F32R)
            WL = sb(ph, "f_lo", [P, 2, KT * P], F32R)
            AH = sb(ph, "act_hi", [P, NF, TOK], F32R)
            AL = sb(ph, "act_lo", [P, NF, TOK], F32R)
            AF = sb(ph, "act_f", [P, 2, TOK])
            UE = sb(ph, "u_ext", [P, 2, SEQ + 2])
            US = sb(ph, "u_ext_s", [P, 2, B, T + 2])
            UC = sb(ph, "u_conv", [P, 2, TOK])
            TL = sb(ph, "u_tail", [P, FT, 2 + SR])
            TO = W[0:2 + SR].rearrange("p s c -> p (s c)")[:, 0:FF]
            ps = banks(ph, "i")
            w_in = [sem(f"up_in{i}") for i in range(4)]
            wh, wl, used, acc, ue, cv, ge, af, ah, al, z9, rd, tl, tev, tout, ch = (sem("f_" + n) for n in (
                "wh", "wl", "used", "acc", "ue", "conv", "gelu", "prod", "ah", "al", "zero", "read", "tail_ps", "tail_ev", "tail_out", "ch"))
            W_up = A["ffn_w_up"][0].rearrange("(k p) n -> p k n", p=P)
            W_dn = A["ffn_w_down"][0].rearrange("(k p) n -> p k n", p=P)
            block = ph.enter_context(nc.Block())
            NTR = FT // 4

            def up_tile(t, s):
                return t[:, s].rearrange("p (k c) -> p k c", c=P)

            def down_tile(t, s):
                return t[:, s].rearrange("p (k c) -> p k c", c=512)

            @block.sync
            def _(sp):
                def load(c, s):
                    if s < 8:
                        off = (s % 2) * FF + (s // 2) * P
                        return sp.dma_start(up_tile(W, s % 4), W_up[:, :, bass.ds(c * 512 + off, P)]).then_inc(w_in[s % 4], 16)
                    return sp.dma_start(down_tile(W, s % 4), W_dn[:, bass.ds(c * NF, NF), (s - 8) * 512:(s - 7) * 512]).then_inc(w_in[s % 4], 16)

                with sp.Fori(0, NCH) as c:
                    for s in range(NTASK):
                        sp.wait_ge(wl, c * NTASK + s + 1)
                        load(c, s)
                sp.wait_ge(tev, NTR)
                sp.dma_start(O[7][0, 0], TO[0:2]).then_inc(tout, 16)
                sp.dma_start(O[13][0].rearrange("b r c -> (b r) c"), TO[2:2 + SR]).then_inc(tout, 16)
                sp.wait_ge(tout, 32)

            @block.gpsimd
            def _(gp):
                gp.sem_inc(wl, 4)
                with gp.Fori(0, NCH) as c:
                    for s in range(NTASK):
                        gp.wait_ge(wh, c * NTASK + s + 1)
                        nc.gpsimd.tensor_tensor(WL[:, s % 2], W[:, s % 4], WH[:, s % 2].bitcast(F32), ALU.subtract).then_inc(wl, 1)

            @block.tensor
            def _(pe):
                pe.sem_inc(acc, 3)
                with pe.Fori(0, NCH) as c:
                    for n in range(NF):
                        pe.wait_ge(rd, c * NUSE + n + 1)
                        for v in range(2):
                            s = 2 * n + v
                            pe.wait_ge(wl, c * NTASK + s + 5)
                            b = 4 * (n % 2) + 2 * v
                            for k in range(KT):
                                last = product(nc, ps[b:b + 2], up_tile(WH, s % 2)[:, k], up_tile(WL, s % 2)[:, k], XH[:, k], XL[:, k],
                                               k == 0, k == KT - 1)
                            last.then_inc(used, 1)
                    for p in range(8):
                        s = 8 + p // 2
                        pe.wait_ge(rd, c * NUSE + NF + p + 1)
                        if p % 2 == 0:
                            pe.wait_ge(wl, c * NTASK + s + 5)
                        for k in range(NF):
                            if p == 0:
                                pe.wait_ge(al, c * NF + k + 1)
                            for j in range(2):
                                col = (p % 2) * 256 + j * P
                                b = 4 * (p % 2) + 2 * j
                                last = product(nc, ps[b:b + 2], down_tile(WH, s % 2)[:, k, col:col + P], down_tile(WL, s % 2)[:, k, col:col + P],
                                               AH[:, k], AL[:, k], k == 0, k == NF - 1)
                        last.then_inc(acc, 1)
                pe.wait_ge(rd, NCH * NUSE + 2)
                for q in range(NTR):
                    if q >= 2:
                        pe.wait_ge(tev, q - 1)
                    for k in range(4):
                        last = nc.tensor.transpose(ps[6 + q % 2][0:2 + SR, k * P:(k + 1) * P], TL[:, q * 4 + k], ident)
                    last.then_inc(tl, 1)

            @block.scalar
            def _(act):
                def high(c, s):
                    act.wait_ge(w_in[s % 4], c * 48 + (s // 4) * 16 + 16)
                    if s in FREED:
                        act.wait_ge(acc, c * 8 + FREED[s])
                    else:
                        act.wait_ge(used, c * 8 + s - 1)
                    nc.scalar.copy(WH[:, s % 2], W[:, s % 4]).then_inc(wh, 1)

                def chunk(c):
                    high(c, 0)
                    high(c, 1)
                    for n in range(NF):
                        high(c, 2 * n + 2)
                        high(c, 2 * n + 3)
                        b = 4 * (n % 2)
                        act.wait_ge(used, c * 8 + 2 * n + 2)
                        act.wait_ge(cv, c * NF + n + 1)
                        nc.scalar.copy(UE[:, n % 2, 2:2 + HT2], ps[b][:, 0:HT2])
                        nc.scalar.copy(UE[:, n % 2, 2 + HT2:], ps[b + 1][:, 0:SP2])
                        nc.scalar.copy(US[:, n % 2, :, 2:], ps[b + 1][:, SP2:HT2].rearrange("p (b t) -> p b t", t=T)).then_inc(ue, 1)
                        act.wait_ge(cv, c * NF + n + 3)
                        nc.scalar.activation(UC[:, n % 2], UC[:, n % 2], ACT.Gelu_apprx_tanh).then_inc(ge, 1)
                        act.wait_ge(af, c * NF + n + 1)
                        nc.scalar.copy(AH[:, n], AF[:, n % 2]).then_inc(ah, 1)
                    for s in range(10, NTASK):
                        high(c, s)

                with act.Fori(0, NCH) as c:
                    chunk(c)
                for q in range(NTR):
                    act.wait_ge(tl, q + 1)
                    nc.scalar.copy(TO[:, q * 512:(q + 1) * 512], ps[6 + q % 2][0:2 + SR, :]).then_inc(tev, 1)

            @block.vector
            def _(dve):
                dve.sem_inc(rd, 2)
                dve.sem_inc(cv, 2)
                nc.vector.memset(UE[:, :, 0:2], 0.0).then_inc(z9, 1)
                dve.wait_ge(z9, 1)
                with dve.Fori(0, NCH) as c:
                    lk = Count(dve, ch, c * 16)
                    for n in range(NF):
                        m = n % 2
                        b = 4 * m
                        j1 = bass.ds(c * NF + n, 1)
                        dve.wait_ge(ue, c * NF + n + 1)
                        lk.link(nc.vector.tensor_copy(US[:, m, :, 0:2], FB[:, j1, 0:SR].rearrange("p o (b j) -> p (o b) j", j=2)))
                        for j in range(3):
                            w = FB[:, j1, SR + j]
                            o, x = UC[:, m, 0:SEQ], UE[:, m, j:j + SEQ]
                            os_, xs = UC[:, m, SEQ:].rearrange("p (b t) -> p b t", t=T), US[:, m, :, j:j + T]
                            if j == 0:
                                nc.vector.tensor_scalar(o, x, w, None, ALU.mult)
                                last = nc.vector.tensor_scalar(os_, xs, w, None, ALU.mult)
                            else:
                                nc.vector.scalar_tensor_tensor(o, x, w, o, ALU.mult, ALU.add)
                                last = nc.vector.scalar_tensor_tensor(os_, xs, w, os_, ALU.mult, ALU.add)
                            if j < 2:
                                lk.link(last)
                        nc.vector.tensor_copy(TL[:, j1, 0:2].rearrange("p o r -> p (o r)"), UE[:, m, SEQ:SEQ + 2])
                        nc.vector.tensor_copy(TL[:, j1, 2:].rearrange("p o (b j) -> p (o b) j", j=2), US[:, m, :, T:T + 2]).then_inc(cv, 1)
                        dve.wait_ge(ge, c * NF + n + 1)
                        for half in range(2):
                            cols = slice(half * HT2, (half + 1) * HT2)
                            last = nc.vector.tensor_tensor(AF[:, m, cols], UC[:, m, cols], ps[b + 2 + half][:, 0:HT2], ALU.mult)
                        last.then_inc(af, 1)
                        dve.wait_ge(ah, c * NF + n + 1)
                        lk.link(nc.vector.tensor_tensor(AL[:, n], AF[:, m], AH[:, n].bitcast(F32), ALU.subtract))
                        dve.sem_inc(rd, 1)
                        dve.sem_inc(al, 1)
                    for p in range(8):
                        dve.wait_ge(acc, c * 8 + p + 4)
                        for j in range(2):
                            for half in range(2):
                                x = HT[:, 2 * p + j, half * HT2:(half + 1) * HT2]
                                last = nc.vector.tensor_tensor(x, x, ps[4 * (p % 2) + 2 * j + half][:, 0:HT2], ALU.add)
                        last.then_inc(rd, 1)

        layer_norm("ln2", HT, HT, "ln2_g", "ln2_b", False)

        with ExitStack() as ph:
            YN = sb(ph, "y_rows", [P, QT + 1, DM])
            ps = banks(ph, "k")
            tr, ev_v, ev_a, out = (sem("y_" + n) for n in ("tr", "ev_v", "ev_a", "out"))
            block = ph.enter_context(nc.Block())

            @block.sync
            def _(sp):
                for t in range(QT + 1):
                    sp.wait_ge(ev_v, 2 * t + 2)
                    sp.wait_ge(ev_a, 2 * t + 2)
                    if t < QT:
                        sp.dma_start(O[0][0, t * P:(t + 1) * P, :], YN[:, t]).then_inc(out, 16)
                    else:
                        sp.dma_start(O[1].rearrange("b t d -> (b t) d"), YN[0:NS, t]).then_inc(out, 16)
                sp.wait_ge(out, 16 * (QT + 1))

            @block.tensor
            def _(pe):
                for u in range(20):
                    tt, kg = u // 4, u % 4
                    n = P if tt < QT else NS
                    if u >= 8:
                        pe.wait_ge(ev_v if u % 2 == 0 else ev_a, (u - 8) // 2 + 1)
                    for k in range(4):
                        last = nc.tensor.transpose(ps[u % 8][0:n, k * P:(k + 1) * P], HT[:, kg * 4 + k, tt * P:tt * P + n], ident)
                    last.then_inc(tr, 1)

            def rows_evac(eng, copy, par, s):
                for u in range(par, 20, 2):
                    tt, kg = u // 4, u % 4
                    n = P if tt < QT else NS
                    eng.wait_ge(tr, u + 1)
                    copy(YN[0:n, tt, kg * 512:(kg + 1) * 512], ps[u % 8][0:n, :]).then_inc(s, 1)

            @block.vector
            def _(dve):
                rows_evac(dve, nc.vector.tensor_copy, 0, ev_v)

            @block.scalar
            def _(act):
                rows_evac(act, nc.scalar.copy, 1, ev_a)
_INS = ['x_prompt','x_sample','cache_cmp_kv','cache_slc_kv','cache_win_kv','state_gdn','state_gdn_conv','state_ffn_conv','page_table','w_in','w_o','cmp_pe','cmp_w1','cmp_w2','gdn_conv_w','gdn_a_log','gdn_dt_bias','gdn_norm_g','ln1_g','ln1_b','ffn_w_up','ffn_conv_w','ffn_w_down','ln2_g','ln2_b']
_OUTS = [(1,512,2048),(8,4,2048),(1,1,512,2,2,128),(1,1,512,2,2,128),(1,1,512,2,2,128),(1,1,8,128,128),(1,1,3,3072),(1,1,2,5632),
         (1,8,4,2,2,128),(1,8,4,2,2,128),(1,8,512,2,2,128),(1,8,8,128,128),(1,8,3,3072),(1,8,2,5632)]


def kernel(**inputs):
    import numpy as _np
    import concourse.bacc as _bacc
    from concourse import mybir as _mybir
    from concourse.bass_utils import run_bass_kernel_spmd as _run

    nc = _bacc.Bacc("TRN2", target_bir_lowering=False, num_devices=1)
    arrays, args = {}, {}
    for name in _INS:
        a = _np.ascontiguousarray(inputs[name])
        arrays[f"in_{name}_dram"] = a
        args[name] = nc.dram_tensor(f"in_{name}_dram", a.shape, _mybir.dt.from_np(a.dtype), kind="ExternalInput").ap()
    table, at = shape_constants()
    arrays['in_consts_dram'] = table
    consts = nc.dram_tensor('in_consts_dram', table.shape, _mybir.dt.float32, kind='ExternalInput').ap()
    outs = []
    for i, shape in enumerate(_OUTS):
        outs.append(nc.dram_tensor(f"out_{i}_dram", shape, _mybir.dt.float32, kind="ExternalOutput").ap())
    build(nc, args, outs, consts, at)
    r = _run(nc, [arrays], core_ids=[0])
    return tuple(r.results[0][f"out_{i}_dram"] for i in range(len(_OUTS)))
```
